# Optimizing a Trainium2 kernel written in Bass

```python
import jax, jax.numpy as jnp
from jax import lax
import numpy as np

D_MODEL = 1024
BATCH = 1
SEQ = 1024
DEPTH = 1
DEC_BATCH = 8
DEC_SEQ = 16
PAST_LEN = 512

CHUNK = 64
RMS_EPS = 1e-6
L2_EPS = 1e-6
A_HEADS = 8
A_HEAD_DIM = 64
A_WIDTH = A_HEADS * A_HEAD_DIM
A_PREV_CHUNKS = 8
A_REACH = A_PREV_CHUNKS * CHUNK
A_BAND = A_REACH + CHUNK
MAX_REL = 128
B_HEADS = 4
B_DK = 128
B_DV = 128
B_KW = B_HEADS * B_DK
B_VW = B_HEADS * B_DV
B_CONV_CH = 2 * B_KW + B_VW
CONV_WIDTH = 4
D_FF = 4 * D_MODEL
IN_SPLIT_SIZES = (A_WIDTH, A_WIDTH, A_WIDTH, B_CONV_CH, B_VW, B_HEADS, B_HEADS, D_MODEL, D_MODEL)
IN_COLS = sum(IN_SPLIT_SIZES)

kernel_name = "hybrid_chunkband_attn_gated_deltanet_step"

def _rms_norm(x, gain):
    xf = x.astype(jnp.float32)
    y = xf * lax.rsqrt(jnp.mean(jnp.square(xf), axis=-1, keepdims=True) + RMS_EPS)
    return (y * gain.astype(jnp.float32)).astype(x.dtype)

def _l2_normalize(x):
    xf = x.astype(jnp.float32)
    return xf * lax.rsqrt(jnp.sum(jnp.square(xf), axis=-1, keepdims=True) + L2_EPS)

def _rel_bias(rel_bias, rel):
    idx = jnp.clip(rel, -MAX_REL, MAX_REL) + MAX_REL
    return jnp.take(rel_bias.astype(jnp.float32), idx, axis=1)

def _band_attention_prompt(q, k, v, rel_bias):
    b, s, h, d = q.shape
    nc = s // CHUNK
    zeros = jnp.zeros((b, A_REACH, h, d), k.dtype)
    k_pad = jnp.concatenate([zeros, k], axis=1)
    v_pad = jnp.concatenate([zeros, v], axis=1)
    q_chunks = jnp.moveaxis(q.reshape(b, nc, CHUNK, h, d), 1, 0)
    t = jnp.arange(CHUNK)[:, None]
    m = jnp.arange(A_BAND)[None, :]
    bias = _rel_bias(rel_bias, t + A_REACH - m)
    scale = A_HEAD_DIM ** -0.5

    def one_chunk(args):
        c, qc = args
        start = c * CHUNK
        kb = lax.dynamic_slice_in_dim(k_pad, start, A_BAND, axis=1)
        vb = lax.dynamic_slice_in_dim(v_pad, start, A_BAND, axis=1)
        valid = jnp.arange(A_BAND) >= A_REACH - start
        sc = jnp.einsum('blhd,bmhd->bhlm', qc, kb, preferred_element_type=jnp.float32) * scale + bias
        sc = jnp.where(valid, sc, -jnp.inf)
        p = jax.nn.softmax(sc, axis=-1)
        return jnp.einsum('bhlm,bmhd->blhd', p.astype(vb.dtype), vb)

    out = lax.map(one_chunk, (jnp.arange(nc), q_chunks))
    return jnp.moveaxis(out, 0, 1).reshape(b, s, h, d)

def _band_attention_sample(q, k_all, v_all, rel_bias):
    t_len = q.shape[1]
    m_len = k_all.shape[1]
    past = m_len - t_len
    rel = jnp.arange(t_len)[:, None] + past - jnp.arange(m_len)[None, :]
    bias = _rel_bias(rel_bias, rel)
    sc = jnp.einsum('blhd,bmhd->bhlm', q, k_all, preferred_element_type=jnp.float32) * (A_HEAD_DIM ** -0.5) + bias
    p = jax.nn.softmax(sc, axis=-1)
    return jnp.einsum('bhlm,bmhd->blhd', p.astype(v_all.dtype), v_all)

def _causal_conv_silu(x_ext, conv_w):
    t_len = x_ext.shape[1] - (CONV_WIDTH - 1)
    y = x_ext[:, 0:t_len] * conv_w[0]
    for i in range(1, CONV_WIDTH):
        y = y + x_ext[:, i:i + t_len] * conv_w[i]
    return jax.nn.silu(y)

def _gated_delta_rule(q, k, v, g, beta, s0):
    f32 = jnp.float32
    b, t_len, h, dk = q.shape
    dv = v.shape[-1]
    L = CHUNK if t_len % CHUNK == 0 else t_len
    nc = t_len // L

    def chunks(x):
        x = x.astype(f32).reshape((b, nc, L, h) + x.shape[3:])
        return jnp.moveaxis(x, 3, 2)

    q = chunks(q) * (dk ** -0.5)
    k = chunks(k)
    v = chunks(v)
    g = chunks(g)
    beta = chunks(beta)
    gc = jnp.cumsum(g, axis=-1)
    tril = jnp.tril(jnp.ones((L, L), bool))
    strict = jnp.tril(jnp.ones((L, L), bool), -1)
    diff = gc[..., :, None] - gc[..., None, :]
    decay = jnp.where(tril, jnp.exp(jnp.where(tril, diff, 0.0)), 0.0)
    kk = jnp.einsum('bnhid,bnhjd->bnhij', k, k)
    a_mat = jnp.where(strict, beta[..., None] * kk * decay, 0.0) + jnp.eye(L, dtype=f32)
    rhs = jnp.concatenate([v * beta[..., None], k * (beta * jnp.exp(gc))[..., None]], axis=-1)
    sol = lax.linalg.triangular_solve(a_mat, rhs, left_side=True, lower=True, unit_diagonal=True)
    u = sol[..., :dv]
    w = sol[..., dv:]
    qk = jnp.einsum('bnhid,bnhjd->bnhij', q, k) * decay
    q_dec = q * jnp.exp(gc)[..., None]
    k_dec = k * jnp.exp(gc[..., -1:] - gc)[..., None]
    g_last = jnp.exp(gc[..., -1])

    def step(s, inp):
        u_c, w_c, qk_c, qd_c, kd_c, gl_c = inp
        v_new = u_c - jnp.einsum('bhld,bhde->bhle', w_c, s)
        o = jnp.einsum('bhld,bhde->bhle', qd_c, s) + jnp.einsum('bhij,bhje->bhie', qk_c, v_new)
        s = s * gl_c[..., None, None] + jnp.einsum('bhld,bhle->bhde', kd_c, v_new)
        return s, o

    xs = tuple(jnp.moveaxis(a, 1, 0) for a in (u, w, qk, q_dec, k_dec, g_last))
    s_fin, o = lax.scan(step, s0.astype(f32), xs)
    o = o.transpose(1, 0, 3, 2, 4).reshape(b, t_len, h, dv)
    return o, s_fin

def _layer(x, cache_k, cache_v, conv_buf, delta_s0,
           norm_mix_pre, w_in, rel_bias, conv_w, a_log, dt_bias, delta_norm_w,
           w_proj_a, w_proj_b, w_out, norm_mix_post, norm_mlp_pre, w_up, w_down, norm_mlp_post):
    b, t_len, _ = x.shape
    h = _rms_norm(x, norm_mix_pre)
    p = h @ w_in
    split_at = [int(i) for i in np.cumsum(IN_SPLIT_SIZES)[:-1]]
    qa, ka, va, qkv_b, z_b, a_b, b_b, gate_a, gate_b = jnp.split(p, split_at, axis=-1)

    qa = qa.reshape(b, t_len, A_HEADS, A_HEAD_DIM)
    ka = ka.reshape(b, t_len, A_HEADS, A_HEAD_DIM)
    va = va.reshape(b, t_len, A_HEADS, A_HEAD_DIM)
    if cache_k is None:
        oa = _band_attention_prompt(qa, ka, va, rel_bias)
        keep = min(A_REACH, t_len)
        new_k, new_v = ka[:, t_len - keep:], va[:, t_len - keep:]
    else:
        k_all = jnp.concatenate([cache_k.astype(ka.dtype), ka], axis=1)
        v_all = jnp.concatenate([cache_v.astype(va.dtype), va], axis=1)
        oa = _band_attention_sample(qa, k_all, v_all, rel_bias)
        new_k, new_v = ka, va

    x_ext = jnp.concatenate([conv_buf.astype(qkv_b.dtype), qkv_b], axis=1)
    new_conv = x_ext[:, -(CONV_WIDTH - 1):]
    c = _causal_conv_silu(x_ext, conv_w)
    qb, kb, vb = jnp.split(c, [B_KW, 2 * B_KW], axis=-1)
    qb = _l2_normalize(qb.reshape(b, t_len, B_HEADS, B_DK))
    kb = _l2_normalize(kb.reshape(b, t_len, B_HEADS, B_DK))
    vb = vb.reshape(b, t_len, B_HEADS, B_DV)
    g = -jnp.exp(a_log.astype(jnp.float32)) * jax.nn.softplus(a_b.astype(jnp.float32) + dt_bias.astype(jnp.float32))
    beta = jax.nn.sigmoid(b_b.astype(jnp.float32))
    ob, s_new = _gated_delta_rule(qb, kb, vb, g, beta, delta_s0)
    zb = z_b.reshape(b, t_len, B_HEADS, B_DV).astype(jnp.float32)
    ob = (_rms_norm(ob, delta_norm_w) * jax.nn.silu(zb)).astype(x.dtype).reshape(b, t_len, B_VW)

    y_a = oa.reshape(b, t_len, A_WIDTH) @ w_proj_a
    y_b = ob @ w_proj_b
    merged = jax.nn.sigmoid(gate_a) * y_a + jax.nn.sigmoid(gate_b) * y_b
    x = x + _rms_norm(merged @ w_out, norm_mix_post)

    h2 = _rms_norm(x, norm_mlp_pre)
    f = jnp.square(jax.nn.relu(h2 @ w_up)) @ w_down
    x = x + _rms_norm(f, norm_mlp_post)
    return x, new_k, new_v, new_conv, s_new.astype(x.dtype)

def setup_inputs(seed: int = 0) -> dict:
    key = jax.random.key(seed)
    ks = jax.random.split(key, 24)
    f32 = jnp.float32
    cache_len = min(A_REACH, PAST_LEN)

    def nrm(k, shape, scale):
        return jax.random.normal(k, shape, f32) * scale

    def gain(k, shape):
        return 1.0 + 0.02 * jax.random.normal(k, shape, f32)

    return {
        'x_prompt': nrm(ks[0], (BATCH, SEQ, D_MODEL), 1.0),
        'x_sample': nrm(ks[1], (DEC_BATCH, DEC_SEQ, D_MODEL), 1.0),
        'cache_attn_k': nrm(ks[2], (DEPTH, DEC_BATCH, cache_len, A_HEADS, A_HEAD_DIM), 1.0),
        'cache_attn_v': nrm(ks[3], (DEPTH, DEC_BATCH, cache_len, A_HEADS, A_HEAD_DIM), 1.0),
        'state_conv': nrm(ks[4], (DEPTH, DEC_BATCH, CONV_WIDTH - 1, B_CONV_CH), 1.0),
        'state_delta': nrm(ks[5], (DEPTH, DEC_BATCH, B_HEADS, B_DK, B_DV), B_DK ** -0.5),
        'norm_mix_pre': gain(ks[6], (DEPTH, D_MODEL)),
        'w_in': nrm(ks[7], (DEPTH, D_MODEL, IN_COLS), D_MODEL ** -0.5),
        'rel_bias': nrm(ks[8], (DEPTH, A_HEADS, 2 * MAX_REL + 1), 0.2),
        'conv_w': nrm(ks[9], (DEPTH, CONV_WIDTH, B_CONV_CH), CONV_WIDTH ** -0.5),
        'a_log': jnp.log(jax.random.uniform(ks[10], (DEPTH, B_HEADS), f32, 1.0, 16.0)),
        'dt_bias': nrm(ks[11], (DEPTH, B_HEADS), 0.1),
        'delta_norm_w': gain(ks[12], (DEPTH, B_DV)),
        'w_proj_a': nrm(ks[13], (DEPTH, A_WIDTH, D_MODEL), A_WIDTH ** -0.5),
        'w_proj_b': nrm(ks[14], (DEPTH, B_VW, D_MODEL), B_VW ** -0.5),
        'w_out': nrm(ks[15], (DEPTH, D_MODEL, D_MODEL), D_MODEL ** -0.5),
        'norm_mix_post': gain(ks[16], (DEPTH, D_MODEL)),
        'norm_mlp_pre': gain(ks[17], (DEPTH, D_MODEL)),
        'w_up': nrm(ks[18], (DEPTH, D_MODEL, D_FF), D_MODEL ** -0.5),
        'w_down': nrm(ks[19], (DEPTH, D_FF, D_MODEL), D_FF ** -0.5),
        'norm_mlp_post': gain(ks[20], (DEPTH, D_MODEL)),
    }

def reference(x_prompt, x_sample, cache_attn_k, cache_attn_v, state_conv, state_delta,
              norm_mix_pre, w_in, rel_bias, conv_w, a_log, dt_bias, delta_norm_w,
              w_proj_a, w_proj_b, w_out, norm_mix_post, norm_mlp_pre, w_up, w_down, norm_mlp_post):
    b = x_prompt.shape[0]
    yp, ys = x_prompt, x_sample
    pk, pv, pc, ps = [], [], [], []
    sk, sv, sc, ss = [], [], [], []
    for l in range(DEPTH):
        weights = (norm_mix_pre[l], w_in[l], rel_bias[l], conv_w[l], a_log[l], dt_bias[l], delta_norm_w[l],
                   w_proj_a[l], w_proj_b[l], w_out[l], norm_mix_post[l], norm_mlp_pre[l], w_up[l], w_down[l],
                   norm_mlp_post[l])
        conv0 = jnp.zeros((b, CONV_WIDTH - 1, B_CONV_CH), yp.dtype)
        s0 = jnp.zeros((b, B_HEADS, B_DK, B_DV), jnp.float32)
        yp, k1, v1, c1, s1 = _layer(yp, None, None, conv0, s0, *weights)
        ys, k2, v2, c2, s2 = _layer(ys, cache_attn_k[l], cache_attn_v[l], state_conv[l], state_delta[l], *weights)
        pk.append(k1); pv.append(v1); pc.append(c1); ps.append(s1)
        sk.append(k2); sv.append(v2); sc.append(c2); ss.append(s2)
    return (yp, ys, jnp.stack(pk), jnp.stack(pv), jnp.stack(pc), jnp.stack(ps),
            jnp.stack(sk), jnp.stack(sv), jnp.stack(sc), jnp.stack(ss))


_drawn_inputs = setup_inputs


def setup_inputs(seed=0):
    import zlib

    import numpy as np

    out = dict(_drawn_inputs(seed))
    spreads = {}
    factors = {'dt_bias': 3.915,
     'delta_norm_w': 37.28,
     'norm_mix_post': 10.265,
     'norm_mlp_pre': 37.399,
     'norm_mlp_post': 64.425,
     'rel_bias': 6.114,
     'cache_attn_k': 3.377}
    for name, (base, spread) in spreads.items():
        noise = np.random.default_rng([zlib.crc32(name.encode()), seed]).standard_normal(out[name].shape)
        drawn = base * np.exp(spread * noise) if base else spread * noise
        out[name] = __import__('jax').numpy.asarray(drawn.astype(out[name].dtype))
    for name, factor in factors.items():
        out[name] = (out[name] * factor).astype(out[name].dtype)
    return out
```

```python
from contextlib import ExitStack

import concourse.bass as bass
from concourse import mybir

ALU = mybir.AluOpType
ACT = mybir.ActivationFunctionType
AX = mybir.AxisListType
F32 = mybir.dt.float32
F32R = mybir.dt.float32r

P = 128
D = 1024
DC = D // P
TP = 1024
NB, TS = 8, 16
T = TP + NB * TS
NT = T // P
NPT = TP // P
TG, NTG = 384, T // 384
AH, AD = 8, 64
AW = AH * AD
REACH = 512
NR = 128
HB, DK = 4, 128
CW = 4
CONV = 3 * HB * DK
CC = CONV // P
FF = 4 * D
EPS = 1e-6
NEG = -1.0e30
COL_Z = 3 * AW + CONV
COL_AB = COL_Z + HB * DK
COL_GATE = COL_AB + 2 * HB
NSLAB = (COL_AB // P, 2 * D // P)
LEVELS = (1, 2, 4, 8, 16, 32)
WRING = 2


def bc(ap, at, n):
    a = ap.unsqueeze(at)
    shape = list(a.shape)
    shape[at] = n
    return a.to_broadcast(shape)


class Env:
    pass


def sems(env, tag, *names):
    made = [env.nc.alloc_semaphore(name=f"{tag}_{n}") for n in names]
    env.sems += made
    return made


def clear_sems(env):
    env.nc.clear_and_free_semaphores(env.sems)
    env.nc.all_engine_barrier()
    env.sems = []


def weight_pipe(env, tag, c):
    nc = env.nc
    w = Env()
    w.raw = [c.enter_context(nc.sbuf_tensor(f"{tag}_w_raw{i}", [P, DC, P], F32)) for i in range(WRING)]
    w.hi = [c.enter_context(nc.sbuf_tensor(f"{tag}_w_hi{i}", [P, DC, P], F32R)) for i in range(WRING)]
    w.lo = [c.enter_context(nc.sbuf_tensor(f"{tag}_w_lo{i}", [P, DC, P], F32R)) for i in range(WRING)]
    w.landed = sems(env, tag, *[f"w_landed{i}" for i in range(WRING)])
    w.hi_made, w.lo_made, w.used = sems(env, tag, "w_hi_made", "w_lo_made", "w_used")
    return w


def load_slab(sp, w, i, s, src):
    sp.wait_ge(w.lo_made, 2 * i + s + 1)
    sp.dma_start(w.raw[s][:, :, :], src).then_inc(w.landed[s], 16)


def split_hi(act, w, i, s):
    act.wait_ge(w.landed[s], 16 * i + 16)
    act.wait_ge(w.used, 2 * i + s + 1)
    act.activation(w.hi[s][:, :, :], w.raw[s][:, :, :], ACT.Copy).then_inc(w.hi_made, 1)


def split_lo(pool, w, i, s):
    pool.wait_ge(w.hi_made, 2 * i + s + 1)
    pool.tensor_tensor(w.lo[s][:, :, :], w.raw[s][:, :, :], w.hi[s][:, :, :].bitcast(F32),
                       ALU.subtract).then_inc(w.lo_made, 1)


def slab_products(pe, w, s, x_hi, x_lo, out, chunks, tokens):
    n = 3 * len(chunks)
    k = 0
    for c in chunks:
        for a, b in ((w.lo, x_hi), (w.hi, x_lo), (w.hi, x_hi)):
            last = pe.matmul(out, a[s][:, c, :], b[:, c, tokens], start=k == 0, stop=k == n - 1)
            k += 1
    return last


def select(pool, out, pattern, base, cm, fill=0.0, op=ALU.is_ge):
    return pool.affine_select(out=out, in_=out, compare_op=op, fill=fill, base=base,
                              pattern=pattern, channel_multiplier=cm)


def stage_norm_in(env):
    nc, I = env.nc, env.inp
    loads, squared, rooted, inv, scaled, turned, gained, hi_made, lo_made, const, st_turned, st_copied, vec = sems(
        env, "n", "loads", "squared", "rooted", "inv", "scaled", "turned", "gained", "hi_made", "lo_made",
        "const", "st_turned", "st_copied", "vec")
    xl = sems(env, "n", *[f"x_landed{t}" for t in range(NT)])
    RING = 4
    with ExitStack() as c:
        x = c.enter_context(nc.sbuf_tensor("n_x", [P, NT, D], F32))
        junk = c.enter_context(nc.sbuf_tensor("n_junk", [P, D], F32))
        ss = c.enter_context(nc.sbuf_tensor("n_ss", [P, NT], F32))
        root = c.enter_context(nc.sbuf_tensor("n_root", [P, NT], F32))
        rstd = c.enter_context(nc.sbuf_tensor("n_rstd", [P, NT], F32))
        h = c.enter_context(nc.sbuf_tensor("n_h", [P, RING, 4, P], F32))
        st = c.enter_context(nc.sbuf_tensor("n_state", [NB * (CW - 1), CONV], F32))
        ps = [c.enter_context(nc.psum_tensor(f"n_ps{i}", [P, 4, P], F32)) for i in range(RING)]
        pst = c.enter_context(nc.psum_tensor("n_pst", [P, CC, NB * (CW - 1)], F32))
        xp = I["x_prompt"].rearrange("a (t p) d -> (a t) p d", p=P)
        xs = I["x_sample"].rearrange("b t d -> (b t) d")
        block = c.enter_context(nc.Block())
        NV = 9

        def out_of(x_part, g):
            return x_part[:, 4 * (g % 2):4 * (g % 2) + 4, (g // 2) * P:(g // 2 + 1) * P]

        def split(act, g):
            act.wait_ge(gained, g + 1)
            act.activation(out_of(env.x_hi, g), h[:, g % RING, :, :], ACT.Copy).then_inc(hi_made, 1)

        def gain(dve, g):
            dve.wait_ge(turned, g + 1)
            if g >= RING:
                dve.wait_ge(hi_made, g - RING + 1)
                dve.wait_ge(lo_made, g - RING + 1)
            half = g % 2
            dve.tensor_tensor(h[:, g % RING, :, :], ps[g % RING][:, :, :],
                              bc(env.gains[:, 0, 4 * half:4 * half + 4], 2, P), ALU.mult).then_inc(gained, 1)

        def split_low(pool, g):
            pool.wait_ge(hi_made, g + 1)
            pool.tensor_tensor(out_of(env.x_lo, g), h[:, g % RING, :, :],
                               out_of(env.x_hi, g).bitcast(F32), ALU.subtract).then_inc(lo_made, 1)

        @block.sync
        def _(sp):
            for t in range(NT):
                sp.dma_start(x[:, t, :], xp[t] if t < NPT else xs).then_inc(xl[t], 16)
            sp.dma_start(st[:, :], I["state_conv"].rearrange("l b w c -> (l b w) c")).then_inc(vec, 16)
            for k, name in enumerate(("norm_mix_pre", "norm_mix_post", "norm_mlp_pre", "norm_mlp_post")):
                sp.dma_start(env.gains[:, k, :], I[name].rearrange("l (c p) -> p (l c)", p=P),
                             allow_slow_non_contiguous=True).then_inc(vec, 16)
            sp.dma_start(env.convw[:, :, :], I["conv_w"].rearrange("l w (c p) -> p (l w) c", p=P),
                         allow_slow_non_contiguous=True).then_inc(vec, 16)
            sp.dma_start(env.dgain[:, :], I["delta_norm_w"].rearrange("l p -> p l"),
                         allow_slow_non_contiguous=True).then_inc(vec, 16)
            sp.dma_start(env.alog[:, :], I["a_log"].to_broadcast([P, HB])).then_inc(vec, 16)
            sp.dma_start(env.dtb[:, :], I["dt_bias"].to_broadcast([P, HB])).then_inc(vec, 16)
            sp.wait_ge(vec, 16 * NV)

        @block.scalar
        def _(act):
            act.wait_ge(const, 1)
            for t in range(NT):
                act.wait_ge(xl[t], 16)
                if t:
                    act.wait_ge(squared, t)
                act.activation(junk[:, :], x[:, t, :], ACT.Square,
                               accum_out=ss[:, t:t + 1]).then_inc(squared, 1)
                act.wait_ge(squared, t + 1)
                act.activation(root[:, t:t + 1], ss[:, t:t + 1], ACT.Sqrt, bias=env.eps[:, 0:1],
                               scale=1.0 / D).then_inc(rooted, 1)
                for g in range(2 * t, 2 * t + 2):
                    if g >= 2:
                        split(act, g - 2)
            split(act, 2 * NT - 2)
            split(act, 2 * NT - 1)

        @block.vector
        def _(dve):
            for t in range(NT):
                dve.wait_ge(rooted, t + 1)
                dve.reciprocal(rstd[:, t:t + 1], root[:, t:t + 1]).then_inc(inv, 1)
                dve.wait_ge(inv, t + 1)
                dve.tensor_scalar(x[:, t, :], x[:, t, :], rstd[:, t:t + 1], None, ALU.mult).then_inc(scaled, 1)
                if t == 0:
                    dve.wait_ge(vec, 16 * NV)
                    dve.wait_ge(st_turned, 1)
                    dve.tensor_copy(env.state_t[:, :, :], pst[:, :, :]).then_inc(st_copied, 1)
                for g in range(2 * t - 2, 2 * t):
                    if g >= 0:
                        gain(dve, g)
            gain(dve, 2 * NT - 2)
            gain(dve, 2 * NT - 1)

        @block.gpsimd
        def _(pool):
            pool.memset(env.eps[:, :], EPS).then_inc(const, 1)
            n = 1

            def fresh(ap, value):
                nonlocal n
                pool.memset(ap, value).then_inc(const, 1)
                n += 1
                pool.wait_ge(const, n)

            def sel(ap, *a, **k):
                nonlocal n
                select(pool, ap, *a, **k).then_inc(const, 1)
                n += 1
                pool.wait_ge(const, n)

            fresh(env.ident[:, :], 0.0)
            sel(env.ident[:, :], [[-1, P]], 0, 1, fill=1.0, op=ALU.not_equal)
            env.n_ident = n
            for g in range(2):
                split_low(pool, g)
            fresh(env.flip[:, :], 0.0)
            sel(env.flip[:, :], [[1, P]], 1 - P, 1, fill=1.0, op=ALU.not_equal)
            fresh(env.ones[:, :], 1.0)
            for k, L in enumerate((64, TS)):
                nb = P // L
                fresh(env.cum[:, k, :], 1.0)
                v = env.cum[:, k, :].rearrange("p (b r) -> p b r", r=L)
                sel(v, [[-L, nb], [0, L]], 0, 1)
                sel(v, [[L, nb], [0, L]], L - 1, -1)
                sel(v, [[L, nb], [1, L]], 0, -1)
                fresh(env.after[:, k, :], 1.0)
                v = env.after[:, k, :].rearrange("p (b r) -> p b r", r=L)
                sel(v, [[-L, nb], [0, L]], 0, 1)
                sel(v, [[L, nb], [0, L]], L - 1, -1)
                sel(v, [[-L, nb], [-1, L]], -1, 1)
                pool.tensor_scalar(env.shut[:, k, :], env.cum[:, k, :], -NEG, NEG, ALU.mult,
                                   ALU.add).then_inc(const, 1)
                n += 1
                pool.wait_ge(const, n)
                member = env.member[:, 0:2] if k == 0 else env.member[:, 2:2 + NB]
                fresh(member, 1.0)
                sel(member, [[-L, nb]], 0, 1)
                sel(member, [[L, nb]], L - 1, -1)
            for k, s in enumerate(LEVELS):
                nb = P // (2 * s)
                fresh(env.level[:, k, :], 1.0)
                v = env.level[:, k, :].rearrange("p (b r) -> p b r", r=2 * s)
                sel(v, [[-2 * s, nb], [0, 2 * s]], 0, 1)
                sel(v, [[2 * s, nb], [0, 2 * s]], s - 1, -1)
                sel(v, [[0, nb], [1, 2 * s]], -s, 0)
            for g in range(2, 2 * NT):
                split_low(pool, g)

        @block.tensor
        def _(pe):
            pe.wait_ge(const, 3)
            pe.wait_ge(vec, 16 * NV)
            r = NB * (CW - 1)
            for k in range(CC):
                last = pe.transpose(pst[:, k, :], st[:, k * P:(k + 1) * P], env.ident[0:r, 0:r])
            last.then_inc(st_turned, 1)
            for g in range(2 * NT):
                pe.wait_ge(scaled, g // 2 + 1)
                if g >= RING:
                    pe.wait_ge(gained, g - RING + 1)
                for k in range(4):
                    cc = 4 * (g % 2) + k
                    last = pe.transpose(ps[g % RING][:, k, :], x[:, g // 2, cc * P:(cc + 1) * P],
                                        env.ident[:, :])
                last.then_inc(turned, 1)


def stage_in_proj(env):
    nc, I = env.nc, env.inp
    with ExitStack() as c:
        w = weight_pipe(env, "i", c)
        prod, free, out_s0, out_s1, ab_made, conv_in, conv_y, conv_c, silued, ab_hi, ab_lo, ab_land, tail, halo = sems(
            env, "i", "prod", "free", "sent0", "sent1", "ab_made", "conv_in", "conv_y", "conv_c", "silued",
            "ab_hi", "ab_lo", "ab_land", "tail", "halo")
        sent = (out_s0, out_s1)
        wab = c.enter_context(nc.sbuf_tensor("i_wab", [P, DC, 2 * HB], F32))
        wab_hi = c.enter_context(nc.sbuf_tensor("i_wab_hi", [P, DC, 2 * HB], F32R))
        wab_lo = c.enter_context(nc.sbuf_tensor("i_wab_lo", [P, DC, 2 * HB], F32R))
        st = [c.enter_context(nc.sbuf_tensor(f"i_out{i}", [P, T], F32)) for i in range(2)]
        rp = [c.enter_context(nc.sbuf_tensor(f"i_raw_prompt{i}", [P, CW - 1 + TP], F32)) for i in range(2)]
        rs = [c.enter_context(nc.sbuf_tensor(f"i_raw_sample{i}", [P, NB, CW - 1 + TS], F32)) for i in range(2)]
        y = [c.enter_context(nc.sbuf_tensor(f"i_y{i}", [P, T], F32)) for i in range(2)]
        ps = [c.enter_context(nc.psum_tensor(f"i_ps{i}", [P, 512], F32)) for i in range(6)]
        pab = c.enter_context(nc.psum_tensor("i_pab", [P, NT, 2 * HB], F32))
        block = c.enter_context(nc.Block())
        NA, NC_, NZ = 3 * AW // P, CC, COL_Z // P
        NS = sum(NSLAB)
        w_in = I["w_in"].rearrange("l (c p) n -> p (l c) n", p=P)
        HALF = NS // 2
        CREDIT = 6

        @block.sync
        def _(sp):
            sp.dma_start(wab[:, :, :], w_in[:, :, COL_AB:COL_GATE]).then_inc(ab_land, 16)
            with sp.Fori(0, NSLAB[0] // 2) as i:
                for s in range(2):
                    load_slab(sp, w, i, s, w_in[:, :, bass.ds((2 * i + s) * P, P)])
            with sp.Fori(0, NSLAB[1] // 2) as i:
                for s in range(2):
                    load_slab(sp, w, i + NSLAB[0] // 2, s,
                              w_in[:, :, bass.ds((2 * i + s) * P + COL_GATE, P)])

        @block.gpsimd
        def _(pool):
            pool.sem_inc(w.lo_made, WRING)
            pool.wait_ge(ab_hi, 1)
            pool.tensor_tensor(wab_lo[:, :, :], wab[:, :, :], wab_hi[:, :, :].bitcast(F32),
                               ALU.subtract).then_inc(ab_lo, 1)
            with pool.Fori(0, HALF) as i:
                for s in range(2):
                    split_lo(pool, w, i, s)

        def store(act, i, s):
            act.dma_start(env.proj[bass.ds((2 * i + s) * P, P), :], st[s][:, :]).then_inc(sent[s], 16)

        @block.scalar
        def _(act):
            act.wait_ge(ab_land, 16)
            act.activation(wab_hi[:, :, :], wab[:, :, :], ACT.Copy).then_inc(ab_hi, 1)
            for s in range(2):
                split_hi(act, w, 0, s)

            def evacuated(i, s):
                act.wait_ge(free, 3 * (2 * i + s) + 3 + CREDIT)

            def plain(a, b):
                with act.Fori(a, b) as i:
                    for s in range(2):
                        split_hi(act, w, i + 1, s)
                        evacuated(i, s)
                        store(act, i, s)

            plain(0, NA // 2)
            with act.Fori(NA // 2, NZ // 2) as i:
                for s in range(2):
                    split_hi(act, w, i + 1, s)
                    n = 2 * i + s - NA
                    act.wait_ge(conv_c, n + 1)
                    act.wait_ge(sent[s], 16 * i + 16)
                    act.activation(st[s][:, :], y[s][:, :], ACT.Silu).then_inc(silued, 1)
                    act.wait_ge(silued, n + 3)
                    store(act, i, s)
            plain(NZ // 2, HALF - 1)
            for s in range(2):
                evacuated(HALF - 1, s)
                store(act, HALF - 1, s)
            for s in range(2):
                act.wait_ge(sent[s], 16 * HALF + 16)

        @block.vector
        def _(dve):
            dve.sem_inc(free, CREDIT)
            for s in range(2):
                dve.sem_inc(sent[s], 16)
            dve.sem_inc(silued, 2)
            for s in range(2):
                dve.memset(rp[s][:, 0:CW - 1], 0.0).then_inc(halo, 1)
            dve.wait_ge(ab_made, 1)
            dve.tensor_copy(env.ab[:, :, :], pab[:, :, :]).then_inc(tail, 1)

            def plain(a, b):
                with dve.Fori(a, b) as i:
                    for s in range(2):
                        dve.wait_ge(sent[s], 16 * i + 16)
                        for g in range(NTG):
                            m = 3 * (2 * i + s) + g
                            dve.wait_ge(prod, m + 1 + CREDIT)
                            dve.tensor_copy(st[s][:, g * TG:(g + 1) * TG],
                                            ps[3 * s + g][:, 0:TG]).then_inc(free, 1)

            plain(0, NA // 2)
            dve.wait_ge(halo, 2)
            with dve.Fori(NA // 2, NZ // 2) as i:
                for s in range(2):
                    n = 2 * i + s - NA
                    cc = n
                    hist = CW - 1
                    dve.tensor_copy(rs[s][:, :, 0:hist],
                                    env.state_t[:, bass.ds(cc, 1), :].rearrange("p a (b w) -> p (a b) w", w=hist)
                                    ).then_inc(conv_in, 1)
                    for g in range(NTG):
                        m = 3 * (2 * i + s) + g
                        dve.wait_ge(prod, m + 1 + CREDIT)
                        if g < NTG - 1:
                            dve.tensor_copy(rp[s][:, hist + g * TG:hist + (g + 1) * TG],
                                            ps[3 * s + g][:, 0:TG]).then_inc(free, 1)
                        else:
                            rest = TP - g * TG
                            dve.tensor_copy(rp[s][:, hist + g * TG:hist + TP],
                                            ps[3 * s + g][:, 0:rest]).then_inc(conv_in, 1)
                            dve.tensor_copy(rs[s][:, :, hist:],
                                            ps[3 * s + g][:, rest:TG].rearrange("p (b t) -> p b t", t=TS)
                                            ).then_inc(free, 1)
                    dve.wait_ge(free, 3 * (2 * i + s) + 3 + CREDIT)
                    dve.wait_ge(conv_in, 2 * n + 2)
                    dve.tensor_copy(env.conv_tail[:, bass.ds(cc, 1), 0:hist],
                                    rp[s][:, TP:TP + hist].unsqueeze(1)).then_inc(tail, 1)
                    dve.tensor_copy(env.conv_tail[:, bass.ds(cc, 1), hist:].rearrange("p a (b w) -> p (a b) w", w=hist),
                                    rs[s][:, :, TS:TS + hist]).then_inc(tail, 1)
                    dve.wait_ge(silued, n + 1)
                    for j in range(CW):
                        for half in range(2):
                            if half == 0:
                                o, v = y[s][:, 0:TP], rp[s][:, j:j + TP]
                            else:
                                o = y[s][:, TP:].rearrange("p (b t) -> p b t", t=TS)
                                v = rs[s][:, :, j:j + TS]
                            wj = env.convw[:, j, bass.ds(cc, 1)]
                            if j == 0:
                                ins = dve.tensor_scalar(o, v, wj, None, ALU.mult)
                            else:
                                dve.wait_ge(conv_y, 6 * n + 2 * (j - 1) + half + 1)
                                ins = dve.scalar_tensor_tensor(out=o, in0=v, scalar=wj, in1=o,
                                                               op0=ALU.mult, op1=ALU.add)
                            if j < CW - 1:
                                ins.then_inc(conv_y, 1)
                            elif half == 1:
                                ins.then_inc(conv_c, 1)
            plain(NZ // 2, HALF)

        @block.tensor
        def _(pe):
            pe.sem_inc(prod, CREDIT)
            pe.sem_inc(w.used, WRING)
            pe.wait_ge(ab_lo, 1)
            for t in range(NT):
                k = 0
                for cc in range(DC):
                    for a, b in ((env.x_lo, wab_hi), (env.x_hi, wab_lo), (env.x_hi, wab_hi)):
                        last = pe.matmul(pab[:, t, :], a[:, cc, t * P:(t + 1) * P], b[:, cc, :],
                                         start=k == 0, stop=k == 3 * DC - 1)
                        k += 1
            last.then_inc(ab_made, 1)
            with pe.Fori(0, HALF) as i:
                for s in range(2):
                    pe.wait_ge(w.lo_made, 2 * i + s + 1 + WRING)
                    for g in range(NTG):
                        m = 3 * (2 * i + s) + g
                        pe.wait_ge(free, m + 1)
                        last = slab_products(pe, w, s, env.x_hi, env.x_lo, ps[3 * s + g][:, 0:TG],
                                             range(DC), slice(g * TG, (g + 1) * TG))
                        last.then_inc(prod, 1)
                    pe.wait_ge(prod, 3 * (2 * i + s) + 3 + CREDIT)
                    pe.sem_inc(w.used, 1)


def stage_attention(env):
    nc, I, O_ = env.nc, env.inp, env.out
    SC = AD ** -0.5
    KEYS = 5 * P
    NPU = NPT * AH
    NU = NPU + NB
    SR = 4
    HIST = CW - 1
    ROWS = (NB + 1) * HIST
    k_l0, v_l0, k_l1, v_l1 = sems(env, "a", "k_cache_landed0", "v_cache_landed0", "k_cache_landed1",
                                  "v_cache_landed1")
    k_landed, v_landed = (k_l0, k_l1), (v_l0, v_l1)
    qk_in, v_in, rb_in, ext_out, hank_in, sb_in = sems(env, "a", "qk_in", "v_in", "rb_in", "ext_out", "hank_in", "sb_in")
    ext_made, pre_made, pre_a, pre_d, bias_made, saved = sems(
        env, "a", "ext_made", "pre_made", "pre_read_act", "pre_read_dve", "bias_made", "saved")
    s_made, s_read, s_biased, s_max, p_made, p_scaled = sems(
        env, "a", "s_made", "s_read", "s_biased", "s_max", "p_made", "p_scaled")
    tr_made, tr_read, av_made, av_read, r_made, qd_made = sems(
        env, "a", "tr_made", "tr_read", "av_made", "av_read", "r_made", "qd_made")
    with ExitStack() as c:
        def sb(name, shape):
            return c.enter_context(nc.sbuf_tensor("a_" + name, shape, F32))

        q, k, v = (sb(n, [P, 4, T]) for n in ("q", "k", "v"))
        vt = sb("v_tok", [P, NT, AW])
        k_out = sb("k_out", [P, NT - NPT // 2, AW])
        tail_out = sb("tail_out", [ROWS, CONV])
        bias = sb("bias", [P, AH, 2 * P])
        bias_s = sb("bias_s", [P, P + TS])
        bias_own = sb("bias_own", [P, NB * (P + TS)])
        bias_own_b = bias_own[:, 0:NB * P].rearrange("p (b m) -> p b m", m=P)
        bias_own_d = bias_own[:, :].rearrange("p (b m) -> p b m", m=P + TS)[:, :, 0:TS]
        rb, ext = sb("rb", [AH, 2 * NR + 1]), sb("ext", [AH, 3 * P])
        kc = [sb(f"k_cache{i}", [P, 4, AW]) for i in range(2)]
        vc = [sb(f"v_cache{i}", [P, 4, AW]) for i in range(2)]
        kt = [sb(f"k_cache_t{i}", [P, 4, REACH]) for i in range(2)]
        hank = kt[0][:, :, :].rearrange("p a b -> p (a b)").rearrange("p (h m) -> p h m", m=2 * P)
        qd = [sb(f"q_diag{i}", [P, 4 * (P + 2 * TS)]) for i in range(2)]
        qd_b = [x[:, 0:4 * P].rearrange("p (j m) -> p j m", m=P) for x in qd]
        qd_d = [x[:, :].rearrange("p (j m) -> p j m", m=P + 2 * TS) for x in qd]
        s = [sb(f"s{i}", [P, KEYS]) for i in range(SR)]
        nmax, rsum, rinv = sb("nmax", [P, SR]), sb("rsum", [P, SR]), sb("rinv", [P, SR])
        pt = [sb(f"p_t{i}", [P, KEYS]) for i in range(2)]
        ot = [sb(f"o_tok{i}", [P, AW]) for i in range(2)]
        S = [c.enter_context(nc.psum_tensor(f"a_S{i}", [P, 1024], F32)) for i in range(2)]
        TR = c.enter_context(nc.psum_tensor("a_TR", [P, 1024], F32))
        O = [c.enter_context(nc.psum_tensor(f"a_O{i}", [P, 512], F32)) for i in range(2)]
        scratch = nc.dram_tensor("bias_ext", [AH, 3 * P], F32).ap()
        overlap = bass.AP(scratch.tensor, 0, [[1, P], [3 * P, AH], [1, 2 * P]])
        block = c.enter_context(nc.Block())

        PRE = ([("v", t) for t in range(NT)] + [("k", t) for t in range(NPT // 2, NT)]
               + [("tail", t) for t in range(CC // 4)] + [("bias", t) for t in range(AH // 2)])
        NPRE = len(PRE)
        banks = [S[0][:, 0:512], S[0][:, 512:1024], S[1][:, 0:512], S[1][:, 512:1024]]

        def keys_of(u):
            b, h = divmod(u, AH)
            n = min(b + 1, 5)
            return b, h, n, (b - n + 1) * P

        def jobs(st):
            out = []
            if 0 <= st - 2 < NU:
                out.append(("P", st - 2))
            if NPU <= st + 1 < NU:
                out += [("K", 2 * (st + 1 - NPU)), ("K", 2 * (st + 1 - NPU) + 1)]
            if st >= 12 and (st - 12) % AH == 0 and (st - 12) // AH < NPT:
                out.append(("O", (st - 12) // AH))
            return out

        STEPS = NU + 6
        order = [j for st in range(STEPS) for j in jobs(st)]
        job = {j: n for n, j in enumerate(order)}

        @block.sync
        def _(sp):
            sp.dma_start(rb[:, :], I["rel_bias"].rearrange("l h r -> (l h) r")).then_inc(rb_in, 16)
            for dst, row, sem in ((v, 2 * AW, v_in), (q, 0, qk_in), (k, AW, qk_in)):
                sp.dma_start(dst[:, :, :], env.proj[row:row + AW, :].rearrange("(c p) t -> p c t", p=P)
                             ).then_inc(sem, 16)
            sp.wait_ge(ext_made, 2)
            sp.dma_start(scratch, ext[:, :]).then_inc(ext_out, 16)
            sp.wait_ge(ext_out, 16)
            sp.dma_start(hank, overlap).then_inc(hank_in, 16)
            def load_k(b):
                if b >= 2:
                    sp.wait_ge(tr_made, job["K", 2 * (b - 2) + 1] + 1)
                sp.dma_start(kc[b % 2][:, :, :], I["cache_attn_k"][0, b].rearrange("(t p) h d -> p t (h d)", p=P)
                             ).then_inc(k_landed[b % 2], 16)

            def load_v(b):
                if b >= 2:
                    sp.wait_ge(av_made, NPU + b - 1)
                sp.dma_start(vc[b % 2][:, :, :], I["cache_attn_v"][0, b].rearrange("(t p) h d -> p t (h d)", p=P)
                             ).then_inc(v_landed[b % 2], 16)

            for b in range(2):
                load_k(b)
                load_v(b)
            sp.wait_ge(pre_d, (NPRE) // 2)
            sp.wait_ge(pre_a, (NPRE + 1) // 2)
            for h in range(AH):
                sp.dma_start(bias_s[h * TS:(h + 1) * TS, :], bias[0:TS, h, 0:P + TS]).then_inc(sb_in, 16)
            half = NPT // 2
            for name, src in (("k", k_out[:, 0:half, :]), ("v", vt[:, half:NPT, :])):
                sp.dma_start(O_[f"prompt_{name}"].rearrange("l a (t p) h d -> p (l a t) (h d)", p=P),
                             src).then_inc(saved, 16)
            for name, src in (("k", k_out[:, half, :]), ("v", vt[:, NPT, :])):
                sp.dma_start(O_[f"sample_{name}"].rearrange("l b t h d -> (l b t) (h d)"),
                             src).then_inc(saved, 16)
            sp.dma_start(O_["prompt_conv"].rearrange("l a w c -> (l a w) c"),
                         tail_out[0:HIST, :]).then_inc(saved, 16)
            sp.dma_start(O_["sample_conv"].rearrange("l b w c -> (l b w) c"),
                         tail_out[HIST:ROWS, :]).then_inc(saved, 16)
            load_k(2)
            load_k(3)
            for b in range(2, NB):
                if b + 2 < NB:
                    load_k(b + 2)
                load_v(b)
            sp.wait_ge(saved, 16 * 6)

        def pre_read(eng, n, copy, sem):
            kind, t = PRE[n]
            eng.wait_ge(pre_made, n + 1)
            bank = banks[n % 4]
            if kind == "v":
                dst, src = vt[:, t, :], bank
            elif kind == "k":
                dst, src = k_out[:, t - NPT // 2, :], bank
            elif kind == "tail":
                dst, src = tail_out[:, t * 512:(t + 1) * 512], bank[0:ROWS, :]
            else:
                dst, src = bias[:, 2 * t:2 * t + 2, :].rearrange("p h m -> p (h m)"), bank
            copy(dst, src).then_inc(sem, 1)

        @block.scalar
        def _(act):
            for n in range(0, NPRE, 2):
                pre_read(act, n, lambda d, x: act.activation(d, x, ACT.Copy), pre_a)

            def tr_out(j):
                kind, x = j
                act.wait_ge(tr_made, job[j] + 1)
                if kind == "P":
                    n = keys_of(x)[2] * P if x < NPU else KEYS
                    if x >= 2:
                        act.wait_ge(av_made, x - 1)
                    dst, src = pt[x % 2][:, 0:n], TR[:, 0:n]
                elif kind == "K":
                    b, half = divmod(x, 2)
                    if b >= 2:
                        act.wait_ge(s_made, NPU + b - 1)
                    dst = kt[b % 2][:, 2 * half:2 * half + 2, :].rearrange("p a b -> p (a b)")
                    src = TR[:, :]
                else:
                    dst = env.oa[:, :, x * P:(x + 1) * P]
                    src = TR[:, 0:AW].rearrange("p (c m) -> p c m", m=P)
                act.activation(dst, src, ACT.Copy).then_inc(tr_read, 1)

            for st in range(STEPS):
                for j in jobs(st):
                    tr_out(j)
                if st < NU:
                    n = keys_of(st)[2] * P if st < NPU else KEYS
                    act.wait_ge(s_max, st + 1)
                    if st >= SR:
                        act.wait_ge(r_made, st - SR + 1)
                    x = s[st % SR][:, 0:n]
                    act.activation(x, x, ACT.Exp, bias=nmax[:, st % SR:st % SR + 1],
                                   accum_out=rsum[:, st % SR:st % SR + 1]).then_inc(p_made, 1)

        @block.vector
        def _(dve):
            dve.wait_ge(rb_in, 16)
            dve.tensor_copy(ext[:, 0:2 * P], rb[:, 1:2 * NR + 1]).then_inc(ext_made, 1)
            dve.tensor_copy(ext[:, 2 * P:3 * P], rb[:, 2 * NR:2 * NR + 1].to_broadcast([AH, P])
                            ).then_inc(ext_made, 1)
            for i in range(2):
                dve.memset(qd[i][:, :], 0.0).then_inc(qd_made, 1)
            dve.memset(bias_own[:, :], NEG).then_inc(bias_made, 1)
            for n in range(1, NPRE, 2):
                pre_read(dve, n, dve.tensor_copy, pre_d)
            dve.wait_ge(pre_a, (NPRE + 1) // 2)
            dve.wait_ge(pre_d, NPRE // 2)
            dve.memset(bias[0:64, :, P + 64:2 * P], NEG).then_inc(bias_made, 1)
            dve.wait_ge(bias_made, 2)
            dve.wait_ge(sb_in, 16 * AH)
            dve.tensor_copy(bias_own_d, bc(bias_s[:, P:P + TS], 1, NB)).then_inc(bias_made, 1)

            biased = 0
            n_qd = 2

            def soft(u):
                nonlocal biased
                r = u % SR
                x, ps = s[r], S[u % 2]
                dve.wait_ge(s_made, u + 1)
                if u >= SR:
                    dve.wait_ge(tr_made, job["P", u - SR] + 1)
                if u < NPU:
                    b, h, n, _ = keys_of(u)
                    W, near = n * P, min(n * P, 2 * P)
                    if W > near:
                        dve.tensor_scalar(x[:, 0:W - near], ps[:, 0:W - near], SC, bias[:, h, 0:1],
                                          ALU.mult, ALU.add).then_inc(s_biased, 1)
                        biased += 1
                    dve.scalar_tensor_tensor(out=x[:, W - near:W], in0=ps[:, W - near:W], scalar=SC,
                                             in1=bias[:, h, 2 * P - near:2 * P], op0=ALU.mult,
                                             op1=ALU.add).then_inc(s_read, 1)
                    dve.wait_ge(s_read, u + 1)
                    if W > near:
                        dve.wait_ge(s_biased, biased)
                    if n == 5:
                        dve.memset(x[64:P, 0:64], NEG).then_inc(s_biased, 1)
                        biased += 1
                        dve.wait_ge(s_biased, biased)
                else:
                    W, b = KEYS, u - NPU
                    dve.tensor_scalar(x[:, 0:3 * P], ps[:, 0:3 * P], SC, bias_s[:, 0:1],
                                      ALU.mult, ALU.add).then_inc(s_biased, 1)
                    dve.scalar_tensor_tensor(out=x[:, 3 * P:4 * P], in0=ps[:, 3 * P:4 * P], scalar=SC,
                                             in1=bias_s[:, 0:P], op0=ALU.mult, op1=ALU.add).then_inc(s_biased, 1)
                    if b == 0:
                        dve.wait_ge(bias_made, 3)
                    dve.scalar_tensor_tensor(out=x[:, 4 * P:5 * P], in0=ps[:, 4 * P:5 * P], scalar=SC,
                                             in1=bias_own_b[:, b, :], op0=ALU.mult, op1=ALU.add).then_inc(s_read, 1)
                    biased += 2
                    dve.wait_ge(s_read, u + 1)
                    dve.wait_ge(s_biased, biased)
                if u >= SR:
                    dve.wait_ge(p_made, u - SR + 1)
                dve.tensor_reduce(nmax[:, r:r + 1], x[:, 0:W], AX.X, ALU.max, negate=True).then_inc(s_max, 1)

            def recip(u):
                r = u % SR
                dve.wait_ge(p_made, u + 1)
                if u >= SR:
                    dve.wait_ge(av_read, u - SR + 1)
                dve.reciprocal(rinv[:, r:r + 1], rsum[:, r:r + 1]).then_inc(r_made, 1)
                dve.wait_ge(r_made, u + 1)

            def out(u):
                r = u % SR
                if u < NPU:
                    b, h = divmod(u, AH)
                    dve.wait_ge(av_made, u + 1)
                    if b >= 2 and h == 0:
                        dve.wait_ge(tr_made, job["O", b - 2] + 1)
                    dve.tensor_scalar(ot[b % 2][:, h * AD:(h + 1) * AD], O[u % 2][:, 0:AD],
                                      rinv[:, r:r + 1], None, ALU.mult).then_inc(av_read, 1)
                else:
                    b = u - NPU
                    dve.wait_ge(av_made, u + 1)
                    for half in range(2):
                        src = O[u % 2][64 * half:64 * half + 64, 0:4 * 2 * TS].rearrange("p (j m) -> p j m", m=2 * TS)
                        ins = dve.tensor_copy(
                            env.oa[64 * half:64 * half + 64, :, TP + TS * b:TP + TS * (b + 1)],
                            src[:, :, TS * half:TS * half + TS])
                    ins.then_inc(av_read, 1)

            for st in range(STEPS):
                if st < NU:
                    soft(st)
                if NPU <= st + 1 < NU:
                    b = st + 1 - NPU
                    if n_qd == 2:
                        dve.wait_ge(qd_made, 2)
                    if b >= 2:
                        dve.wait_ge(s_made, NPU + b - 1)
                    for half in range(2):
                        dve.tensor_copy(qd_d[b % 2][64 * half:64 * half + 64, :, TS * half:TS * half + TS],
                                        q[64 * half:64 * half + 64, :, TP + TS * b:TP + TS * (b + 1)]
                                        ).then_inc(qd_made, 1)
                    n_qd += 2
                u = st - 1
                if 0 <= u < NU:
                    recip(u)
                if NPU <= u < NU:
                    x = s[u % SR][:, :]
                    dve.tensor_scalar(x, x, rinv[:, u % SR:u % SR + 1], None, ALU.mult).then_inc(p_scaled, 1)
                if 0 <= st - 3 < NU:
                    out(st - 3)

        @block.tensor
        def _(pe):
            for n, (kind, t) in enumerate(PRE):
                if n >= 4:
                    pe.wait_ge(pre_a if n % 2 == 0 else pre_d, (n - 4) // 2 + 1)
                bank = banks[n % 4]
                if n == 0:
                    pe.wait_ge(v_in, 16)
                if kind == "k":
                    pe.wait_ge(qk_in, 32)
                if kind == "bias" and t == 0:
                    pe.wait_ge(hank_in, 16)
                for i in range(4):
                    o = bank[:, i * P:(i + 1) * P]
                    if kind == "v":
                        last = pe.transpose(o, v[:, i, t * P:(t + 1) * P], env.ident[:, :])
                    elif kind == "k":
                        last = pe.transpose(o, k[:, i, t * P:(t + 1) * P], env.ident[:, :])
                    elif kind == "tail":
                        last = pe.transpose(bank[0:ROWS, i * P:(i + 1) * P], env.conv_tail[:, 4 * t + i, :],
                                            env.ident[:, :])
                    else:
                        h, half = 2 * t + i // 2, i % 2
                        last = pe.matmul(o, hank[:, h, (1 - half) * P:(2 - half) * P], env.flip[:, :],
                                         start=True, stop=True)
                last.then_inc(pre_made, 1)
            pe.wait_ge(pre_a, (NPRE + 1) // 2)
            pe.wait_ge(pre_d, NPRE // 2)

            def scores(u):
                if u >= 2:
                    pe.wait_ge(s_read, u - 1)
                ps = S[u % 2]
                if u < NPU:
                    b, h, n, k0 = keys_of(u)
                    base, cc = AD * (h % 2), h // 2
                    for a in range(0, n * P, 512):
                        z = min(n * P, a + 512)
                        last = pe.matmul(ps[:, a:z], q[base:base + AD, cc, b * P:(b + 1) * P],
                                         k[base:base + AD, cc, k0 + a:k0 + z], start=True, stop=True)
                else:
                    b = u - NPU
                    pe.wait_ge(tr_read, job["K", 2 * b + 1] + 1)
                    pe.wait_ge(qd_made, 2 + 2 * (b + 1))
                    for j in range(4):
                        pe.matmul(ps[:, 0:REACH], qd_b[b % 2][:, j, :], kt[b % 2][:, j, :],
                                  start=j == 0, stop=j == 3)
                    for j in range(4):
                        last = pe.matmul(ps[:, REACH:KEYS], qd_b[b % 2][:, j, :], k[:, j, TP:T],
                                         start=j == 0, stop=j == 3)
                last.then_inc(s_made, 1)

            def turn(j):
                kind, x = j
                if job[j]:
                    pe.wait_ge(tr_read, job[j])
                if kind == "P":
                    if x < NPU:
                        pe.wait_ge(p_made, x + 1)
                        n = keys_of(x)[2]
                    else:
                        pe.wait_ge(p_scaled, x - NPU + 1)
                        n = 5
                    for i in range(n):
                        last = pe.transpose(TR[:, i * P:(i + 1) * P], s[x % SR][:, i * P:(i + 1) * P],
                                            env.ident[:, :])
                elif kind == "K":
                    b, half = divmod(x, 2)
                    pe.wait_ge(k_landed[b % 2], 16 * (b // 2 + 1))
                    for i in range(8):
                        pair, t = 2 * half + i // 4, i % 4
                        last = pe.transpose(TR[:, i * P:(i + 1) * P], kc[b % 2][:, t, pair * P:(pair + 1) * P],
                                            env.ident[:, :])
                else:
                    pe.wait_ge(av_read, AH * (x + 1))
                    for i in range(4):
                        last = pe.transpose(TR[:, i * P:(i + 1) * P], ot[x % 2][:, i * P:(i + 1) * P],
                                            env.ident[:, :])
                last.then_inc(tr_made, 1)

            def values(u):
                pe.wait_ge(tr_read, job["P", u] + 1)
                if u >= 2:
                    pe.wait_ge(av_read, u - 1)
                if u < NPU:
                    b, h, n, k0 = keys_of(u)
                    for i in range(n):
                        last = pe.matmul(O[u % 2][:, 0:AD], pt[u % 2][:, i * P:(i + 1) * P],
                                         vt[:, k0 // P + i, h * AD:(h + 1) * AD], start=i == 0, stop=i == n - 1)
                else:
                    b = u - NPU
                    pe.wait_ge(v_landed[b % 2], 16 * (b // 2 + 1))
                    for j in range(4):
                        for i in range(5):
                            vals = vc[b % 2][:, i, j * P:(j + 1) * P] if i < 4 else vt[:, NPT, j * P:(j + 1) * P]
                            last = pe.matmul(O[u % 2][:, 2 * TS * j:2 * TS * (j + 1)], vals,
                                             pt[u % 2][:, i * P + 2 * TS * j:i * P + 2 * TS * (j + 1)],
                                             start=i == 0, stop=i == 4)
                last.then_inc(av_made, 1)

            for st in range(STEPS):
                if st < NU:
                    scores(st)
                for j in jobs(st):
                    if j[0] != "O":
                        turn(j)
                if 0 <= st - 3 < NU:
                    values(st - 3)
                for j in jobs(st):
                    if j[0] == "O":
                        turn(j)


def stage_delta(env):
    nc, I, O_ = env.nc, env.inp, env.out
    L = 64
    KD = DK
    PAIRS = [tuple(range(t, min(t + 2, NT))) for t in range(0, NT, 2)]

    def levels(t):
        return len(LEVELS) if t < NPT else 4

    def steps(t):
        inv = [(f"inv{j}{x}") for j in range(1, levels(t)) for x in "ab"]
        return ["turn", "norm_turn", "decay", "pair", "inv0"] + inv + ["solve"]

    PIECES = ("read", "write")

    def schedule():
        out = []
        for p, tiles in enumerate(PAIRS):
            scan = [("scan", t, ch, x) for t in (PAIRS[p - 1] if p else ()) for ch in range(2) for x in PIECES]
            for k in range(len(steps(0))):
                out += [("prep", t, steps(t)[k]) for t in tiles if k < len(steps(t))]
                if k % 2 and scan:
                    out.append(scan.pop(0))
            out += [x for x in scan]
        return out + [("heads", NPT, h, x) for h in range(HB) for x in ("read", "mask", "write")]

    SCHED = schedule()

    def has(eng, item):
        kind, t, *rest = item
        if kind == "prep":
            s = rest[0]
            lev = int(s[3]) if s.startswith("inv") else None
            return {"pe": True,
                    "act": s in ("turn", "norm_turn", "decay", "solve") or s.endswith("a"),
                    "dve": s in ("turn", "decay", "pair", "inv0") or s.endswith("b"),
                    "pool": s in ("norm_turn", "pair", "inv0") or (s.endswith("a") and lev + 1 < levels(t))}[eng]
        if kind == "scan":
            ch, x = rest
            return {"pe": True, "dve": True, "act": x == "write" and ch == 1, "pool": x == "read"}[eng]
        h, x = rest
        return {"pe": x != "mask", "dve": True, "act": x == "write" and h == HB - 1, "pool": x == "mask"}[eng]

    place = {}
    for eng in ("pe", "act", "dve", "pool"):
        for kind in ("prep", "scan", "heads"):
            for n, item in enumerate(x for x in SCHED if x[0] == kind and has(eng, x)):
                place[(eng, *item)] = n + 1

    sem = {}
    for eng, what in (("pe", "products"), ("act", "moved"), ("dve", "combined"), ("pool", "masked")):
        for kind in ("prep", "scan", "heads"):
            sem[eng, kind], = sems(env, "d", f"{kind}_{what}")

    def wait(e, eng, *item):
        e.wait_ge(sem[eng, item[0]], place[(eng, *item)])

    def did(eng, ins, item):
        ins.then_inc(sem[eng, item[0]], 1)

    c_in, z_in, sq_made, ss_made, ss_read, vecs, gates, gmat, sums, cleared, dstep = sems(
        env, "d", "c_in", "z_in", "sq_made", "ss_made", "ss_read", "vecs", "gates", "gmat", "sums", "cleared", "dstep")
    st_l = sems(env, "d", "state_landed0", "state_landed1")
    sent0, sent1, z_ready, o_norm, o_turned, o_out, o_root, actv, own = sems(
        env, "d", "state_sent0", "state_sent1", "z_ready", "o_norm", "o_turned", "o_out", "o_root", "actv", "own")
    sent = (sent0, sent1)
    with ExitStack() as c:
        def sb(name, shape):
            return c.enter_context(nc.sbuf_tensor("d_" + name, shape, F32))

        C = sb("c", [P, CC, T])
        pairb = sb("pair", [P, 18, 512])

        def slot2(i, t):
            return pairb[:, 9 * (t % 2) + i, :].rearrange("p (h m) -> p h m", m=P)

        kn, kb, qn, qd, kbe, knT, kbT, qnT, AT = (lambda t, i=i: slot2(i, t) for i in range(9))
        Dm, DT, X, M0, M1 = kn, kb, qn, qd, kbT
        quad = sb("quad", [P, 20, 512])

        def slot4(i, t):
            return quad[:, 5 * (t % 4) + i, :].rearrange("p (h m) -> p h m", m=P)

        kd, qdT, QK, WT, U = (lambda t, i=i: slot4(i, t) for i in range(5))
        vn = sb("v_new", [P, HB, P])
        S, Sd = sb("state", [P, HB, P]), sb("state_decayed", [P, HB, P])
        vec = sb("vec", [P, 14, NT, HB])
        (sp_m, sp_e, g, beta, gc, eg, er, s_kn, s_kb, s_kbe, s_kd, s_qn, s_qd, at) = (vec[:, i, :, :] for i in range(14))
        nea = sb("nea", [P, HB])
        ss, rs = sb("ss", [P, NT, 2 * HB]), sb("rs", [P, NT, 2 * HB])
        sso, rso = sb("sso", [P, NT, HB]), sb("rso", [P, NT, HB])
        gm = sb("gm", [P, 2 * NPT + NB, HB])
        gl = sb("g_last", [P, 2 * NPT + NB, HB])
        sqo = sb("sqo", [P, HB, P])
        SQR = 3
        sq = [pairb[:, 3 * i:3 * i + 3, :].rearrange("p a b -> p (a b)")[:, 0:T] for i in range(SQR)]
        flat = pairb[:, :, :].rearrange("p a b -> p (a b)")
        W_ = NB * (P + TS)
        sh = [flat[:, i * 1024:(i + 1) * 1024].rearrange("p (b v) -> p b v", v=P) for i in range(2)]
        wm, qm = flat[:, 2048:2048 + W_], flat[:, 2048 + W_:2048 + 2 * W_]
        vm = flat[:, 2048 + 2 * W_:2048 + 2 * W_ + 1024].rearrange("p (b v) -> p b v", v=P)
        B = [[c.enter_context(nc.psum_tensor(f"d_B{i}{j}", [P, HB, P], F32)) for j in range(3)] for i in range(2)]
        Z6, Z7 = (c.enter_context(nc.psum_tensor(f"d_Z{i}", [P, HB, P], F32)) for i in (6, 7))
        block = c.enter_context(nc.Block())

        def kb_of(t):
            return 0 if t < NPT else 1

        def store_state(sp, h):
            wait(sp, "dve", "heads", NPT, h, "write")
            sp.dma_start(O_["sample_delta"][0, :, h].rearrange("b k v -> k b v"), sh[h % 2]).then_inc(sent[h % 2], 16)

        def squares(dve, item):
            wait(dve, "act", *item)
            dve.tensor_reduce(sso[:, item[1], :], sqo[:, :, :], AX.X, ALU.add).then_inc(dstep, 1)

        @block.sync
        def _(sp):
            for a, z in ((0, 4), (4, 8), (8, 12)):
                sp.dma_start(C[:, a:z, :], env.proj[3 * AW + a * P:3 * AW + z * P, :].rearrange("(c p) t -> p c t", p=P)
                             ).then_inc(c_in, 16)
                sp.wait_ge(c_in, 16 * (a // 4 + 1))
            wait(sp, "pe", "prep", NPT, "turn")
            sp.dma_start(C[:, 8:12, :], env.proj[COL_Z:COL_Z + 4 * P, :].rearrange("(c p) t -> p c t", p=P)
                         ).then_inc(z_in, 16)
            wait(sp, "dve", "scan", NPT - 1, 1, "write")
            sp.dma_start(O_["prompt_delta"].rearrange("l a h k v -> k (l a h) v"), S[:, :, :]).then_inc(own, 16)
            wait(sp, "act", "prep", NPT, "solve")
            wait(sp, "pe", "prep", NPT, "solve")
            wait(sp, "dve", "prep", NPT, "inv3b")
            for h in range(HB):
                if h >= 2:
                    sp.wait_ge(sent[h % 2], 16 * (h // 2))
                sp.dma_start(sh[h % 2], I["state_delta"][0, :, h].rearrange("b k v -> k b v")).then_inc(st_l[h % 2], 16)
                if h >= 1:
                    store_state(sp, h - 1)
            store_state(sp, HB - 1)
            sp.wait_ge(sent[0], 32)
            sp.wait_ge(sent[1], 32)
            sp.wait_ge(own, 16)

        @block.gpsimd
        def _(pool):
            pool.memset(S[:, :, :], 0.0).then_inc(cleared, 1)
            for item in SCHED:
                kind, t, *rest = item
                if not has("pool", item):
                    continue
                if kind == "prep":
                    s = rest[0]
                    if s == "norm_turn":
                        if t == 0:
                            pool.wait_ge(gates, 1)
                            pool.wait_ge(ss_made, 8)
                        if t >= 2:
                            wait(pool, "dve", "prep", t - 2, f"inv{levels(t - 2) - 1}b")
                        ins = pool.tensor_tensor(AT(t), bc(env.cum[:, kb_of(t), :], 1, HB), bc(g[:, t, :], 2, P), ALU.mult)
                    elif s == "pair":
                        wait(pool, "dve", "prep", t, "pair")
                        wait(pool, "pe", "prep", t, "decay")
                        ins = pool.tensor_tensor(M0(t), AT(t), bc(env.level[:, 0, :], 1, HB), ALU.mult)
                    elif s == "inv0":
                        wait(pool, "pool", "prep", t, "pair")
                        pool.tensor_tensor(DT(t), bc(env.ident[:, :], 1, HB), M0(t), ALU.subtract)
                        wait(pool, "pe", "prep", t, "pair")
                        ins = pool.tensor_tensor(M1(t), AT(t), bc(env.level[:, 1, :], 1, HB), ALU.mult)
                    else:
                        j = int(s[3])
                        wait(pool, "pe", "prep", t, f"inv{j - 1}a" if j > 1 else "inv0")
                        if j == 1:
                            wait(pool, "pool", "prep", t, "inv0")
                        M = (M0, M1)[(j + 1) % 2]
                        ins = pool.tensor_tensor(M(t), AT(t), bc(env.level[:, j + 1, :], 1, HB), ALU.mult)
                    did("pool", ins, item)
                elif kind == "scan":
                    ch = rest[0]
                    if (t, ch) == (0, 0):
                        pool.wait_ge(cleared, 1)
                        pool.wait_ge(actv, 8)
                    elif ch == 0:
                        wait(pool, "dve", "scan", t - 1, 1, "write")
                    else:
                        wait(pool, "dve", "scan", t, 0, "write")
                    did("pool", pool.tensor_tensor(Sd[:, :, :], S[:, :, :], bc(gl[:, 2 * t + ch, :], 2, P), ALU.mult), item)
                else:
                    h = rest[0]
                    wait(pool, "pe", "heads", t, h, "read")
                    did("pool", pool.tensor_tensor(sh[h % 2], sh[h % 2], bc(gl[:, 2 * NPT:, h], 2, P), ALU.mult), item)

        @block.scalar
        def _(act):
            for k in range(2 * HB):
                act.wait_ge(c_in, 16 * (1 + k // HB))
                if k >= SQR:
                    act.wait_ge(ss_made, k - SQR + 1)
                act.activation(sq[k % SQR], C[:, k, :], ACT.Square).then_inc(sq_made, 1)
            act.wait_ge(ss_made, 2 * HB)
            act.activation(rs[:, :, :], Z6[:, 0, 0:NT * 2 * HB].rearrange("p (t k) -> p t k", k=2 * HB), ACT.Sqrt,
                           bias=env.eps[:, 0:1]).then_inc(ss_read, 1)
            act.activation(beta, env.ab[:, :, HB:], ACT.Sigmoid).then_inc(actv, 1)
            act.activation(nea[:, :], env.alog[:, :], ACT.Exp).then_inc(actv, 1)
            act.wait_ge(vecs, 3)
            act.activation(sp_e, sp_e, ACT.Exp, scale=-1.0).then_inc(actv, 1)
            act.wait_ge(actv, 3)
            act.activation(sp_e, sp_e, ACT.Ln, bias=1.0).then_inc(actv, 1)
            act.wait_ge(sums, 1)
            act.activation(gc, Z7[:, 0, 0:NT * HB].rearrange("p (t h) -> p t h", h=HB), ACT.Copy).then_inc(actv, 1)
            act.activation(eg, Z7[:, 0, 0:NT * HB].rearrange("p (t h) -> p t h", h=HB), ACT.Exp).then_inc(actv, 1)
            act.activation(er, Z7[:, 1, 0:NT * HB].rearrange("p (t h) -> p t h", h=HB), ACT.Exp).then_inc(actv, 1)
            act.activation(gl[:, :, :], Z7[:, 2, 0:(2 * NPT + NB) * HB].rearrange("p (t h) -> p t h", h=HB), ACT.Exp).then_inc(actv, 1)
            act.wait_ge(actv, 8)
            for item in SCHED:
                kind, t, *rest = item
                if not has("act", item):
                    continue
                if kind == "prep":
                    s, b = rest[0], B[t % 2]
                    wait(act, "pe", *item)
                    if s == "turn":
                        if t >= 4:
                            wait(act, "pe", "scan", t - 4, 1, "write")
                            wait(act, "dve", "scan", t - 4, 1, "read")
                        for h in range(HB):
                            ins = act.activation(U(t)[:, h, :], b[2][:, h, :], ACT.Copy, scale=beta[:, t, h:h + 1])
                    elif s == "norm_turn":
                        for i, dst in enumerate((knT, kbT, qnT)):
                            ins = act.activation(dst(t), b[i][:, :, :], ACT.Copy)
                    elif s == "decay":
                        act.activation(qdT(t), b[0][:, :, :], ACT.Copy)
                        wait(act, "dve", *item)
                        ins = act.activation(QK(t), QK(t), ACT.Exp)
                    elif s == "solve":
                        act.activation(WT(t), b[0][:, :, :], ACT.Copy)
                        ins = act.activation(U(t), b[1][:, :, :], ACT.Copy)
                    else:
                        ins = act.activation(X(t), b[0][:, :, :], ACT.Copy)
                    did("act", ins, item)
                else:
                    wait(act, "pe", *item)
                    act.activation(C[:, 0:HB, t * P:(t + 1) * P], Z7[:, :, :], ACT.Copy)
                    if t:
                        act.wait_ge(dstep, t)
                    did("act", act.activation(sqo[:, :, :], Z7[:, :, :], ACT.Square), item)
            act.wait_ge(dstep, NT)
            act.activation(rso[:, :, :], sso[:, :, :], ACT.Sqrt, bias=env.eps[:, 0:1], scale=1.0 / DK).then_inc(o_root, 1)
            act.wait_ge(z_in, 16)
            act.activation(C[:, 8:12, :], C[:, 8:12, :], ACT.Silu).then_inc(z_ready, 1)

        @block.vector
        def _(dve):
            nv = 0

            def step(ins):
                nonlocal nv
                ins.then_inc(vecs, 1)
                nv += 1
                dve.wait_ge(vecs, nv)

            step(dve.tensor_tensor(at, env.ab[:, :, 0:HB], bc(env.dtb[:, :], 1, NT), ALU.add))
            step(dve.tensor_scalar(sp_m, at, 0.0, None, ALU.max))
            step(dve.scalar_tensor_tensor(out=sp_e, in0=sp_m, scalar=2.0, in1=at, op0=ALU.mult,
                                          op1=ALU.subtract))
            dve.wait_ge(actv, 4)
            step(dve.tensor_tensor(sp_m, sp_m, sp_e, ALU.add))
            step(dve.tensor_scalar(sp_m, sp_m, -1.0, None, ALU.mult))
            dve.tensor_tensor(g, sp_m, bc(nea[:, :], 1, NT), ALU.mult).then_inc(gates, 1)
            dve.wait_ge(gates, 1)
            for ch in range(2):
                dve.tensor_scalar(gm[:, ch:2 * NPT:2, :], g[:, 0:NPT, :], env.member[:, ch:ch + 1], None,
                                  ALU.mult).then_inc(gmat, 1)
            dve.tensor_tensor(gm[:, 2 * NPT:, :], bc(g[:, NPT, :], 1, NB), bc(env.member[:, 2:2 + NB], 2, HB),
                              ALU.mult).then_inc(gmat, 1)
            dve.wait_ge(ss_read, 1)
            step(dve.reciprocal(rs[:, :, :], rs[:, :, :]))
            dve.wait_ge(actv, 8)
            step(dve.tensor_scalar(s_qn, rs[:, :, 0:HB], KD ** -0.5, None, ALU.mult))
            step(dve.tensor_copy(s_kn, rs[:, :, HB:]))
            step(dve.tensor_tensor(s_qd, s_qn, eg, ALU.mult))
            step(dve.tensor_tensor(s_kb, s_kn, beta, ALU.mult))
            step(dve.tensor_tensor(s_kbe, s_kb, eg, ALU.mult))
            step(dve.tensor_tensor(s_kd, s_kn, er, ALU.mult))

            for item in SCHED:
                kind, t, *rest = item
                if not has("dve", item):
                    continue
                if kind == "prep":
                    s, b = rest[0], B[t % 2]
                    wait(dve, "pe", *item)
                    if s == "turn":
                        if t >= 4:
                            wait(dve, "pe", "scan", t - 4, 1, "write")
                        for dst, src, col in ((kn, 1, s_kn), (kb, 1, s_kb), (qn, 0, s_qn), (kbe, 1, s_kbe),
                                              (kd, 1, s_kd), (qd, 0, s_qd)):
                            ins = dve.tensor_tensor(dst(t), b[src][:, :, :], bc(col[:, t, :], 2, P), ALU.mult)
                    elif s == "decay":
                        ins = dve.tensor_tensor(QK(t), b[1][:, :, :], bc(gc[:, t, :], 2, P), ALU.subtract)
                    elif s == "pair":
                        wait(dve, "act", "prep", t, "decay")
                        dve.tensor_tensor(AT(t), b[2][:, :, :], QK(t), ALU.mult)
                        ins = dve.tensor_tensor(QK(t), b[0][:, :, :], QK(t), ALU.mult)
                    elif s == "inv0":
                        ins = dve.tensor_tensor(Dm(t), bc(env.ident[:, :], 1, HB), b[1][:, :, :], ALU.subtract)
                    else:
                        if s == "inv1b":
                            wait(dve, "pool", "prep", t, "inv0")
                            wait(dve, "dve", "prep", t, "inv0")
                        else:
                            wait(dve, "dve", "prep", t, f"inv{int(s[3]) - 1}b")
                        ins = dve.tensor_tensor(DT(t), DT(t), b[2][:, :, :], ALU.subtract)
                        if int(s[3]) + 1 < levels(t):
                            ins = dve.tensor_tensor(Dm(t), Dm(t), b[1][:, :, :], ALU.subtract)
                    did("dve", ins, item)
                elif kind == "scan":
                    ch, x = rest
                    wait(dve, "pe", *item)
                    if x == "read":
                        wait(dve, "act", "prep", t, "solve")
                        r = slice(L * ch, L * ch + L)
                        ins = dve.tensor_tensor(vn[r, :, :], U(t)[r, :, :], Z6[r, :, :], ALU.subtract)
                    else:
                        wait(dve, "pool", "scan", t, ch, "read")
                        ins = dve.tensor_tensor(S[:, :, :], Sd[:, :, :], Z6[:, :, :], ALU.add)
                    did("dve", ins, item)
                    if ch == 1 and x == "write":
                        squares(dve, item)
                else:
                    h, x = rest
                    if x == "read":
                        if h == 0:
                            wait(dve, "act", "prep", t, "solve")
                            wait(dve, "pe", "prep", t, "solve")
                            dve.memset(wm, 0.0).then_inc(cleared, 1)
                            dve.memset(qm, 0.0).then_inc(cleared, 1)
                            dve.wait_ge(cleared, 3)
                        else:
                            wait(dve, "pe", "heads", t, h - 1, "read")
                        for m, src in ((wm, WT), (qm, qdT)):
                            ins = dve.tensor_copy(m.rearrange("p (b v) -> p b v", v=P + TS)[:, :, 0:TS],
                                                  src(t)[:, h, :].rearrange("p (b v) -> p b v", v=TS))
                    elif x == "mask":
                        wait(dve, "pe", "heads", t, h, "read")
                        step(dve.tensor_tensor(vn[:, h, :], U(t)[:, h, :], Z6[:, 0, :], ALU.subtract))
                        if h:
                            wait(dve, "pe", "heads", t, h - 1, "write")
                        ins = dve.tensor_tensor(vm, bc(vn[:, h, :], 1, NB), bc(env.member[:, 2:2 + NB], 2, P), ALU.mult)
                    else:
                        wait(dve, "pe", "heads", t, h, "write")
                        wait(dve, "pool", "heads", t, h, "mask")
                        for i in range(2):
                            o = sh[h % 2][:, 4 * i:4 * i + 4, :]
                            ins = dve.tensor_tensor(o, o, B[0][i][:, :, :], ALU.add)
                    did("dve", ins, item)
                    if h == HB - 1 and x == "write":
                        squares(dve, item)
            dve.wait_ge(dstep, NT)
            dve.wait_ge(o_root, 1)
            step(dve.reciprocal(rso[:, :, :], rso[:, :, :]))

            def scale_o(t):
                o = C[:, 0:HB, t * P:(t + 1) * P]
                dve.tensor_tensor(o, o, bc(rso[:, t, :], 2, P), ALU.mult).then_inc(o_norm, 1)

            dve.wait_ge(z_ready, 1)
            scale_o(0)
            for t in range(NT):
                if t + 1 < NT:
                    scale_o(t + 1)
                dve.wait_ge(o_turned, t + 1)
                tk = slice(t * P, (t + 1) * P)
                dve.scalar_tensor_tensor(out=env.ob[:, :, tk], in0=B[t % 2][0][:, :, :], scalar=env.dgain[:, 0:1],
                                         in1=C[:, 8:12, tk], op0=ALU.mult, op1=ALU.mult).then_inc(o_out, 1)

        @block.tensor
        def _(pe):
            for k in range(2 * HB):
                pe.wait_ge(sq_made, k + 1)
                for t in range(NT):
                    j = t * 2 * HB + k
                    last = pe.matmul(Z6[:, 0, j:j + 1], sq[k % SQR][:, t * P:(t + 1) * P], env.ones[:, 0:1],
                                     start=True, stop=True)
                last.then_inc(ss_made, 1)
            pe.wait_ge(gmat, 3)
            for i, m in enumerate((env.cum, env.after)):
                pe.matmul(Z7[:, i, 0:NPT * HB], m[:, 0, :], g[:, 0:NPT, :], start=True, stop=True)
                pe.matmul(Z7[:, i, NPT * HB:NT * HB], m[:, 1, :], g[:, NPT, :], start=True, stop=True)
            pe.matmul(Z7[:, 2, 0:(2 * NPT + NB) * HB], env.ones[:, :], gm[:, :, :], start=True, stop=True).then_inc(sums, 1)
            pe.wait_ge(c_in, 48)
            pe.wait_ge(actv, 8)
            for item in SCHED:
                kind, t, *rest = item
                if not has("pe", item):
                    continue
                if kind == "prep":
                    s, b = rest[0], B[t % 2]

                    def heads(bank, lhs, rhs, turn=False):
                        for h in range(HB):
                            a, r = lhs(t)[:, h, :], (env.ident[:, :] if rhs is None else rhs(t)[:, h, :])
                            if turn:
                                last = pe.transpose(bank[:, h, :], a, env.ident[:, :])
                            else:
                                last = pe.matmul(bank[:, h, :], a, r, start=True, stop=True)
                        return last

                    def sofar(eng, s_):
                        wait(pe, eng, "prep", t, s_)

                    if s == "turn":
                        if t >= 2:
                            wait(pe, "act", "prep", t - 2, "solve")
                            wait(pe, "dve", "prep", t - 2, f"inv{levels(t - 2) - 1}b")
                        for i in range(3):
                            ins = heads(b[i], lambda t_, i=i: C[:, 4 * i:4 * i + 4, t * P:(t + 1) * P], None, True)
                    elif s == "norm_turn":
                        sofar("dve", "turn")
                        heads(b[0], kn, None, True)
                        heads(b[1], kb, None, True)
                        sofar("act", "turn")
                        ins = heads(b[2], qn, None, True)
                    elif s == "decay":
                        sofar("act", "norm_turn")
                        heads(b[0], qd, None, True)
                        sofar("pool", "norm_turn")
                        pe.matmul(b[1][:, :, :], env.ones[:, :], AT(t), start=True, stop=False)
                        ins = pe.matmul(b[1][:, :, :], env.ident[:, :], bc(env.shut[:, kb_of(t), :], 1, HB),
                                        start=False, stop=True)
                    elif s == "pair":
                        heads(b[2], knT, kbT)
                        sofar("act", "decay")
                        ins = heads(b[0], knT, qnT)
                    elif s == "inv0":
                        sofar("pool", "pair")
                        ins = heads(b[1], M0, None)
                    elif s.endswith("a"):
                        j = int(s[3])
                        if j == 1:
                            sofar("pool", "inv0")
                            sofar("dve", "inv0")
                        else:
                            sofar("pool", f"inv{j - 1}a")
                            sofar("dve", f"inv{j - 1}b")
                        ins = heads(b[0], (M0, M1)[j % 2], Dm)
                    elif s.endswith("b"):
                        sofar("act", s[:-1] + "a")
                        ins = heads(b[2], X, DT)
                        if int(s[3]) + 1 < levels(t):
                            ins = heads(b[1], DT, X)
                    else:
                        sofar("dve", f"inv{levels(t) - 1}b")
                        heads(b[0], kbe, DT)
                        ins = heads(b[1], DT, U)
                    did("pe", ins, item)
                elif kind == "scan":
                    ch, x = rest
                    r = slice(L * ch, L * ch + L)
                    if x == "read":
                        wait(pe, "act", "prep", t, "solve")
                        if (t, ch) == (0, 0):
                            pe.wait_ge(cleared, 1)
                        elif ch == 0:
                            wait(pe, "dve", "scan", t - 1, 1, "write")
                            wait(pe, "act", "scan", t - 1, 1, "write")
                        else:
                            wait(pe, "dve", "scan", t, 0, "write")
                        for h in range(HB):
                            last = pe.matmul(Z6[r, h, :], WT(t)[:, h, r], S[:, h, :], start=True, stop=True)
                        for h in range(HB):
                            last = pe.matmul(Z7[r, h, :], qdT(t)[:, h, r], S[:, h, :], start=h == 0, stop=False,
                                             skip_group_check=True)
                        did("pe", last, item)
                    else:
                        wait(pe, "dve", "scan", t, ch, "read")
                        for h in range(HB):
                            last = pe.matmul(Z6[:, h, :], kd(t)[r, h, :], vn[r, h, :], start=True, stop=True)
                        if ch == 1:
                            for h in range(HB):
                                last = pe.matmul(Z7[:, h, :], QK(t)[:, h, :], vn[:, h, :], start=False,
                                                 stop=h == HB - 1, skip_group_check=True)
                        did("pe", last, item)
                else:
                    h, x = rest
                    if x == "read":
                        wait(pe, "dve", *item)
                        pe.wait_ge(st_l[h % 2], 16 * (h // 2 + 1))
                        if h == 0:
                            wait(pe, "act", "scan", NPT - 1, 1, "write")
                            wait(pe, "dve", "scan", NPT - 1, 1, "write")
                        else:
                            wait(pe, "dve", "heads", t, h - 1, "mask")
                        for bank, m, k in ((Z6, wm, 0), (Z7, qm, h)):
                            for b_ in range(NB):
                                last = pe.matmul(bank[:, k, :], m[:, b_ * P:(b_ + 1) * P], sh[h % 2][:, b_, :],
                                                 start=b_ == 0, stop=False if k or m is qm else b_ == NB - 1,
                                                 skip_group_check=True)
                        did("pe", last, item)
                    else:
                        wait(pe, "dve", "heads", t, h, "mask")
                        if h:
                            wait(pe, "dve", "heads", t, h - 1, "write")
                        pe.matmul(Z7[:, h, :], QK(t)[:, h, :], vn[:, h, :], start=False, stop=True, skip_group_check=True)
                        for i in range(2):
                            last = pe.matmul(B[0][i][:, :, :], kd(t)[:, h, :], vm[:, 4 * i:4 * i + 4, :],
                                             start=True, stop=True)
                        did("pe", last, item)
            for t in range(NT):
                pe.wait_ge(o_norm, t + 1)
                if t == 0:
                    wait(pe, "dve", "heads", NPT, HB - 1, "write")
                if t >= 2:
                    pe.wait_ge(o_out, t - 1)
                for h in range(HB):
                    last = pe.transpose(B[t % 2][0][:, h, :], C[:, h, t * P:(t + 1) * P], env.ident[:, :])
                last.then_inc(o_turned, 1)


def split_activations(env, tag, c, src, ready=None):
    hi, lo_p, lo_d = sems(env, tag, "x_hi_made", "x_lo_pool", "x_lo_dve")

    def act(e):
        for k in range(DC):
            if ready:
                ready(e, k)
            e.activation(env.x_hi[:, k, :], src(k), ACT.Copy).then_inc(hi, 1)

    def low(e, mine, sem):
        for k in mine:
            e.wait_ge(hi, k + 1)
            e.tensor_tensor(env.x_lo[:, k, :], src(k), env.x_hi[:, k, :].bitcast(F32),
                            ALU.subtract).then_inc(sem, 1)

    def wait(e):
        e.wait_ge(lo_p, 2)
        e.wait_ge(lo_d, 6)

    return act, lambda e: low(e, (3, 7), lo_p), lambda e: low(e, (0, 1, 2, 4, 5, 6), lo_d), wait


class TokenStats:

    def __init__(self, env, tag, c, bank, wide, memory=None):
        self.env, self.bank, self.wide = env, bank, wide
        nc = env.nc
        if memory is None:
            self.sq = c.enter_context(nc.sbuf_tensor(f"{tag}_sumsq", [P, T], F32))
            self.col = c.enter_context(nc.sbuf_tensor(f"{tag}_rms", [P, NT], F32))
            self.diag = c.enter_context(nc.sbuf_tensor(f"{tag}_rms_diag", [P, NT, P], F32))
            self.out = c.enter_context(nc.sbuf_tensor(f"{tag}_rstd", [P, T], F32))
        else:
            self.sq, self.col, self.diag, self.out = memory.sq, memory.col, memory.diag, memory.out
        self.signals(tag)

    def signals(self, tag):
        env = self.env
        self.total, self.root, self.inv, self.diag_made, self.spread, self.done = sems(
            env, tag, "sq_total", "sq_root", "rms_inv", "rms_diag", "rms_spread", "rstd_made")

    def pe(self, e, ready):
        ready(e)
        for t in range(NT):
            last = e.matmul(self.bank[:, t:t + 1], self.sq[:, t * P:(t + 1) * P], self.env.ones[:, 0:1],
                            start=True, stop=True)
        last.then_inc(self.total, 1)
        e.wait_ge(self.diag_made, 1)
        for g in range(NTG):
            e.matmul(self.wide[g][:, 0:TG], self.env.ones[:, :], self.diag[:, 3 * g:3 * g + 3, :],
                     start=True, stop=True).then_inc(self.spread, 1)

    def act(self, e):
        e.wait_ge(self.total, 1)
        e.activation(self.col[:, :], self.bank[:, 0:NT], ACT.Sqrt, bias=self.env.eps[:, 0:1],
                     scale=1.0 / D).then_inc(self.root, 1)
        for g in range(NTG):
            e.wait_ge(self.spread, g + 1)
            e.activation(self.out[:, g * TG:(g + 1) * TG], self.wide[g][:, 0:TG], ACT.Copy).then_inc(self.done, 1)

    def dve(self, e):
        e.wait_ge(self.root, 1)
        e.reciprocal(self.col[:, :], self.col[:, :]).then_inc(self.inv, 1)
        e.wait_ge(self.inv, 1)
        e.tensor_tensor(self.diag[:, :, :], bc(self.env.ident[:, :], 1, NT), bc(self.col[:, :], 2, P),
                        ALU.mult).then_inc(self.diag_made, 1)

    def wait(self, e):
        e.wait_ge(self.done, NTG)


def stage_merge(env):
    nc, I = env.nc, env.inp
    with ExitStack() as c:
        w = weight_pipe(env, "m", c)
        prod, free, g_free, sig, part, merged = sems(env, "m", "prod", "free", "gates_free", "sigmoids", "gated", "merged")
        g_in = sems(env, "m", "gates_landed0", "gates_landed1")
        gate = [c.enter_context(nc.sbuf_tensor(f"m_gates{i}", [P, 2, T], F32)) for i in range(2)]
        ps = [c.enter_context(nc.psum_tensor(f"m_ps{i}", [P, 512], F32)) for i in range(6)]
        s_act, s_pool, s_dve, s_wait = split_activations(
            env, "m", c, lambda k: (env.oa if k < 4 else env.ob)[:, k % 4, :])
        block = c.enter_context(nc.Block())
        CREDIT = 6
        HALF = DC // 2
        wa = I["w_proj_a"].rearrange("l (c p) n -> p (l c) n", p=P)
        wb = I["w_proj_b"].rearrange("l (c p) n -> p (l c) n", p=P)

        @block.sync
        def _(sp):
            with sp.Fori(0, HALF) as i:
                for s in range(2):
                    m = 2 * i + s
                    sp.wait_ge(w.lo_made, m + 1)
                    for k, src in enumerate((wa, wb)):
                        sp.dma_start(w.raw[s][:, 4 * k:4 * k + 4, :], src[:, :, bass.ds(m * P, P)]
                                     ).then_inc(w.landed[s], 16)
                    sp.wait_ge(g_free, m + 1)
                    row = (NSLAB[0] + m) * P
                    for k in range(2):
                        sp.dma_start(gate[s][:, k, :], env.proj[bass.ds(row + k * D, P), :]).then_inc(g_in[s], 16)

        @block.gpsimd
        def _(pool):
            pool.sem_inc(w.lo_made, WRING)
            s_pool(pool)
            with pool.Fori(0, HALF) as i:
                for s in range(2):
                    split_lo(pool, w, i, s)

        @block.scalar
        def _(act):
            def hi(i, s):
                act.wait_ge(w.landed[s], 32 * i + 32)
                act.wait_ge(w.used, 2 * i + s + 1)
                act.activation(w.hi[s][:, :, :], w.raw[s][:, :, :], ACT.Copy).then_inc(w.hi_made, 1)

            def gates(i, s):
                act.wait_ge(g_in[s], 32 * i + 32)
                act.activation(gate[s][:, :, :], gate[s][:, :, :], ACT.Sigmoid).then_inc(sig, 1)

            s_act(act)
            with act.Fori(0, HALF) as i:
                for s in range(2):
                    hi(i, s)
                    gates(i, s)

        @block.vector
        def _(dve):
            dve.sem_inc(free, CREDIT)
            dve.sem_inc(g_free, 2)
            s_dve(dve)
            with dve.Fori(0, HALF) as i:
                for s in range(2):
                    m = 2 * i + s
                    dve.wait_ge(sig, m + 1)
                    for g in range(NTG):
                        tk = slice(g * TG, (g + 1) * TG)
                        dve.wait_ge(prod, NTG * m + g + 1)
                        for k in range(2):
                            dve.tensor_tensor(gate[s][:, k, tk], gate[s][:, k, tk], ps[2 * g + k][:, 0:TG],
                                              ALU.mult).then_inc(free, 1)
                    dve.wait_ge(free, 6 * m + 6 + CREDIT)
                    dve.tensor_tensor(env.merged[:, bass.ds(m, 1), :], gate[s][:, 0:1, :], gate[s][:, 1:2, :],
                                      ALU.add).then_inc(g_free, 1)

        @block.tensor
        def _(pe):
            pe.sem_inc(w.used, WRING)
            s_wait(pe)
            with pe.Fori(0, HALF) as i:
                for s in range(2):
                    m = 2 * i + s
                    pe.wait_ge(w.lo_made, m + 1 + WRING)
                    for g in range(NTG):
                        pe.wait_ge(free, 6 * m + 2 * g + 2)
                        for k in range(2):
                            last = slab_products(pe, w, s, env.x_hi, env.x_lo, ps[2 * g + k][:, 0:TG],
                                                 range(4 * k, 4 * k + 4), slice(g * TG, (g + 1) * TG))
                        last.then_inc(prod, 1)
                    pe.wait_ge(prod, NTG * m + NTG)
                    pe.sem_inc(w.used, 1)


def stage_out_proj(env):
    nc, I = env.nc, env.inp
    with ExitStack() as c:
        w = weight_pipe(env, "o", c)
        prod, free, sq_made, sq_free, x_turned, x_read_d, x_read_a, summed, added, squared2, sum2, saved, normed = sems(
            env, "o", "prod", "free", "sq_made", "sq_free", "x_turned", "x_read_dve", "x_read_act", "summed",
            "added", "squared2", "sum2", "saved", "normed")
        x_in = sems(env, "o", "x_in0", "x_in1", "x_in2")
        xt = c.enter_context(nc.sbuf_tensor("o_xt", [P, DC, T], F32))
        XR = 2
        x = [c.enter_context(nc.sbuf_tensor(f"o_x{i}", [P, D], F32)) for i in range(XR)]
        sq = [c.enter_context(nc.sbuf_tensor(f"o_sq{i}", [P, T], F32)) for i in range(2)]
        ps = [c.enter_context(nc.psum_tensor(f"o_ps{i}", [P, 512], F32)) for i in range(6)]
        bank = c.enter_context(nc.psum_tensor("o_bank", [P, 512], F32))
        st1 = TokenStats(env, "o1", c, bank, ps[0:3])
        st2 = TokenStats(env, "o2", c, bank, ps[0:3], memory=st1)
        hi2, lo2p, lo2d, normed2 = sems(env, "o", "h_hi_made", "h_lo_pool", "h_lo_dve", "y_normed")
        y = env.merged
        s_act, s_pool, s_dve, s_wait = split_activations(env, "o", c, lambda k: y[:, k, :])
        block = c.enter_context(nc.Block())
        CREDIT = 6
        HALF = DC // 2
        w_out = I["w_out"].rearrange("l (c p) n -> p (l c) n", p=P)
        xp = I["x_prompt"].rearrange("a (t p) d -> (a t) p d", p=P)
        xs = I["x_sample"].rearrange("b t d -> (b t) d")
        NG = 2 * NT

        def group(g):
            return xt[:, 4 * (g % 2):4 * (g % 2) + 4, (g // 2) * P:(g // 2 + 1) * P]

        def x_read(e, g, sem, copy):
            e.wait_ge(x_turned, g + 1)
            copy(group(g), ps[g % 6][:, :].rearrange("p (c m) -> p c m", m=P)).then_inc(sem, 1)

        @block.sync
        def _(sp):
            for s in range(2):
                sp.dma_start(w.raw[s][:, :, :], w_out[:, :, s * P:(s + 1) * P]).then_inc(w.landed[s], 16)
            for t in range(NT):
                if t >= XR:
                    sp.wait_ge(x_turned, 2 * (t - XR) + 2)
                sp.dma_start(x[t % XR][:, :], xp[t] if t < NPT else xs).then_inc(x_in[t % XR], 16)
            with sp.Fori(1, HALF) as i:
                for s in range(2):
                    load_slab(sp, w, i, s, w_out[:, :, bass.ds((2 * i + s) * P, P)])
            for k in range(DC):
                sp.wait_ge(added, k + 1)
                sp.dma_start(env.resid[k * P:(k + 1) * P, :], xt[:, k, :]).then_inc(saved, 16)
            sp.wait_ge(saved, 16 * DC)

        @block.gpsimd
        def _(pool):
            pool.sem_inc(w.lo_made, WRING)
            pool.sem_inc(sq_free, 2)
            pool.memset(st1.sq[:, :], 0.0).then_inc(summed, 1)
            s_pool(pool)
            split_lo(pool, w, 0, 0)
            with pool.Fori(0, HALF - 1) as i:
                for s in range(2):
                    split_lo(pool, w, i + s, 1 - s)
                    pool.wait_ge(summed, 2 * i + s + 1)
                    pool.wait_ge(sq_made, 2 * i + s + 1)
                    pool.tensor_tensor(st1.sq[:, :], st1.sq[:, :], sq[s][:, :], ALU.add).then_inc(summed, 1)
                    pool.wait_ge(summed, 2 * i + s + 2)
                    pool.sem_inc(sq_free, 1)
            split_lo(pool, w, HALF - 1, 1)
            for m in range(DC - 2, DC):
                pool.wait_ge(summed, m + 1)
                pool.wait_ge(sq_made, m + 1)
                pool.tensor_tensor(st1.sq[:, :], st1.sq[:, :], sq[m % 2][:, :], ALU.add).then_inc(summed, 1)
            for k in range(DC):
                pool.wait_ge(squared2, k + 1)
                if k == 0:
                    ins = pool.tensor_copy(st1.sq[:, :], sq[0][:, :])
                else:
                    pool.wait_ge(sum2, k)
                    ins = pool.tensor_tensor(st1.sq[:, :], st1.sq[:, :], sq[k % 2][:, :], ALU.add)
                ins.then_inc(sum2, 1)
            for k in (3, 7):
                pool.wait_ge(hi2, k + 1)
                pool.tensor_tensor(env.x_lo[:, k, :], y[:, k, :], env.x_hi[:, k, :].bitcast(F32),
                                   ALU.subtract).then_inc(lo2p, 1)

        @block.scalar
        def _(act):
            s_act(act)
            split_hi(act, w, 0, 0)
            for g in range(1, NG, 2):
                x_read(act, g, x_read_a, lambda d, s_: act.activation(d, s_, ACT.Copy))

            def square(m, s):
                act.wait_ge(free, 3 * m + 3 + CREDIT)
                act.wait_ge(sq_free, m + 1)
                act.activation(sq[s][:, :].unsqueeze(1), y[:, bass.ds(m, 1), :], ACT.Square).then_inc(sq_made, 1)

            with act.Fori(0, HALF - 1) as i:
                for s in range(2):
                    split_hi(act, w, i + s, 1 - s)
                    square(2 * i + s, s)
            split_hi(act, w, HALF - 1, 1)
            square(DC - 2, 0)
            square(DC - 1, 1)
            st1.act(act)
            for k in range(DC):
                act.wait_ge(added, k + 1)
                if k == 0:
                    act.wait_ge(summed, DC + 1)
                if k >= 2:
                    act.wait_ge(sum2, k - 1)
                act.activation(sq[k % 2][:, :], xt[:, k, :], ACT.Square).then_inc(squared2, 1)
            st2.act(act)
            for k in range(DC):
                act.wait_ge(normed, k + 1)
                act.activation(env.x_hi[:, k, :], y[:, k, :], ACT.Copy).then_inc(hi2, 1)

        @block.vector
        def _(dve):
            dve.sem_inc(free, CREDIT)
            s_dve(dve)
            for g in range(0, NG, 2):
                x_read(dve, g, x_read_d, dve.tensor_copy)
            s_wait(dve)
            with dve.Fori(0, HALF) as i:
                for s in range(2):
                    for g in range(NTG):
                        m = 3 * (2 * i + s) + g
                        dve.wait_ge(prod, m + 1 + CREDIT)
                        dve.tensor_copy(y[:, bass.ds(2 * i + s, 1), g * TG:(g + 1) * TG],
                                        ps[3 * s + g][:, 0:TG].unsqueeze(1)).then_inc(free, 1)
            st1.dve(dve)
            st1.wait(dve)
            n = 0
            for k in range(DC):
                dve.scalar_tensor_tensor(out=y[:, k, :], in0=y[:, k, :], scalar=env.gains[:, 1, k:k + 1],
                                         in1=st1.out[:, :], op0=ALU.mult, op1=ALU.mult).then_inc(normed2, 1)
                if k:
                    dve.wait_ge(normed2, k)
                    if k == 1:
                        dve.wait_ge(x_read_a, NT)
                    dve.tensor_tensor(xt[:, k - 1, :], xt[:, k - 1, :], y[:, k - 1, :], ALU.add).then_inc(added, 1)
            dve.wait_ge(normed2, DC)
            dve.tensor_tensor(xt[:, DC - 1, :], xt[:, DC - 1, :], y[:, DC - 1, :], ALU.add).then_inc(added, 1)
            st2.dve(dve)
            st2.wait(dve)
            dve.wait_ge(added, DC)
            for k in range(DC):
                dve.scalar_tensor_tensor(out=y[:, k, :], in0=xt[:, k, :], scalar=env.gains[:, 2, k:k + 1],
                                         in1=st2.out[:, :], op0=ALU.mult, op1=ALU.mult).then_inc(normed, 1)
            for k in (0, 1, 2, 4, 5, 6):
                dve.wait_ge(hi2, k + 1)
                dve.tensor_tensor(env.x_lo[:, k, :], y[:, k, :], env.x_hi[:, k, :].bitcast(F32),
                                  ALU.subtract).then_inc(lo2d, 1)

        @block.tensor
        def _(pe):
            pe.sem_inc(prod, CREDIT)
            pe.sem_inc(w.used, WRING)
            for g in range(NG):
                t = g // 2
                pe.wait_ge(x_in[t % XR], 16 * (t // XR + 1))
                if g >= 6:
                    n = g - 6
                    pe.wait_ge(x_read_a if n % 2 else x_read_d, n // 2 + 1)
                for k in range(4):
                    cc = 4 * (g % 2) + k
                    last = pe.transpose(ps[g % 6][:, k * P:(k + 1) * P], x[t % XR][:, cc * P:(cc + 1) * P],
                                        env.ident[:, :])
                last.then_inc(x_turned, 1)
            pe.wait_ge(x_read_a, NT)
            pe.wait_ge(x_read_d, NT)
            s_wait(pe)
            with pe.Fori(0, HALF) as i:
                for s in range(2):
                    pe.wait_ge(w.lo_made, 2 * i + s + 1 + WRING)
                    for g in range(NTG):
                        m = 3 * (2 * i + s) + g
                        pe.wait_ge(free, m + 1)
                        last = slab_products(pe, w, s, env.x_hi, env.x_lo, ps[3 * s + g][:, 0:TG],
                                             range(DC), slice(g * TG, (g + 1) * TG))
                        last.then_inc(prod, 1)
                    pe.wait_ge(prod, 3 * (2 * i + s) + 3 + CREDIT)
                    pe.sem_inc(w.used, 1)
            pe.wait_ge(free, 3 * DC + CREDIT)
            st1.pe(pe, lambda e: e.wait_ge(summed, DC + 1))
            st2.pe(pe, lambda e: e.wait_ge(sum2, DC))


def stage_mlp(env):
    nc, I = env.nc, env.inp
    NP_ = FF // (2 * P)
    with ExitStack() as c:
        def sb(name, shape, dt=F32):
            return c.enter_context(nc.sbuf_tensor("f_" + name, shape, dt))

        raw = [sb(f"w_raw{i}", [P, DC, P]) for i in range(2)]
        w_hi = [sb(f"w_hi{i}", [P, DC, P], F32R) for i in range(4)]
        w_lo = [sb(f"w_lo{i}", [P, DC, P], F32R) for i in range(4)]
        f_hi = [[sb(f"f_hi{i}{a}", [P, T], F32R) for a in range(2)] for i in range(2)]
        f_lo = [[sb(f"f_lo{i}{a}", [P, T], F32R) for a in range(2)] for i in range(2)]
        r = [sb(f"relu{i}", [P, TG]) for i in range(2)]
        f = [sb(f"f{i}", [P, TG]) for i in range(2)]
        acc = env.merged
        up = [c.enter_context(nc.psum_tensor(f"f_up{i}", [P, 512], F32)) for i in range(3)]
        down = [c.enter_context(nc.psum_tensor(f"f_down{i}", [P, 512], F32)) for i in range(4)]
        landed = sems(env, "f", "w_landed0", "w_landed1")
        hi_made, lo_made, used = sems(env, "f", "w_hi_made", "w_lo_made", "w_used")
        up_made, up_read, squared, f_hi_made, f_lo_made = sems(
            env, "f", "up_made", "up_read", "squared", "f_hi_made", "f_lo_made")
        down_made, added, acc_clear = sems(env, "f", "down_made", "added", "acc_clear")
        block = c.enter_context(nc.Block())
        CU, CD = 3, 4
        w_up = I["w_up"].rearrange("l (c p) n -> p (l c) n", p=P)
        w_down = I["w_down"].rearrange("l (k p) n -> (l k) p n", p=P)
        N_D = DC * NTG


        @block.sync
        def _(sp):
            def load(n, a, src):
                sp.wait_ge(lo_made, n + 1)
                sp.dma_start(raw[a][:, :, :] if src[1] == "up" else raw[a][:, :, :].rearrange("p c n -> p (c n)"),
                             src[0]).then_inc(landed[a], 16)

            for a in range(2):
                load(a, a, (w_up[:, :, a * P:(a + 1) * P], "up"))
            with sp.Fori(0, NP_ - 1) as j:
                for a in range(2):
                    load(j * 4 + 2 + a, a, (w_up[:, :, bass.ds(j * 2 * P + (2 + a) * P, P)], "up"))
                for a in range(2):
                    load(j * 4 + 4 + a, a, (w_down[bass.ds(j * 2 + a, 1)].rearrange("k p n -> p (k n)"), "down"))
            for a in range(2):
                load(4 * NP_ - 2 + a, a, (w_down[2 * NP_ - 2 + a], "down"))

        def cycle(eng, split, hidden, j, par, last=False):
            split(j * 4 + 3, j * 2 + 1, 1, 1)
            hidden(j + 1, 1 - par, 0)
            split(j * 4 + 4, j * 2 + 2, 0, 2)
            split(j * 4 + 5, j * 2 + 2, 1, 3)
            hidden(j + 1, 1 - par, 1)
            split(j * 4 + 6, j * 2 + 3, 0, 2 if last else 0, last)

        def program(eng, split, hidden):
            split(0, 0, 0, 0)
            split(1, 0, 1, 1)
            for a in range(2):
                hidden(0, 0, a)
            split(2, 1, 0, 0, True)
            split(3, 1, 1, 1, True)
            hidden(1, 1, 0)
            split(4, 2, 0, 2)
            split(5, 2, 1, 3)
            hidden(1, 1, 1)
            split(6, 3, 0, 0)
            cycle(eng, split, hidden, 1, 1)
            with eng.Fori(1, (NP_ - 2) // 2) as i:
                for par in range(2):
                    cycle(eng, split, hidden, i * 2 + par, par)
            cycle(eng, split, hidden, NP_ - 2, 0, last=True)
            split(4 * NP_ - 1, 2 * NP_ - 1, 1, 3, True)

        @block.scalar
        def _(act):
            def split(n, half, a, slot, near=False):
                act.wait_ge(landed[a], half * 16 + 16)
                act.wait_ge(used, n + (3 if near else 1))
                act.activation(w_hi[slot][:, :, :], raw[a][:, :, :], ACT.Copy).then_inc(hi_made, 1)

            def hidden(j, par, a):
                for g in range(NTG):
                    e, s = j * 6 + 3 * a + g, (3 * a + g) % 2
                    act.wait_ge(up_made, e + 1)
                    act.activation(r[s][:, :], up[g][:, 0:TG], ACT.Relu).then_inc(up_read, 1)
                    act.wait_ge(up_read, e + 1 + CU)
                    act.wait_ge(f_lo_made, e + 1)
                    act.activation(f[s][:, :], r[s][:, :], ACT.Square).then_inc(squared, 1)
                    act.wait_ge(squared, e + 1)
                    act.activation(f_hi[par][a][:, g * TG:(g + 1) * TG], f[s][:, :], ACT.Copy).then_inc(f_hi_made, 1)

            act.sem_inc(up_read, CU)
            program(act, split, hidden)

        @block.gpsimd
        def _(pool):
            def split(n, half, a, slot, near=False):
                pool.wait_ge(hi_made, n + 1)
                pool.tensor_tensor(w_lo[slot][:, :, :], raw[a][:, :, :], w_hi[slot][:, :, :].bitcast(F32),
                                   ALU.subtract).then_inc(lo_made, 1)

            def hidden(j, par, a):
                for g in range(NTG):
                    e, s = j * 6 + 3 * a + g, (3 * a + g) % 2
                    tk = slice(g * TG, (g + 1) * TG)
                    pool.wait_ge(f_hi_made, e + 1)
                    pool.tensor_tensor(f_lo[par][a][:, tk], f[s][:, :], f_hi[par][a][:, tk].bitcast(F32),
                                       ALU.subtract).then_inc(f_lo_made, 1)

            pool.sem_inc(lo_made, 2)
            pool.sem_inc(f_lo_made, 2)
            program(pool, split, hidden)

        @block.vector
        def _(dve):
            dve.sem_inc(added, CD)
            dve.memset(acc[:, :, :], 0.0).then_inc(acc_clear, 1)
            dve.wait_ge(acc_clear, 1)
            with dve.Fori(0, NP_) as j:
                dve.wait_ge(added, j * N_D + CD)
                for d in range(N_D):
                    o, g = divmod(d, NTG)
                    a = acc[:, o, g * TG:(g + 1) * TG]
                    dve.wait_ge(down_made, j * N_D + d + 1)
                    dve.tensor_tensor(a, a, down[d % 4][:, 0:TG], ALU.add).then_inc(added, 1)

        @block.tensor
        def _(pe):
            pe.sem_inc(used, 4)

            def make_up(j):
                for a in range(2):
                    n = a if isinstance(j, int) and j == 0 else j * 4 - 2 + a
                    pe.wait_ge(lo_made, n + 1 + 2)
                    for g in range(NTG):
                        tk = slice(g * TG, (g + 1) * TG)
                        pe.wait_ge(up_read, j * 6 + 3 * a + g + 1)
                        k = 0
                        for cc in range(DC):
                            for p_, q_ in ((w_lo, env.x_hi), (w_hi, env.x_lo), (w_hi, env.x_hi)):
                                last = pe.matmul(up[g][:, 0:TG], p_[a][:, cc, :], q_[:, cc, tk],
                                                 start=k == 0, stop=k == 3 * DC - 1)
                                k += 1
                        last.then_inc(up_made, 1)
                    pe.wait_ge(up_made, j * 6 + 3 * a + 3)
                    pe.sem_inc(used, 1)

            def make_down(j, par, n):
                pe.wait_ge(lo_made, n + 2 + 2)
                pe.wait_ge(f_lo_made, j * 6 + 6 + 2)
                for d in range(N_D):
                    o, g = divmod(d, NTG)
                    tk = slice(g * TG, (g + 1) * TG)
                    pe.wait_ge(added, j * N_D + d + 1)
                    k = 0
                    for a in range(2):
                        for p_, q_ in ((w_lo, f_hi), (w_hi, f_lo), (w_hi, f_hi)):
                            last = pe.matmul(down[d % 4][:, 0:TG], p_[2 + a][:, o, :], q_[par][a][:, tk],
                                             start=k == 0, stop=k == 5)
                            k += 1
                    last.then_inc(down_made, 1)
                pe.wait_ge(down_made, j * N_D + N_D)
                pe.sem_inc(used, 2)

            make_up(0)
            make_up(1)
            make_down(0, 0, 4)
            make_up(2)
            make_down(1, 1, 8)
            with pe.Fori(1, (NP_ - 2) // 2) as i:
                for par in range(2):
                    j = i * 2 + par
                    make_up(j + 1)
                    make_down(j, par, j * 4 + 4)
            make_up(NP_ - 1)
            make_down(NP_ - 2, 0, 4 * NP_ - 4)
            make_down(NP_ - 1, 1, 4 * NP_ - 2)


def stage_norm_out(env):
    nc, O_ = env.nc, env.out
    with ExitStack() as c:
        acc = env.merged
        res = c.enter_context(nc.sbuf_tensor("e_resid", [P, DC, T], F32))
        sq = [c.enter_context(nc.sbuf_tensor(f"e_sq{i}", [P, T], F32)) for i in range(3)]
        y = [c.enter_context(nc.sbuf_tensor(f"e_y{i}", [P, D], F32)) for i in range(3)]
        ps = [c.enter_context(nc.psum_tensor(f"e_ps{i}", [P, 512], F32)) for i in range(4)]
        wide = [c.enter_context(nc.psum_tensor(f"e_wide{i}", [P, 512], F32)) for i in range(NTG)]
        bank = c.enter_context(nc.psum_tensor("e_bank", [P, 512], F32))
        st = TokenStats(env, "e1", c, bank, wide)
        res_in, squared, summed, scaled, added, turned, moved_a, moved_d, sent0, sent1, sent2 = sems(
            env, "e", "res_in", "squared", "summed", "scaled", "added", "turned", "moved_act", "moved_dve",
            "sent0", "sent1", "sent2")
        sent = (sent0, sent1, sent2)
        block = c.enter_context(nc.Block())

        @block.sync
        def _(sp):
            sp.dma_start(res[:, :, :], env.resid.rearrange("(c p) t -> p c t", p=P)).then_inc(res_in, 16)
            yp = O_["y_prompt"].rearrange("a (t p) d -> (a t) p d", p=P)
            ys = O_["y_sample"].rearrange("b t d -> (b t) d")
            for t in range(NT):
                sp.wait_ge(moved_a, t + 1)
                sp.wait_ge(moved_d, t + 1)
                sp.dma_start(yp[t] if t < NPT else ys, y[t % 3][:, :]).then_inc(sent[t % 3], 16)
            for i in range(3):
                sp.wait_ge(sent[i], 16 * (NT // 3))

        def move(e, t, half, copy, sem):
            if t >= 3:
                e.wait_ge(sent[t % 3], 16 * (t // 3))
            n = 2 * t + half
            e.wait_ge(turned, n + 1)
            copy(y[t % 3][:, half * 512:(half + 1) * 512], ps[n % 4][:, :]).then_inc(sem, 1)

        @block.gpsimd
        def _(pool):
            for k in range(DC):
                pool.wait_ge(squared, k + 1)
                if k == 0:
                    ins = pool.tensor_copy(st.sq[:, :], sq[0][:, :])
                else:
                    pool.wait_ge(summed, k)
                    ins = pool.tensor_tensor(st.sq[:, :], st.sq[:, :], sq[k % 3][:, :], ALU.add)
                ins.then_inc(summed, 1)

        @block.scalar
        def _(act):
            for k in range(DC):
                if k >= 3:
                    act.wait_ge(summed, k - 2)
                act.activation(sq[k % 3][:, :], acc[:, k, :], ACT.Square).then_inc(squared, 1)
            st.act(act)
            for t in range(NT):
                move(act, t, 0, lambda d, s: act.activation(d, s, ACT.Copy), moved_a)

        @block.vector
        def _(dve):
            st.dve(dve)
            st.wait(dve)
            dve.wait_ge(res_in, 16)
            for g in range(NTG):
                tk = slice(g * TG, (g + 1) * TG)
                for k in range(DC):
                    dve.scalar_tensor_tensor(out=acc[:, k, tk], in0=acc[:, k, tk], scalar=env.gains[:, 3, k:k + 1],
                                             in1=st.out[:, tk], op0=ALU.mult, op1=ALU.mult).then_inc(scaled, 1)
                dve.wait_ge(scaled, DC * (g + 1))
                for k in range(DC):
                    ins = dve.tensor_tensor(acc[:, k, tk], acc[:, k, tk], res[:, k, tk], ALU.add)
                ins.then_inc(added, 1)
                if g:
                    for t in range(3 * g - 3, 3 * g):
                        move(dve, t, 1, dve.tensor_copy, moved_d)
            for t in range(NT - 3, NT):
                move(dve, t, 1, dve.tensor_copy, moved_d)

        @block.tensor
        def _(pe):
            st.pe(pe, lambda e: e.wait_ge(summed, DC))
            for t in range(NT):
                pe.wait_ge(added, t // 3 + 1)
                for half in range(2):
                    n = 2 * t + half
                    if t >= 2:
                        pe.wait_ge(moved_d if half else moved_a, t - 1)
                    for i in range(4):
                        last = pe.transpose(ps[n % 4][:, i * P:(i + 1) * P], acc[:, 4 * half + i, t * P:(t + 1) * P],
                                            env.ident[:, :])
                    last.then_inc(turned, 1)


def build(nc, inp, out):
    with ExitStack() as ctx:
        env = Env()
        env.nc, env.inp, env.out, env.sems = nc, inp, out, []

        def sb(name, shape, dt=F32, c=ctx):
            return c.enter_context(nc.sbuf_tensor(name, shape, dt))

        env.ident, env.ones = sb("ident", [P, P]), sb("ones", [P, P])
        env.eps = sb("eps", [P, 1])
        env.gains = sb("gains", [P, 4, DC])
        env.proj = nc.dram_tensor("proj", [sum(NSLAB) * P, T], F32).ap()
        env.resid = nc.dram_tensor("resid", [D, T], F32).ap()
        with ExitStack() as branches:
            env.oa = branches.enter_context(nc.sbuf_tensor("oa", [P, 4, T], F32, side="right"))
            with ExitStack() as mix:
                env.flip = sb("flip", [P, P], c=mix)
                env.cum, env.after, env.shut = (sb(n, [P, 2, P], c=mix) for n in ("cum", "after", "shut"))
                env.level = sb("level", [P, len(LEVELS), P], c=mix)
                env.member = sb("member", [P, 2 + NB], c=mix)
                env.convw = sb("convw", [P, CW, CC], c=mix)
                env.dgain = sb("dgain", [P, 1], c=mix)
                env.alog, env.dtb = sb("alog", [P, HB], c=mix), sb("dtb", [P, HB], c=mix)
                env.state_t = sb("state_t", [P, CC, NB * (CW - 1)], c=mix)
                env.conv_tail = sb("conv_tail", [P, CC, (NB + 1) * (CW - 1)], c=mix)
                env.ab = sb("ab", [P, NT, 2 * HB], c=mix)
                with ExitStack() as xc:
                    env.x_hi, env.x_lo = sb("x_hi", [P, DC, T], F32R, xc), sb("x_lo", [P, DC, T], F32R, xc)
                    stage_norm_in(env)
                    stage_in_proj(env)
                stage_attention(env)
                env.ob = branches.enter_context(nc.sbuf_tensor("ob", [P, 4, T], F32, side="right"))
                stage_delta(env)
            clear_sems(env)
            env.merged = sb("merged", [P, DC, T])
            inputs = ctx.enter_context(ExitStack())
            env.x_hi, env.x_lo = (sb(n, [P, DC, T], F32R, inputs) for n in ("h_hi", "h_lo"))
            stage_merge(env)
        stage_out_proj(env)
        stage_mlp(env)
        inputs.close()
        stage_norm_out(env)


_INS = ['x_prompt', 'x_sample', 'cache_attn_k', 'cache_attn_v', 'state_conv', 'state_delta', 'norm_mix_pre', 'w_in',
        'rel_bias', 'conv_w', 'a_log', 'dt_bias', 'delta_norm_w', 'w_proj_a', 'w_proj_b', 'w_out', 'norm_mix_post',
        'norm_mlp_pre', 'w_up', 'w_down', 'norm_mlp_post']
_OUTS = {'y_prompt': (1, TP, D), 'y_sample': (NB, TS, D),
         'prompt_k': (1, 1, REACH, AH, AD), 'prompt_v': (1, 1, REACH, AH, AD),
         'prompt_conv': (1, 1, CW - 1, CONV), 'prompt_delta': (1, 1, HB, DK, DK),
         'sample_k': (1, NB, TS, AH, AD), 'sample_v': (1, NB, TS, AH, AD),
         'sample_conv': (1, NB, CW - 1, CONV), 'sample_delta': (1, NB, HB, DK, DK)}


def kernel(**inputs):
    import numpy as _np
    import concourse.bacc as _bacc
    from concourse import mybir as _mybir
    from concourse.bass_utils import run_bass_kernel_spmd as _run

    nc = _bacc.Bacc("TRN2", target_bir_lowering=False, num_devices=1)
    arrays, inp, out = {}, {}, {}
    for name in _INS:
        a = _np.ascontiguousarray(inputs[name])
        arrays[f"in_{name}"] = a
        inp[name] = nc.dram_tensor(f"in_{name}", a.shape, _mybir.dt.from_np(a.dtype), kind="ExternalInput").ap()
    for name, shape in _OUTS.items():
        out[name] = nc.dram_tensor(f"out_{name}", shape, _mybir.dt.float32, kind="ExternalOutput").ap()
    build(nc, inp, out)
    r = _run(nc, [arrays], core_ids=[0])
    return tuple(r.results[0][f"out_{name}"] for name in _OUTS)
```

```python
from contextlib import ExitStack

import concourse.bass as bass
from concourse import mybir

ALU = mybir.AluOpType
ACT = mybir.ActivationFunctionType
AX = mybir.AxisListType
F32 = mybir.dt.float32
F32R = mybir.dt.float32r

P = 128
D = 1024
DC = D // P
TP = 1024
NB, TS = 8, 16
T = TP + NB * TS
NT = T // P
NPT = TP // P
TG, NTG = 384, T // 384
AH, AD = 8, 64
AW = AH * AD
REACH = 512
NR = 128
HB, DK = 4, 128
CW = 4
CONV = 3 * HB * DK
CC = CONV // P
FF = 4 * D
EPS = 1e-6
NEG = -1.0e30
COL_Z = 3 * AW + CONV
COL_AB = COL_Z + HB * DK
COL_GATE = COL_AB + 2 * HB
NSLAB = (COL_AB // P, 2 * D // P)
LEVELS = (1, 2, 4, 8, 16, 32)
WRING = 2


def bc(ap, at, n):
    a = ap.unsqueeze(at)
    shape = list(a.shape)
    shape[at] = n
    return a.to_broadcast(shape)


class Env:
    pass


def sems(env, tag, *names):
    made = [env.nc.alloc_semaphore(name=f"{tag}_{n}") for n in names]
    env.sems += made
    return made


def clear_sems(env):
    env.nc.clear_and_free_semaphores(env.sems)
    env.nc.all_engine_barrier()
    env.sems = []


def weight_pipe(env, tag, memory):
    w = Env()
    w.raw, w.hi, w.lo = memory
    w.landed = sems(env, tag, *[f"w_landed{i}" for i in range(WRING)])
    w.hi_made, w.lo_made, w.prod = sems(env, tag, "w_hi_made", "w_lo_made", "prod")
    return w


def slab_memory(env, tag, c):
    return [[c.enter_context(env.nc.sbuf_tensor(f"{tag}_{kind}{i}", [P, DC, P], dt)) for i in range(WRING)]
            for kind, dt in (("w_raw", F32), ("w_hi", F32R), ("w_lo", F32R))]


def load_slab(sp, w, i, s, src):
    sp.wait_ge(w.lo_made, 2 * i + s + 1)
    sp.dma_start(w.raw[s][:, :, :], src).then_inc(w.landed[s], 16)


def split_hi(act, w, i, s, last=None):
    act.wait_ge(w.landed[s], 16 * i + 16)
    act.wait_ge(*(last or (w.prod, NTG * (2 * i + s + 1))))
    act.activation(w.hi[s][:, :, :], w.raw[s][:, :, :], ACT.Copy).then_inc(w.hi_made, 1)


def split_lo(pool, w, i, s):
    pool.wait_ge(w.hi_made, 2 * i + s + 1)
    pool.tensor_tensor(w.lo[s][:, :, :], w.raw[s][:, :, :], w.hi[s][:, :, :].bitcast(F32),
                       ALU.subtract).then_inc(w.lo_made, 1)


def slab_products(pe, w, s, x_hi, x_lo, out, chunks, tokens):
    n = 3 * len(chunks)
    k = 0
    for c in chunks:
        for a, b in ((w.lo, x_hi), (w.hi, x_lo), (w.hi, x_hi)):
            last = pe.matmul(out, a[s][:, c, :], b[:, c, tokens], start=k == 0, stop=k == n - 1)
            k += 1
    return last


def select(pool, out, pattern, base, cm, fill=0.0, op=ALU.is_ge):
    return pool.affine_select(out=out, in_=out, compare_op=op, fill=fill, base=base,
                              pattern=pattern, channel_multiplier=cm)


def stage_norm_in(env):
    nc, I = env.nc, env.inp
    squared, rooted, inv, scaled, turned, gained, hi_made, lo_made, const, st_turned, st_copied, vec, gain_in = sems(
        env, "n", "squared", "rooted", "inv", "scaled", "turned", "gained", "hi_made", "lo_made",
        "const", "st_turned", "st_copied", "vec", "gain_in")
    xl = sems(env, "n", *[f"x_landed{t}" for t in range(NT)])
    RING = 4
    with ExitStack() as c:
        x = c.enter_context(nc.sbuf_tensor("n_x", [P, NT, D], F32))
        junk = c.enter_context(nc.sbuf_tensor("n_junk", [P, D], F32))
        ss = c.enter_context(nc.sbuf_tensor("n_ss", [P, NT], F32))
        root = c.enter_context(nc.sbuf_tensor("n_root", [P, NT], F32))
        rstd = c.enter_context(nc.sbuf_tensor("n_rstd", [P, NT], F32))
        h = c.enter_context(nc.sbuf_tensor("n_h", [P, RING, 4, P], F32))
        st = c.enter_context(nc.sbuf_tensor("n_state", [NB * (CW - 1), CONV], F32))
        ps = [c.enter_context(nc.psum_tensor(f"n_ps{i}", [P, 4, P], F32)) for i in range(RING)]
        pst = c.enter_context(nc.psum_tensor("n_pst", [P, CC, NB * (CW - 1)], F32))
        xp = I["x_prompt"].rearrange("a (t p) d -> (a t) p d", p=P)
        xs = I["x_sample"].rearrange("b t d -> (b t) d")
        block = c.enter_context(nc.Block())
        NV = 8
        w = env.w_in_pipe
        w_in = I["w_in"].rearrange("l (c p) n -> p (l c) n", p=P)
        AHEAD = 3

        def out_of(x_part, g):
            return x_part[:, 4 * (g % 2):4 * (g % 2) + 4, (g // 2) * P:(g // 2 + 1) * P]

        def split(act, g):
            act.wait_ge(gained, g + 1)
            act.activation(out_of(env.x_hi, g), h[:, g % RING, :, :], ACT.Copy).then_inc(hi_made, 1)

        def gain(dve, g):
            dve.wait_ge(turned, g + 1)
            if g >= RING:
                dve.wait_ge(hi_made, g - RING + 1)
                dve.wait_ge(lo_made, g - RING + 1)
            half = g % 2
            dve.tensor_tensor(h[:, g % RING, :, :], ps[g % RING][:, :, :],
                              bc(env.gains[:, 0, 4 * half:4 * half + 4], 2, P), ALU.mult).then_inc(gained, 1)

        def split_low(pool, g):
            pool.wait_ge(hi_made, g + 1)
            pool.tensor_tensor(out_of(env.x_lo, g), h[:, g % RING, :, :],
                               out_of(env.x_hi, g).bitcast(F32), ALU.subtract).then_inc(lo_made, 1)

        @block.sync
        def _(sp):
            def gains(k, name, sem):
                sp.dma_start(env.gains[:, k, :], I[name].rearrange("l (c p) -> p (l c)", p=P),
                             allow_slow_non_contiguous=True).then_inc(sem, 16)

            sp.dma_start(x[:, 0, :], xp[0]).then_inc(xl[0], 16)
            gains(0, "norm_mix_pre", gain_in)
            for t in range(1, NT):
                sp.dma_start(x[:, t, :], xp[t] if t < NPT else xs).then_inc(xl[t], 16)
            sp.dma_start(env.wab[:, :, :], w_in[:, :, COL_AB:COL_GATE]).then_inc(env.ab_land, 16)
            for s in range(WRING):
                sp.dma_start(w.raw[s][:, :, :], w_in[:, :, s * P:(s + 1) * P]).then_inc(w.landed[s], 16)
            sp.dma_start(st[:, :], I["state_conv"].rearrange("l b w c -> (l b w) c")).then_inc(vec, 16)
            for k, name in enumerate(("norm_mix_post", "norm_mlp_pre", "norm_mlp_post")):
                gains(k + 1, name, vec)
            sp.dma_start(env.convw[:, :, :], I["conv_w"].rearrange("l w (c p) -> p (l w) c", p=P),
                         allow_slow_non_contiguous=True).then_inc(vec, 16)
            sp.dma_start(env.dgain[:, :], I["delta_norm_w"].rearrange("l p -> p l"),
                         allow_slow_non_contiguous=True).then_inc(vec, 16)
            sp.dma_start(env.alog[:, :], I["a_log"].to_broadcast([P, HB])).then_inc(vec, 16)
            sp.dma_start(env.dtb[:, :], I["dt_bias"].to_broadcast([P, HB])).then_inc(vec, 16)
            sp.wait_ge(vec, 16 * NV)

        @block.scalar
        def _(act):
            act.wait_ge(const, 1)
            for t in range(NT):
                act.wait_ge(xl[t], 16)
                if t:
                    act.wait_ge(squared, t)
                act.activation(junk[:, :], x[:, t, :], ACT.Square,
                               accum_out=ss[:, t:t + 1]).then_inc(squared, 1)
                act.wait_ge(squared, t + 1)
                act.activation(root[:, t:t + 1], ss[:, t:t + 1], ACT.Sqrt, bias=env.eps[:, 0:1],
                               scale=1.0 / D).then_inc(rooted, 1)
                if t >= AHEAD:
                    for g in range(2 * (t - AHEAD), 2 * (t - AHEAD) + 2):
                        split(act, g)
            for g in range(2 * (NT - AHEAD), 2 * NT):
                split(act, g)

        @block.vector
        def _(dve):
            for t in range(NT):
                dve.wait_ge(rooted, t + 1)
                dve.reciprocal(rstd[:, t:t + 1], root[:, t:t + 1]).then_inc(inv, 1)
                dve.wait_ge(inv, t + 1)
                dve.tensor_scalar(x[:, t, :], x[:, t, :], rstd[:, t:t + 1], None, ALU.mult).then_inc(scaled, 1)
                if t == 0:
                    dve.wait_ge(gain_in, 16)
                for g in range(2 * t - 2, 2 * t):
                    if g >= 0:
                        gain(dve, g)
            gain(dve, 2 * NT - 2)
            gain(dve, 2 * NT - 1)
            dve.wait_ge(st_turned, 1)
            dve.tensor_copy(env.state_t[:, :, :], pst[:, :, :]).then_inc(st_copied, 1)

        @block.gpsimd
        def _(pool):
            pool.memset(env.eps[:, :], EPS).then_inc(const, 1)
            n = 1

            def fresh(ap, value):
                nonlocal n
                pool.memset(ap, value).then_inc(const, 1)
                n += 1
                pool.wait_ge(const, n)

            def sel(ap, *a, **k):
                nonlocal n
                select(pool, ap, *a, **k).then_inc(const, 1)
                n += 1
                pool.wait_ge(const, n)

            fresh(env.ident[:, :], 0.0)
            sel(env.ident[:, :], [[-1, P]], 0, 1, fill=1.0, op=ALU.not_equal)
            fresh(env.flip[:, :], 0.0)
            sel(env.flip[:, :], [[1, P]], 1 - P, 1, fill=1.0, op=ALU.not_equal)
            fresh(env.ones[:, :], 1.0)
            for k, L in enumerate((64, TS)):
                nb = P // L
                fresh(env.cum[:, k, :], 1.0)
                v = env.cum[:, k, :].rearrange("p (b r) -> p b r", r=L)
                sel(v, [[-L, nb], [0, L]], 0, 1)
                sel(v, [[L, nb], [0, L]], L - 1, -1)
                sel(v, [[L, nb], [1, L]], 0, -1)
                fresh(env.after[:, k, :], 1.0)
                v = env.after[:, k, :].rearrange("p (b r) -> p b r", r=L)
                sel(v, [[-L, nb], [0, L]], 0, 1)
                sel(v, [[L, nb], [0, L]], L - 1, -1)
                sel(v, [[-L, nb], [-1, L]], -1, 1)
                pool.tensor_scalar(env.shut[:, k, :], env.cum[:, k, :], -NEG, NEG, ALU.mult,
                                   ALU.add).then_inc(const, 1)
                n += 1
                pool.wait_ge(const, n)
                member = env.member[:, 0:2] if k == 0 else env.member[:, 2:2 + NB]
                fresh(member, 1.0)
                sel(member, [[-L, nb]], 0, 1)
                sel(member, [[L, nb]], L - 1, -1)
            for k, s in enumerate(LEVELS):
                nb = P // (2 * s)
                fresh(env.level[:, k, :], 1.0)
                v = env.level[:, k, :].rearrange("p (b r) -> p b r", r=2 * s)
                sel(v, [[-2 * s, nb], [0, 2 * s]], 0, 1)
                sel(v, [[2 * s, nb], [0, 2 * s]], s - 1, -1)
                sel(v, [[0, nb], [1, 2 * s]], -s, 0)
            for g in range(2 * NT):
                split_low(pool, g)

        @block.tensor
        def _(pe):
            pe.wait_ge(const, 3)
            for g in range(2 * NT):
                pe.wait_ge(scaled, g // 2 + 1)
                if g >= RING:
                    pe.wait_ge(gained, g - RING + 1)
                for k in range(4):
                    cc = 4 * (g % 2) + k
                    last = pe.transpose(ps[g % RING][:, k, :], x[:, g // 2, cc * P:(cc + 1) * P],
                                        env.ident[:, :])
                last.then_inc(turned, 1)
            pe.wait_ge(vec, 16 * NV)
            r = NB * (CW - 1)
            for k in range(CC):
                last = pe.transpose(pst[:, k, :], st[:, k * P:(k + 1) * P], env.ident[0:r, 0:r])
            last.then_inc(st_turned, 1)


def stage_in_proj(env):
    nc, I = env.nc, env.inp
    with ExitStack() as c:
        w = env.w_in_pipe
        free, out_s0, out_s1, ab_made, conv_in, conv_y, conv_c, silued, ab_hi, ab_lo, tail, halo = sems(
            env, "i", "free", "sent0", "sent1", "ab_made", "conv_in", "conv_y", "conv_c", "silued",
            "ab_hi", "ab_lo", "tail", "halo")
        ab_rows, ab_read = sems(env, "i", "ab_rows", "ab_rows_read")
        sent = (out_s0, out_s1)
        prod = w.prod
        wab, ab_land = env.wab, env.ab_land
        wab_hi = c.enter_context(nc.sbuf_tensor("i_wab_hi", [P, DC, 2 * HB], F32R))
        wab_lo = c.enter_context(nc.sbuf_tensor("i_wab_lo", [P, DC, 2 * HB], F32R))
        st = [c.enter_context(nc.sbuf_tensor(f"i_out{i}", [P, T], F32)) for i in range(2)]
        rp = [c.enter_context(nc.sbuf_tensor(f"i_raw_prompt{i}", [P, CW - 1 + TP], F32)) for i in range(2)]
        rs = [c.enter_context(nc.sbuf_tensor(f"i_raw_sample{i}", [P, NB, CW - 1 + TS], F32)) for i in range(2)]
        y = [c.enter_context(nc.sbuf_tensor(f"i_y{i}", [P, T], F32)) for i in range(2)]
        ps = [c.enter_context(nc.psum_tensor(f"i_ps{i}", [P, 512], F32)) for i in range(6)]
        ab_row = c.enter_context(nc.sbuf_tensor("i_ab_row", [2 * HB, T], F32))
        pab = c.enter_context(nc.psum_tensor("i_pab", [P, NT, 2 * HB], F32))
        block = c.enter_context(nc.Block())
        NA, NZ = 3 * AW // P, COL_Z // P
        NS = sum(NSLAB)
        w_in = I["w_in"].rearrange("l (c p) n -> p (l c) n", p=P)
        HALF = NS // 2
        CREDIT = 6

        @block.sync
        def _(sp):
            with sp.Fori(1, NSLAB[0] // 2) as i:
                for s in range(2):
                    load_slab(sp, w, i, s, w_in[:, :, bass.ds((2 * i + s) * P, P)])
            for s in range(2):
                sp.wait_ge(sent[s], 16 * (NA // 2) + 16)
            for dst, row, sem in ((env.v, 2 * AW, env.v_in), (env.q, 0, env.qk_in), (env.k, AW, env.qk_in)):
                sp.dma_start(dst[:, :, :], env.proj[row:row + AW, :].rearrange("(c p) t -> p c t", p=P)
                             ).then_inc(sem, 16)
            with sp.Fori(0, NSLAB[1] // 2) as i:
                for s in range(2):
                    load_slab(sp, w, i + NSLAB[0] // 2, s,
                              w_in[:, :, bass.ds((2 * i + s) * P + COL_GATE, P)])

        @block.gpsimd
        def _(pool):
            pool.sem_inc(w.lo_made, WRING)
            pool.wait_ge(ab_hi, 1)
            pool.tensor_tensor(wab_lo[:, :, :], wab[:, :, :], wab_hi[:, :, :].bitcast(F32),
                               ALU.subtract).then_inc(ab_lo, 1)
            with pool.Fori(0, HALF) as i:
                for s in range(2):
                    split_lo(pool, w, i, s)

        def store(act, i, s):
            act.dma_start(env.proj[bass.ds((2 * i + s) * P, P), :], st[s][:, :]).then_inc(sent[s], 16)

        @block.scalar
        def _(act):
            act.wait_ge(ab_land, 16)
            act.activation(wab_hi[:, :, :], wab[:, :, :], ACT.Copy).then_inc(ab_hi, 1)
            for s in range(2):
                split_hi(act, w, 0, s)

            def evacuated(i, s):
                act.wait_ge(free, 3 * (2 * i + s) + 3 + CREDIT)

            def plain(a, b):
                with act.Fori(a, b) as i:
                    for s in range(2):
                        split_hi(act, w, i + 1, s)
                        evacuated(i, s)
                        store(act, i, s)

            plain(0, NA // 2)
            with act.Fori(NA // 2, NZ // 2) as i:
                for s in range(2):
                    split_hi(act, w, i + 1, s)
                    n = 2 * i + s - NA
                    act.wait_ge(conv_c, n + 1)
                    act.wait_ge(sent[s], 16 * i + 16)
                    act.activation(st[s][:, :], y[s][:, :], ACT.Silu).then_inc(silued, 1)
                    act.wait_ge(silued, n + 3)
                    store(act, i, s)
            plain(NZ // 2, HALF - 1)
            for s in range(2):
                evacuated(HALF - 1, s)
                store(act, HALF - 1, s)
            for s in range(2):
                act.wait_ge(sent[s], 16 * HALF + 16)
            act.wait_ge(env.v_in, 16)
            act.wait_ge(env.qk_in, 32)

        @block.vector
        def _(dve):
            dve.sem_inc(free, CREDIT)
            for s in range(2):
                dve.sem_inc(sent[s], 16)
            dve.sem_inc(silued, 2)
            for s in range(2):
                dve.memset(rp[s][:, 0:CW - 1], 0.0).then_inc(halo, 1)
            dve.wait_ge(ab_rows, 1)
            for g in range(NTG):
                dve.tensor_copy(ab_row[:, g * TG:(g + 1) * TG], ps[g][0:2 * HB, 0:TG]).then_inc(ab_read, 1)
            dve.wait_ge(ab_made, 1)
            dve.tensor_copy(env.ab[:, :, :], pab[:, :, :]).then_inc(tail, 1)

            def plain(a, b):
                with dve.Fori(a, b) as i:
                    for s in range(2):
                        dve.wait_ge(sent[s], 16 * i + 16)
                        for g in range(NTG):
                            m = 3 * (2 * i + s) + g
                            dve.wait_ge(prod, m + 1 + CREDIT)
                            dve.tensor_copy(st[s][:, g * TG:(g + 1) * TG],
                                            ps[3 * s + g][:, 0:TG]).then_inc(free, 1)

            plain(0, NA // 2)
            dve.wait_ge(halo, 2)
            with dve.Fori(NA // 2, NZ // 2) as i:
                for s in range(2):
                    n = 2 * i + s - NA
                    cc = n
                    hist = CW - 1
                    dve.tensor_copy(rs[s][:, :, 0:hist],
                                    env.state_t[:, bass.ds(cc, 1), :].rearrange("p a (b w) -> p (a b) w", w=hist)
                                    ).then_inc(conv_in, 1)
                    for g in range(NTG):
                        m = 3 * (2 * i + s) + g
                        dve.wait_ge(prod, m + 1 + CREDIT)
                        if g < NTG - 1:
                            dve.tensor_copy(rp[s][:, hist + g * TG:hist + (g + 1) * TG],
                                            ps[3 * s + g][:, 0:TG]).then_inc(free, 1)
                        else:
                            rest = TP - g * TG
                            dve.tensor_copy(rp[s][:, hist + g * TG:hist + TP],
                                            ps[3 * s + g][:, 0:rest]).then_inc(conv_in, 1)
                            dve.tensor_copy(rs[s][:, :, hist:],
                                            ps[3 * s + g][:, rest:TG].rearrange("p (b t) -> p b t", t=TS)
                                            ).then_inc(free, 1)
                    dve.wait_ge(free, 3 * (2 * i + s) + 3 + CREDIT)
                    dve.wait_ge(conv_in, 2 * n + 2)
                    dve.tensor_copy(env.conv_tail[:, bass.ds(cc, 1), 0:hist],
                                    rp[s][:, TP:TP + hist].unsqueeze(1)).then_inc(tail, 1)
                    dve.tensor_copy(env.conv_tail[:, bass.ds(cc, 1), hist:].rearrange("p a (b w) -> p (a b) w", w=hist),
                                    rs[s][:, :, TS:TS + hist]).then_inc(tail, 1)
                    dve.wait_ge(silued, n + 1)
                    for j in range(CW):
                        for half in range(2):
                            if half == 0:
                                o, v = y[s][:, 0:TP], rp[s][:, j:j + TP]
                            else:
                                o = y[s][:, TP:].rearrange("p (b t) -> p b t", t=TS)
                                v = rs[s][:, :, j:j + TS]
                            wj = env.convw[:, j, bass.ds(cc, 1)]
                            if j == 0:
                                ins = dve.tensor_scalar(o, v, wj, None, ALU.mult)
                            else:
                                dve.wait_ge(conv_y, 6 * n + 2 * (j - 1) + half + 1)
                                ins = dve.scalar_tensor_tensor(out=o, in0=v, scalar=wj, in1=o,
                                                               op0=ALU.mult, op1=ALU.add)
                            if j < CW - 1:
                                ins.then_inc(conv_y, 1)
                            elif half == 1:
                                ins.then_inc(conv_c, 1)
            plain(NZ // 2, HALF)

        @block.tensor
        def _(pe):
            pe.sem_inc(prod, CREDIT)
            pe.wait_ge(ab_lo, 1)
            for g in range(NTG):
                k = 0
                for cc in range(DC):
                    for a, b in ((wab_hi, env.x_lo), (wab_lo, env.x_hi), (wab_hi, env.x_hi)):
                        last = pe.matmul(ps[g][0:2 * HB, 0:TG], a[:, cc, :], b[:, cc, g * TG:(g + 1) * TG],
                                         start=k == 0, stop=k == 3 * DC - 1)
                        k += 1
            last.then_inc(ab_rows, 1)
            pe.wait_ge(ab_read, NTG)
            for t in range(NT):
                last = pe.transpose(pab[:, t, :], ab_row[:, t * P:(t + 1) * P], env.ident[0:2 * HB, 0:2 * HB])
            last.then_inc(ab_made, 1)
            with pe.Fori(0, HALF) as i:
                for s in range(2):
                    pe.wait_ge(w.lo_made, 2 * i + s + 1 + WRING)
                    for g in range(NTG):
                        m = 3 * (2 * i + s) + g
                        pe.wait_ge(free, m + 1)
                        last = slab_products(pe, w, s, env.x_hi, env.x_lo, ps[3 * s + g][:, 0:TG],
                                             range(DC), slice(g * TG, (g + 1) * TG))
                        last.then_inc(prod, 1)


def stage_attention(env):
    nc, I, O_ = env.nc, env.inp, env.out
    SC = AD ** -0.5
    KEYS = 5 * P
    STEP = AH + 1
    NU = NPT * STEP
    SR = 5
    HIST = CW - 1
    ROWS = (NB + 1) * HIST
    k_l0, v_l0, k_l1, v_l1 = sems(env, "a", "k_cache_landed0", "v_cache_landed0", "k_cache_landed1",
                                  "v_cache_landed1")
    k_landed, v_landed = (k_l0, k_l1), (v_l0, v_l1)
    rb_in, ext_out, hank_in, sb_in = sems(env, "a", "rb_in", "ext_out", "hank_in", "sb_in")
    ext_made, pre_made, pre_a, pre_d, bias_made, saved = sems(
        env, "a", "ext_made", "pre_made", "pre_read_act", "pre_read_dve", "bias_made", "saved")
    q_clear, q_padded = sems(env, "a", "q_clear", "q_padded")
    s_made, s_read, s_biased, s_max, p_made, p_scaled = sems(
        env, "a", "s_made", "s_read", "s_biased", "s_max", "p_made", "p_scaled")
    tr_made, tr_read, av_made, av_read, r_made, qd_made = sems(
        env, "a", "tr_made", "tr_read", "av_made", "av_read", "r_made", "qd_made")
    with ExitStack() as c:
        def sb(name, shape):
            return c.enter_context(nc.sbuf_tensor("a_" + name, shape, F32))

        q, k, v = env.q, env.k, env.v
        vt = sb("v_tok", [P, NT, AW])
        k_out = sb("k_out", [P, NT - NPT // 2, AW])
        tail_out = sb("tail_out", [ROWS, CONV])
        bias = sb("bias", [P, AH, 2 * P])
        bias_s = sb("bias_s", [P, P + TS])
        bias_own = sb("bias_own", [P, NB * (P + TS)])
        bias_own_b = bias_own[:, 0:NB * P].rearrange("p (b m) -> p b m", m=P)
        bias_own_d = bias_own[:, :].rearrange("p (b m) -> p b m", m=P + TS)[:, :, 0:TS]
        rb, ext = sb("rb", [AH, 2 * NR + 1]), sb("ext", [AH, 3 * P])
        kc = [sb(f"k_cache{i}", [P, 4, AW]) for i in range(2)]
        vc = [sb(f"v_cache{i}", [P, 4, AW]) for i in range(2)]
        kt = [sb(f"k_cache_t{i}", [P, 4, REACH]) for i in range(2)]
        hank = kt[0][:, :, :].rearrange("p a b -> p (a b)").rearrange("p (h m) -> p h m", m=2 * P)
        qd = [sb(f"q_diag{i}", [P, 4 * (P + 2 * TS)]) for i in range(2)]
        qd_b = [x[:, 0:4 * P].rearrange("p (j m) -> p j m", m=P) for x in qd]
        qd_d = [x[:, :].rearrange("p (j m) -> p j m", m=P + 2 * TS) for x in qd]
        s = [sb(f"s{i}", [P, KEYS]) for i in range(SR)]
        nmax, rsum, rinv = sb("nmax", [P, SR]), sb("rsum", [P, SR]), sb("rinv", [P, SR])
        pt = [sb(f"p_t{i}", [P, KEYS]) for i in range(2)]
        qz = [sb(f"q_padded{i}", [P, P]) for i in range(4)]
        S = [c.enter_context(nc.psum_tensor(f"a_S{i}", [P, 1024], F32)) for i in range(2)]
        TR = c.enter_context(nc.psum_tensor("a_TR", [P, 1024], F32))
        O = [c.enter_context(nc.psum_tensor(f"a_O{i}", [P, 512], F32)) for i in range(2)]
        scratch = nc.dram_tensor("bias_ext", [AH, 3 * P], F32).ap()
        overlap = bass.AP(scratch.tensor, 0, [[1, P], [3 * P, AH], [1, 2 * P]])
        block = c.enter_context(nc.Block())

        PRE = ([("v", t) for t in range(NT)] + [("k", t) for t in range(NPT // 2, NT)]
               + [("tail", t) for t in range(CC // 4)] + [("bias", t) for t in range(AH // 2)])
        NPRE = len(PRE)
        banks = [S[0][:, 0:512], S[0][:, 512:1024], S[1][:, 0:512], S[1][:, 512:1024]]

        def prompt(u):
            return u % STEP < AH

        def stream(b):
            return b * STEP + AH

        def keys_of(u):
            b, h = divmod(u, STEP)
            n = min(b + 1, 5)
            return b, h, n, (b - n + 1) * P

        def jobs(st):
            out = []
            if 0 <= st - 3 < NU:
                out.append(("P", st - 3))
            b, h = divmod(st, STEP)
            if b < NB and h in (AH - 4, AH - 2):
                out.append(("K", 2 * b + (h == AH - 2)))
            return out

        STEPS = NU + 6
        order = [j for st in range(STEPS) for j in jobs(st)]
        job = {j: n for n, j in enumerate(order)}

        @block.sync
        def _(sp):
            sp.dma_start(rb[:, :], I["rel_bias"].rearrange("l h r -> (l h) r")).then_inc(rb_in, 16)
            sp.wait_ge(ext_made, 2)
            sp.dma_start(scratch, ext[:, :]).then_inc(ext_out, 16)
            sp.wait_ge(ext_out, 16)
            sp.dma_start(hank, overlap).then_inc(hank_in, 16)
            def load_k(b):
                if b >= 2:
                    sp.wait_ge(tr_made, job["K", 2 * (b - 2) + 1] + 1)
                sp.dma_start(kc[b % 2][:, :, :], I["cache_attn_k"][0, b].rearrange("(t p) h d -> p t (h d)", p=P)
                             ).then_inc(k_landed[b % 2], 16)

            def load_v(b):
                if b >= 2:
                    sp.wait_ge(av_made, stream(b - 2) + 1)
                sp.dma_start(vc[b % 2][:, :, :], I["cache_attn_v"][0, b].rearrange("(t p) h d -> p t (h d)", p=P)
                             ).then_inc(v_landed[b % 2], 16)

            for b in range(2):
                load_k(b)
                load_v(b)
            sp.wait_ge(pre_d, (NPRE) // 2)
            sp.wait_ge(pre_a, (NPRE + 1) // 2)
            for h in range(AH):
                sp.dma_start(bias_s[h * TS:(h + 1) * TS, :], bias[0:TS, h, 0:P + TS]).then_inc(sb_in, 16)
            half = NPT // 2
            for name, src in (("k", k_out[:, 0:half, :]), ("v", vt[:, half:NPT, :])):
                sp.dma_start(O_[f"prompt_{name}"].rearrange("l a (t p) h d -> p (l a t) (h d)", p=P),
                             src).then_inc(saved, 16)
            for name, src in (("k", k_out[:, half, :]), ("v", vt[:, NPT, :])):
                sp.dma_start(O_[f"sample_{name}"].rearrange("l b t h d -> (l b t) (h d)"),
                             src).then_inc(saved, 16)
            sp.dma_start(O_["prompt_conv"].rearrange("l a w c -> (l a w) c"),
                         tail_out[0:HIST, :]).then_inc(saved, 16)
            sp.dma_start(O_["sample_conv"].rearrange("l b w c -> (l b w) c"),
                         tail_out[HIST:ROWS, :]).then_inc(saved, 16)
            for b in range(2, NB):
                load_k(b)
                load_v(b)
            sp.wait_ge(saved, 16 * 6)

        def pre_read(eng, n, copy, sem):
            kind, t = PRE[n]
            eng.wait_ge(pre_made, n + 1)
            bank = banks[n % 4]
            if kind == "v":
                dst, src = vt[:, t, :], bank
            elif kind == "k":
                dst, src = k_out[:, t - NPT // 2, :], bank
            elif kind == "tail":
                dst, src = tail_out[:, t * 512:(t + 1) * 512], bank[0:ROWS, :]
            else:
                dst, src = bias[:, 2 * t:2 * t + 2, :].rearrange("p h m -> p (h m)"), bank
            copy(dst, src).then_inc(sem, 1)

        @block.scalar
        def _(act):
            for n in range(0, NPRE, 2):
                pre_read(act, n, lambda d, x: act.activation(d, x, ACT.Copy), pre_a)

            def tr_out(j):
                kind, x = j
                act.wait_ge(tr_made, job[j] + 1)
                if kind == "P":
                    n = keys_of(x)[2] * P if prompt(x) else KEYS
                    if x >= 2:
                        act.wait_ge(av_made, x - 1)
                    dst, src = pt[x % 2][:, 0:n], TR[:, 0:n]
                else:
                    b, half = divmod(x, 2)
                    if b >= 2:
                        act.wait_ge(s_made, stream(b - 2) + 1)
                    dst = kt[b % 2][:, 2 * half:2 * half + 2, :].rearrange("p a b -> p (a b)")
                    src = TR[:, :]
                act.activation(dst, src, ACT.Copy).then_inc(tr_read, 1)

            for st in range(STEPS):
                for j in jobs(st):
                    tr_out(j)
                if st < NU:
                    n = keys_of(st)[2] * P if prompt(st) else KEYS
                    act.wait_ge(s_max, st + 1)
                    if st >= SR:
                        act.wait_ge(r_made, st - SR + 1)
                    x = s[st % SR][:, 0:n]
                    act.activation(x, x, ACT.Exp, bias=nmax[:, st % SR:st % SR + 1],
                                   accum_out=rsum[:, st % SR:st % SR + 1]).then_inc(p_made, 1)

        @block.gpsimd
        def _(pool):
            for i in range(4):
                pool.memset(qz[i][:, :], 0.0).then_inc(q_clear, 1)
            pool.wait_ge(q_clear, 4)
            for p in range(NPT * AH):
                b, h = divmod(p, AH)
                if p >= 4:
                    b_, h_ = divmod(p - 4, AH)
                    pool.wait_ge(s_made, b_ * STEP + h_ + 1)
                half = slice(AD * (h % 2), AD * (h % 2) + AD)
                pool.tensor_copy(qz[p % 4][half, :], q[half, h // 2, b * P:(b + 1) * P]).then_inc(q_padded, 1)

        @block.vector
        def _(dve):
            dve.wait_ge(rb_in, 16)
            dve.tensor_copy(ext[:, 0:2 * P], rb[:, 1:2 * NR + 1]).then_inc(ext_made, 1)
            dve.tensor_copy(ext[:, 2 * P:3 * P], rb[:, 2 * NR:2 * NR + 1].to_broadcast([AH, P])
                            ).then_inc(ext_made, 1)
            for i in range(2):
                dve.memset(qd[i][:, :], 0.0).then_inc(qd_made, 1)
            dve.memset(bias_own[:, :], NEG).then_inc(bias_made, 1)
            for n in range(1, NPRE, 2):
                pre_read(dve, n, dve.tensor_copy, pre_d)
            dve.wait_ge(pre_a, (NPRE + 1) // 2)
            dve.wait_ge(pre_d, NPRE // 2)
            dve.memset(bias[0:64, :, P + 64:2 * P], NEG).then_inc(bias_made, 1)
            dve.wait_ge(bias_made, 2)

            biased = 0
            n_qd = 2

            def soft(u):
                nonlocal biased
                r = u % SR
                x, ps = s[r], S[u % 2]
                dve.wait_ge(s_made, u + 1)
                if u >= SR:
                    dve.wait_ge(tr_made, job["P", u - SR] + 1)
                if prompt(u):
                    b, h, n, _ = keys_of(u)
                    W, near = n * P, min(n * P, 2 * P)
                    if W > near:
                        dve.tensor_scalar(x[:, 0:W - near], ps[:, 0:W - near], SC, bias[:, h, 0:1],
                                          ALU.mult, ALU.add).then_inc(s_biased, 1)
                        biased += 1
                    dve.scalar_tensor_tensor(out=x[:, W - near:W], in0=ps[:, W - near:W], scalar=SC,
                                             in1=bias[:, h, 2 * P - near:2 * P], op0=ALU.mult,
                                             op1=ALU.add).then_inc(s_read, 1)
                    dve.wait_ge(s_read, u + 1)
                    if W > near:
                        dve.wait_ge(s_biased, biased)
                    if n == 5:
                        dve.memset(x[64:P, 0:64], NEG).then_inc(s_biased, 1)
                        biased += 1
                        dve.wait_ge(s_biased, biased)
                else:
                    W, b = KEYS, u // STEP
                    if b == 0:
                        dve.wait_ge(sb_in, 16 * AH)
                        dve.tensor_copy(bias_own_d, bc(bias_s[:, P:P + TS], 1, NB)).then_inc(bias_made, 1)
                    dve.tensor_scalar(x[:, 0:3 * P], ps[:, 0:3 * P], SC, bias_s[:, 0:1],
                                      ALU.mult, ALU.add).then_inc(s_biased, 1)
                    dve.scalar_tensor_tensor(out=x[:, 3 * P:4 * P], in0=ps[:, 3 * P:4 * P], scalar=SC,
                                             in1=bias_s[:, 0:P], op0=ALU.mult, op1=ALU.add).then_inc(s_biased, 1)
                    if b == 0:
                        dve.wait_ge(bias_made, 3)
                    dve.scalar_tensor_tensor(out=x[:, 4 * P:5 * P], in0=ps[:, 4 * P:5 * P], scalar=SC,
                                             in1=bias_own_b[:, b, :], op0=ALU.mult, op1=ALU.add).then_inc(s_read, 1)
                    biased += 2
                    dve.wait_ge(s_read, u + 1)
                    dve.wait_ge(s_biased, biased)
                if u >= SR:
                    dve.wait_ge(p_made, u - SR + 1)
                dve.tensor_reduce(nmax[:, r:r + 1], x[:, 0:W], AX.X, ALU.max, negate=True).then_inc(s_max, 1)

            def recip(u):
                r = u % SR
                dve.wait_ge(p_made, u + 1)
                if u >= SR:
                    dve.wait_ge(p_scaled, u - SR + 1)
                dve.reciprocal(rinv[:, r:r + 1], rsum[:, r:r + 1]).then_inc(r_made, 1)
                dve.wait_ge(r_made, u + 1)
                x = s[r][:, 0:keys_of(u)[2] * P if prompt(u) else KEYS]
                dve.tensor_scalar(x, x, rinv[:, r:r + 1], None, ALU.mult).then_inc(p_scaled, 1)

            def out(u):
                if prompt(u):
                    b, h = divmod(u, STEP)
                    half = slice(AD * (h % 2), AD * (h % 2) + AD)
                    dve.wait_ge(av_made, u + 1)
                    dve.tensor_copy(env.oa[half, h // 2, b * P:(b + 1) * P], O[u % 2][half, 0:P]).then_inc(av_read, 1)
                else:
                    b = u // STEP
                    dve.wait_ge(av_made, u + 1)
                    for j in range(4):
                        for half in range(2):
                            col = j * P + 2 * TS * j + TS * half
                            ins = dve.tensor_copy(
                                env.oa[64 * half:64 * half + 64, j, TP + TS * b:TP + TS * (b + 1)],
                                O[u % 2][64 * half:64 * half + 64, col:col + TS])
                    ins.then_inc(av_read, 1)

            for st in range(STEPS):
                if st < NU:
                    soft(st)
                if st + 1 < NU and not prompt(st + 1):
                    b = (st + 1) // STEP
                    if n_qd == 2:
                        dve.wait_ge(qd_made, 2)
                    if b >= 2:
                        dve.wait_ge(s_made, stream(b - 2) + 1)
                    for half in range(2):
                        dve.tensor_copy(qd_d[b % 2][64 * half:64 * half + 64, :, TS * half:TS * half + TS],
                                        q[64 * half:64 * half + 64, :, TP + TS * b:TP + TS * (b + 1)]
                                        ).then_inc(qd_made, 1)
                    n_qd += 2
                u = st - 1
                if 0 <= u < NU:
                    recip(u)
                if 0 <= st - 4 < NU:
                    out(st - 4)

        @block.tensor
        def _(pe):
            for n, (kind, t) in enumerate(PRE):
                if n >= 4:
                    pe.wait_ge(pre_a if n % 2 == 0 else pre_d, (n - 4) // 2 + 1)
                bank = banks[n % 4]
                if kind == "bias" and t == 0:
                    pe.wait_ge(hank_in, 16)
                for i in range(4):
                    o = bank[:, i * P:(i + 1) * P]
                    if kind == "v":
                        last = pe.transpose(o, v[:, i, t * P:(t + 1) * P], env.ident[:, :])
                    elif kind == "k":
                        last = pe.transpose(o, k[:, i, t * P:(t + 1) * P], env.ident[:, :])
                    elif kind == "tail":
                        last = pe.transpose(bank[0:ROWS, i * P:(i + 1) * P], env.conv_tail[:, 4 * t + i, :],
                                            env.ident[:, :])
                    else:
                        h, half = 2 * t + i // 2, i % 2
                        last = pe.matmul(o, hank[:, h, (1 - half) * P:(2 - half) * P], env.flip[:, :],
                                         start=True, stop=True)
                last.then_inc(pre_made, 1)
            pe.wait_ge(pre_a, (NPRE + 1) // 2)
            pe.wait_ge(pre_d, NPRE // 2)

            def scores(u):
                if u >= 2:
                    pe.wait_ge(s_read, u - 1)
                ps = S[u % 2]
                if prompt(u):
                    b, h, n, k0 = keys_of(u)
                    p = b * AH + h
                    pe.wait_ge(q_padded, p + 1)
                    for a in range(0, n * P, 512):
                        z = min(n * P, a + 512)
                        last = pe.matmul(ps[:, a:z], qz[p % 4][:, :], k[:, h // 2, k0 + a:k0 + z],
                                         start=True, stop=True)
                else:
                    b = u // STEP
                    pe.wait_ge(tr_read, job["K", 2 * b + 1] + 1)
                    pe.wait_ge(qd_made, 2 + 2 * (b + 1))
                    for j in range(4):
                        pe.matmul(ps[:, 0:REACH], qd_b[b % 2][:, j, :], kt[b % 2][:, j, :],
                                  start=j == 0, stop=j == 3)
                    for j in range(4):
                        last = pe.matmul(ps[:, REACH:KEYS], qd_b[b % 2][:, j, :], k[:, j, TP:T],
                                         start=j == 0, stop=j == 3)
                last.then_inc(s_made, 1)

            def turn(j):
                kind, x = j
                if job[j]:
                    pe.wait_ge(tr_read, job[j])
                if kind == "P":
                    pe.wait_ge(p_scaled, x + 1)
                    n = keys_of(x)[2] if prompt(x) else 5
                    for i in range(n):
                        last = pe.transpose(TR[:, i * P:(i + 1) * P], s[x % SR][:, i * P:(i + 1) * P],
                                            env.ident[:, :])
                else:
                    b, half = divmod(x, 2)
                    pe.wait_ge(k_landed[b % 2], 16 * (b // 2 + 1))
                    for i in range(8):
                        pair, t = 2 * half + i // 4, i % 4
                        last = pe.transpose(TR[:, i * P:(i + 1) * P], kc[b % 2][:, t, pair * P:(pair + 1) * P],
                                            env.ident[:, :])
                last.then_inc(tr_made, 1)

            def values(u):
                pe.wait_ge(tr_read, job["P", u] + 1)
                if u >= 2:
                    pe.wait_ge(av_read, u - 1)
                if prompt(u):
                    b, h, n, k0 = keys_of(u)
                    for i in range(n):
                        last = pe.matmul(O[u % 2][AD * (h % 2):AD * (h % 2) + AD, 0:P],
                                         vt[:, k0 // P + i, h * AD:(h + 1) * AD], pt[u % 2][:, i * P:(i + 1) * P],
                                         start=i == 0, stop=i == n - 1)
                else:
                    b = u // STEP
                    pe.wait_ge(v_landed[b % 2], 16 * (b // 2 + 1))
                    for j in range(4):
                        for i in range(5):
                            vals = vc[b % 2][:, i, j * P:(j + 1) * P] if i < 4 else vt[:, NPT, j * P:(j + 1) * P]
                            last = pe.matmul(O[u % 2][:, j * P:(j + 1) * P], vals, pt[u % 2][:, i * P:(i + 1) * P],
                                             start=i == 0, stop=i == 4)
                last.then_inc(av_made, 1)

            for st in range(STEPS):
                if st < NU:
                    scores(st)
                for j in jobs(st):
                    turn(j)
                if 0 <= st - 4 < NU:
                    values(st - 4)


def stage_delta(env):
    nc, I, O_ = env.nc, env.inp, env.out
    L = 64
    KD = DK
    PAIRS = [tuple(range(t, min(t + 2, NT))) for t in range(0, NT, 2)]

    def levels(t):
        return len(LEVELS) if t < NPT else 4

    def steps(t):
        inv = [(f"inv{j}{x}") for j in range(1, levels(t)) for x in "ab"]
        return ["turn", "norm_turn", "decay", "pair", "inv0"] + inv + ["solve"]

    PIECES = ("read", "write")

    def schedule():
        out = []
        for p, tiles in enumerate(PAIRS):
            scan = [("scan", t, ch, x) for t in (PAIRS[p - 1] if p else ()) for ch in range(2) for x in PIECES]
            for k in range(len(steps(0))):
                out += [("prep", t, steps(t)[k]) for t in tiles if k < len(steps(t))]
                if k % 2 and scan:
                    out.append(scan.pop(0))
            out += [x for x in scan]
        out += [("heads", NPT, h, x) for h, x in ((0, "read"), (1, "read"), (0, "mask"))]
        for h in range(HB):
            if h + 1 < HB:
                out.append(("heads", NPT, h + 1, "mask"))
            out.append(("heads", NPT, h, "write"))
            if h + 2 < HB:
                out.append(("heads", NPT, h + 2, "read"))
            out += [("final", 2 * h), ("final", 2 * h + 1)]
        return out + [("final", NPT)]

    SCHED = schedule()

    def has(eng, item):
        kind, t, *rest = item
        if kind == "prep":
            s = rest[0]
            lev = int(s[3]) if s.startswith("inv") else None
            return {"pe": True,
                    "act": s in ("turn", "norm_turn", "decay", "solve") or s.endswith("a"),
                    "dve": s in ("turn", "norm_turn", "decay", "pair", "inv0") or s.endswith("b"),
                    "pool": s in ("norm_turn", "pair", "inv0") or (s.endswith("a") and lev + 1 < levels(t))}[eng]
        if kind == "scan":
            ch, x = rest
            return {"pe": True, "dve": True, "act": x == "write" and ch == 1, "pool": x == "read"}[eng]
        if kind == "final":
            return {"pe": True, "dve": True, "act": t in (0, NPT), "pool": False}[eng]
        h, x = rest
        return {"pe": x != "mask", "dve": True, "act": x == "write" and h == HB - 1, "pool": x == "mask"}[eng]

    place = {}
    for eng in ("pe", "act", "dve", "pool"):
        for kind in ("prep", "scan", "heads"):
            for n, item in enumerate(x for x in SCHED if x[0] == kind and has(eng, x)):
                place[(eng, *item)] = n + 1

    sem = {}
    for eng, what in (("pe", "products"), ("act", "moved"), ("dve", "combined"), ("pool", "masked")):
        for kind in ("prep", "scan", "heads"):
            sem[eng, kind], = sems(env, "d", f"{kind}_{what}")

    def wait(e, eng, *item):
        e.wait_ge(sem[eng, item[0]], place[(eng, *item)])

    def did(eng, ins, item):
        ins.then_inc(sem[eng, item[0]], 1)

    rows_read, ss_turned, picked = sems(env, "d", "rows_read", "ss_turned", "picked")
    c_in, z_in, sq_made, ss_made, ss_read, vecs, gates, gmat, sums, cleared, dstep = sems(
        env, "d", "c_in", "z_in", "sq_made", "ss_made", "ss_read", "vecs", "gates", "gmat", "sums", "cleared", "dstep")
    st_l = sems(env, "d", *[f"state_landed{h}" for h in range(HB)])
    sent, z_ready, o_norm, o_turned, o_out, o_root, actv, own = sems(
        env, "d", "state_sent", "z_ready", "o_norm", "o_turned", "o_out", "o_root", "actv", "own")
    with ExitStack() as c:
        def sb(name, shape):
            return c.enter_context(nc.sbuf_tensor("d_" + name, shape, F32))

        C = sb("c", [P, CC, T])
        pairb = sb("pair", [P, 18, 512])

        def slot2(i, t):
            return pairb[:, 9 * (t % 2) + i, :].rearrange("p (h m) -> p h m", m=P)

        kn, kb, qn, qd, kbe, knT, kbT, qnT, AT = (lambda t, i=i: slot2(i, t) for i in range(9))
        Dm, DT, X, M0, M1 = kn, kb, qn, qd, kbT
        quad = sb("quad", [P, 20, 512])

        def slot4(i, t):
            return quad[:, 5 * (t % 4) + i, :].rearrange("p (h m) -> p h m", m=P)

        kd, qdT, QK, WT, U = (lambda t, i=i: slot4(i, t) for i in range(5))
        vn = sb("v_new", [P, HB, P])
        S, Sd = sb("state", [P, HB, P]), sb("state_decayed", [P, HB, P])
        vec = sb("vec", [P, 11, NT, HB])
        (sp_m, sp_e, g, beta, gc, eg, er, s_kn, s_kb, s_qn, at) = (vec[:, i, :, :] for i in range(11))
        nea = sb("nea", [P, HB])
        rs = sb("rs", [P, NT, 2 * HB])
        sso, rso = sb("sso", [P, NT, HB]), sb("rso", [P, NT, HB])
        gm = sb("gm", [P, 2 * NPT + NB, HB])
        gl = sb("g_last", [P, 2 * NPT + NB, HB])
        sqo = sb("sqo", [P, HB, P])
        row = sb("ss_row", [2 * HB, T])
        pick = sb("pick", [P, 4 * HB - 1])
        SQR = 3
        sq = [pairb[:, 3 * i:3 * i + 3, :].rearrange("p a b -> p (a b)")[:, 0:T] for i in range(SQR)]
        W_ = NB * (P + TS)
        keys = C[:, 4:8, :].rearrange("p a b -> p (a b)")
        sh = [keys[:, h * NB * P:(h + 1) * NB * P].rearrange("p (b v) -> p b v", v=P) for h in range(HB)]
        odd, even = (pairb[:, a:a + 9, :].rearrange("p a b -> p (a b)") for a in (9, 0))
        wm, qm = ([odd[:, (2 * i + j) * W_:(2 * i + j + 1) * W_] for i in range(2)] for j in range(2))
        vm = even[:, 0:NB * P].rearrange("p (b v) -> p b v", v=P)
        B = [[c.enter_context(nc.psum_tensor(f"d_B{i}{j}", [P, HB, P], F32)) for j in range(3)] for i in range(2)]
        Z6, Z7 = (c.enter_context(nc.psum_tensor(f"d_Z{i}", [P, HB, P], F32)) for i in (6, 7))
        ZR = (Z6, B[0][2])
        rows = [B[0][i][0:2 * HB, :, :].rearrange("p a b -> p (a b)")[:, 0:TG] for i in range(NTG)]
        block = c.enter_context(nc.Block())

        def kb_of(t):
            return 0 if t < NPT else 1

        def squares(dve, item):
            wait(dve, "act", *item)
            dve.tensor_reduce(sso[:, item[1], :], sqo[:, :, :], AX.X, ALU.add).then_inc(dstep, 1)

        @block.sync
        def _(sp):
            for a, z in ((0, 4), (4, 8), (8, 12)):
                sp.dma_start(C[:, a:z, :], env.proj[3 * AW + a * P:3 * AW + z * P, :].rearrange("(c p) t -> p c t", p=P)
                             ).then_inc(c_in, 16)
                sp.wait_ge(c_in, 16 * (a // 4 + 1))
            wait(sp, "pe", "prep", NPT, "turn")
            sp.dma_start(C[:, 8:12, :], env.proj[COL_Z:COL_Z + 4 * P, :].rearrange("(c p) t -> p c t", p=P)
                         ).then_inc(z_in, 16)
            for h in range(HB):
                sp.dma_start(sh[h], I["state_delta"][0, :, h].rearrange("b k v -> k b v")).then_inc(st_l[h], 16)
            wait(sp, "dve", "scan", NPT - 1, 1, "write")
            sp.dma_start(O_["prompt_delta"].rearrange("l a h k v -> k (l a h) v"), S[:, :, :]).then_inc(own, 16)
            for h in range(HB):
                wait(sp, "dve", "heads", NPT, h, "write")
                sp.dma_start(O_["sample_delta"][0, :, h].rearrange("b k v -> k b v"), sh[h]).then_inc(sent, 16)
            sp.wait_ge(sent, 16 * HB)
            sp.wait_ge(own, 16)

        @block.gpsimd
        def _(pool):
            pool.memset(pick[:, :], 0.0).then_inc(picked, 1)
            pool.wait_ge(picked, 1)
            pool.memset(pick[:, 2 * HB - 1:2 * HB], 1.0).then_inc(picked, 1)
            pool.memset(S[:, :, :], 0.0).then_inc(cleared, 1)
            for item in SCHED:
                kind, t, *rest = item
                if not has("pool", item):
                    continue
                if kind == "prep":
                    s = rest[0]
                    if s == "norm_turn":
                        if t == 0:
                            pool.wait_ge(gates, 1)
                            pool.wait_ge(ss_made, 8)
                        if t >= 2:
                            wait(pool, "dve", "prep", t - 2, f"inv{levels(t - 2) - 1}b")
                        ins = pool.tensor_tensor(AT(t), bc(env.cum[:, kb_of(t), :], 1, HB), bc(g[:, t, :], 2, P), ALU.mult)
                    elif s == "pair":
                        wait(pool, "dve", "prep", t, "pair")
                        wait(pool, "pe", "prep", t, "decay")
                        ins = pool.tensor_tensor(M0(t), AT(t), bc(env.level[:, 0, :], 1, HB), ALU.mult)
                    elif s == "inv0":
                        wait(pool, "pe", "prep", t, "pair")
                        ins = pool.tensor_tensor(M1(t), AT(t), bc(env.level[:, 1, :], 1, HB), ALU.mult)
                    else:
                        j = int(s[3])
                        wait(pool, "pe", "prep", t, f"inv{j - 1}a" if j > 1 else "inv0")
                        if j == 1:
                            wait(pool, "pool", "prep", t, "inv0")
                            wait(pool, "dve", "prep", t, "inv0")
                        M = (M0, M1)[(j + 1) % 2]
                        ins = pool.tensor_tensor(M(t), AT(t), bc(env.level[:, j + 1, :], 1, HB), ALU.mult)
                    did("pool", ins, item)
                elif kind == "scan":
                    ch = rest[0]
                    if (t, ch) == (0, 0):
                        pool.wait_ge(cleared, 1)
                        pool.wait_ge(actv, 8)
                    elif ch == 0:
                        wait(pool, "dve", "scan", t - 1, 1, "write")
                    else:
                        wait(pool, "dve", "scan", t, 0, "write")
                    did("pool", pool.tensor_tensor(Sd[:, :, :], S[:, :, :], bc(gl[:, 2 * t + ch, :], 2, P), ALU.mult), item)
                else:
                    h = rest[0]
                    if h == 0:
                        for eng, last in (("act", "solve"), ("pe", "solve"), ("dve", f"inv{len(LEVELS) - 1}b")):
                            wait(pool, eng, "prep", NPT - 1, last)
                        for m in wm + qm:
                            pool.memset(m, 0.0).then_inc(cleared, 1)
                    wait(pool, "pe", "heads", t, h, "read")
                    did("pool", pool.tensor_tensor(sh[h], sh[h], bc(gl[:, 2 * NPT:, h], 2, P), ALU.mult), item)

        @block.scalar
        def _(act):
            def square(k):
                act.wait_ge(c_in, 16 * (1 + k // HB))
                if k >= SQR:
                    act.wait_ge(ss_made, k - SQR + 1)
                act.activation(sq[k % SQR], C[:, k, :], ACT.Square).then_inc(sq_made, 1)

            act.activation(beta, env.ab[:, :, HB:], ACT.Sigmoid).then_inc(actv, 1)
            act.activation(nea[:, :], env.alog[:, :], ACT.Exp).then_inc(actv, 1)
            act.wait_ge(vecs, 3)
            act.activation(sp_e, sp_e, ACT.Exp, scale=-1.0).then_inc(actv, 1)
            act.wait_ge(actv, 3)
            act.activation(sp_e, sp_e, ACT.Ln, bias=1.0).then_inc(actv, 1)
            for k in range(SQR):
                square(k)
            act.wait_ge(sums, 1)
            act.activation(gc, Z7[:, 0, 0:NT * HB].rearrange("p (t h) -> p t h", h=HB), ACT.Copy).then_inc(actv, 1)
            act.activation(eg, Z7[:, 0, 0:NT * HB].rearrange("p (t h) -> p t h", h=HB), ACT.Exp).then_inc(actv, 1)
            act.activation(er, Z7[:, 1, 0:NT * HB].rearrange("p (t h) -> p t h", h=HB), ACT.Exp).then_inc(actv, 1)
            act.activation(gl[:, :, :], Z7[:, 2, 0:(2 * NPT + NB) * HB].rearrange("p (t h) -> p t h", h=HB), ACT.Exp).then_inc(actv, 1)
            act.wait_ge(actv, 8)
            for k in range(SQR, 2 * HB):
                square(k)
            act.wait_ge(ss_turned, 1)
            act.activation(rs[:, :, :], Z6[:, 0, 0:NT * 2 * HB].rearrange("p (t k) -> p t k", k=2 * HB), ACT.Sqrt,
                           bias=env.eps[:, 0:1]).then_inc(ss_read, 1)
            for item in SCHED:
                kind, t, *rest = item
                if not has("act", item):
                    continue
                if kind == "prep":
                    s, b = rest[0], B[t % 2]
                    wait(act, "pe", *item)
                    if s == "turn":
                        if t >= 4:
                            wait(act, "pe", "scan", t - 4, 1, "write")
                            wait(act, "dve", "scan", t - 4, 1, "read")
                        for h in range(HB):
                            ins = act.activation(U(t)[:, h, :], b[2][:, h, :], ACT.Copy, scale=beta[:, t, h:h + 1])
                    elif s == "norm_turn":
                        for i, dst in enumerate((knT, kbT, qnT)):
                            ins = act.activation(dst(t), b[i][:, :, :], ACT.Copy)
                    elif s == "decay":
                        act.activation(qdT(t), b[0][:, :, :], ACT.Copy)
                        wait(act, "dve", *item)
                        ins = act.activation(QK(t), QK(t), ACT.Exp)
                    elif s == "solve":
                        act.activation(WT(t), b[0][:, :, :], ACT.Copy)
                        ins = act.activation(U(t), b[1][:, :, :], ACT.Copy)
                    else:
                        ins = act.activation(X(t), b[0][:, :, :], ACT.Copy)
                    did("act", ins, item)
                elif kind == "final":
                    tiles = slice(0, NPT) if t == 0 else slice(NPT, NT)
                    act.wait_ge(dstep, tiles.stop)
                    act.activation(rso[:, tiles, :], sso[:, tiles, :], ACT.Sqrt, bias=env.eps[:, 0:1],
                                   scale=1.0 / DK).then_inc(o_root, 1)
                    if t == 0:
                        act.wait_ge(z_in, 16)
                        act.activation(C[:, 8:12, :], C[:, 8:12, :], ACT.Silu).then_inc(z_ready, 1)
                else:
                    wait(act, "pe", *item)
                    act.activation(C[:, 0:HB, t * P:(t + 1) * P], Z7[:, :, :], ACT.Copy)
                    if t:
                        act.wait_ge(dstep, t)
                    did("act", act.activation(sqo[:, :, :], Z7[:, :, :], ACT.Square), item)

        @block.vector
        def _(dve):
            nv = 0

            def step(ins):
                nonlocal nv
                ins.then_inc(vecs, 1)
                nv += 1
                dve.wait_ge(vecs, nv)

            step(dve.tensor_tensor(at, env.ab[:, :, 0:HB], bc(env.dtb[:, :], 1, NT), ALU.add))
            step(dve.tensor_scalar(sp_m, at, 0.0, None, ALU.max))
            step(dve.scalar_tensor_tensor(out=sp_e, in0=sp_m, scalar=2.0, in1=at, op0=ALU.mult,
                                          op1=ALU.subtract))
            dve.wait_ge(actv, 4)
            step(dve.tensor_tensor(sp_m, sp_m, sp_e, ALU.add))
            step(dve.tensor_scalar(sp_m, sp_m, -1.0, None, ALU.mult))
            dve.tensor_tensor(g, sp_m, bc(nea[:, :], 1, NT), ALU.mult).then_inc(gates, 1)
            dve.wait_ge(gates, 1)
            for ch in range(2):
                dve.tensor_scalar(gm[:, ch:2 * NPT:2, :], g[:, 0:NPT, :], env.member[:, ch:ch + 1], None,
                                  ALU.mult).then_inc(gmat, 1)
            dve.tensor_tensor(gm[:, 2 * NPT:, :], bc(g[:, NPT, :], 1, NB), bc(env.member[:, 2:2 + NB], 2, HB),
                              ALU.mult).then_inc(gmat, 1)
            dve.wait_ge(ss_made, 2 * HB)
            for i in range(NTG):
                dve.tensor_copy(row[:, i * TG:(i + 1) * TG], rows[i]).then_inc(rows_read, 1)
            dve.wait_ge(ss_read, 1)
            step(dve.reciprocal(rs[:, :, :], rs[:, :, :]))
            dve.wait_ge(actv, 8)
            step(dve.tensor_scalar(s_qn, rs[:, :, 0:HB], KD ** -0.5, None, ALU.mult))
            step(dve.tensor_copy(s_kn, rs[:, :, HB:]))
            step(dve.tensor_tensor(s_kb, s_kn, beta, ALU.mult))

            def scale_o(t):
                o = C[:, 0:HB, t * P:(t + 1) * P]
                dve.tensor_tensor(o, o, bc(rso[:, t, :], 2, P), ALU.mult).then_inc(o_norm, 1)

            def final(t):
                if t in (0, NPT):
                    tiles = slice(0, NPT) if t == 0 else slice(NPT, NT)
                    dve.wait_ge(o_root, 1 if t == 0 else 2)
                    step(dve.reciprocal(rso[:, tiles, :], rso[:, tiles, :]))
                    scale_o(t)
                if t + 1 < NPT:
                    scale_o(t + 1)
                if t == 0:
                    dve.wait_ge(z_ready, 1)
                dve.wait_ge(o_turned, t + 1)
                tk = slice(t * P, (t + 1) * P)
                dve.scalar_tensor_tensor(out=env.ob[:, :, tk], in0=B[1][t % 2][:, :, :], scalar=env.dgain[:, 0:1],
                                         in1=C[:, 8:12, tk], op0=ALU.mult, op1=ALU.mult).then_inc(o_out, 1)

            for item in SCHED:
                kind, t, *rest = item
                if not has("dve", item):
                    continue
                if kind == "final":
                    final(t)
                    continue
                if kind == "prep":
                    s, b = rest[0], B[t % 2]
                    if s != "norm_turn":
                        wait(dve, "pe", *item)
                    if s == "turn":
                        if t >= 4:
                            wait(dve, "pe", "scan", t - 4, 1, "write")
                        for dst, src, col in ((qn, 0, s_qn), (kn, 1, s_kn), (kb, 1, s_kb)):
                            ins = dve.tensor_tensor(dst(t), b[src][:, :, :], bc(col[:, t, :], 2, P), ALU.mult)
                    elif s == "norm_turn":
                        wait(dve, "dve", "prep", t, "turn")
                        did("dve", dve.tensor_tensor(qd(t), qn(t), bc(eg[:, t, :], 2, P), ALU.mult), item)
                        dve.tensor_tensor(kbe(t), kb(t), bc(eg[:, t, :], 2, P), ALU.mult)
                        dve.tensor_tensor(kd(t), kn(t), bc(er[:, t, :], 2, P), ALU.mult)
                        continue
                    elif s == "decay":
                        ins = dve.tensor_tensor(QK(t), b[1][:, :, :], bc(gc[:, t, :], 2, P), ALU.subtract)
                    elif s == "pair":
                        wait(dve, "act", "prep", t, "decay")
                        dve.tensor_tensor(AT(t), b[2][:, :, :], QK(t), ALU.mult)
                        ins = dve.tensor_tensor(QK(t), b[0][:, :, :], QK(t), ALU.mult)
                    elif s == "inv0":
                        wait(dve, "pool", "prep", t, "pair")
                        dve.tensor_tensor(DT(t), bc(env.ident[:, :], 1, HB), M0(t), ALU.subtract)
                        ins = dve.tensor_tensor(Dm(t), bc(env.ident[:, :], 1, HB), b[1][:, :, :], ALU.subtract)
                    else:
                        if s == "inv1b":
                            wait(dve, "dve", "prep", t, "inv0")
                        else:
                            wait(dve, "dve", "prep", t, f"inv{int(s[3]) - 1}b")
                        ins = dve.tensor_tensor(DT(t), DT(t), b[2][:, :, :], ALU.subtract)
                        if int(s[3]) + 1 < levels(t):
                            ins = dve.tensor_tensor(Dm(t), Dm(t), b[1][:, :, :], ALU.subtract)
                    did("dve", ins, item)
                elif kind == "scan":
                    ch, x = rest
                    wait(dve, "pe", *item)
                    if x == "read":
                        wait(dve, "act", "prep", t, "solve")
                        r = slice(L * ch, L * ch + L)
                        ins = dve.tensor_tensor(vn[r, :, :], U(t)[r, :, :], Z6[r, :, :], ALU.subtract)
                    else:
                        wait(dve, "pool", "scan", t, ch, "read")
                        ins = dve.tensor_tensor(S[:, :, :], Sd[:, :, :], Z6[:, :, :], ALU.add)
                    did("dve", ins, item)
                    if ch == 1 and x == "write":
                        squares(dve, item)
                else:
                    h, x = rest
                    if x == "read":
                        if h == 0:
                            wait(dve, "act", "prep", t, "solve")
                            wait(dve, "pe", "prep", t, "solve")
                            dve.wait_ge(cleared, 5)
                        elif h >= 2:
                            wait(dve, "pe", "heads", t, h - 2, "read")
                        for m, src in ((wm[h % 2], WT), (qm[h % 2], qdT)):
                            ins = dve.tensor_copy(m.rearrange("p (b v) -> p b v", v=P + TS)[:, :, 0:TS],
                                                  src(t)[:, h, :].rearrange("p (b v) -> p b v", v=TS))
                    elif x == "mask":
                        wait(dve, "pe", "heads", t, h, "read")
                        step(dve.tensor_tensor(vn[:, h, :], U(t)[:, h, :], ZR[h % 2][:, 0, :], ALU.subtract))
                        if h:
                            wait(dve, "pe", "heads", t, h - 1, "write")
                        ins = dve.tensor_tensor(vm, bc(vn[:, h, :], 1, NB), bc(env.member[:, 2:2 + NB], 2, P), ALU.mult)
                    else:
                        wait(dve, "pe", "heads", t, h, "write")
                        wait(dve, "pool", "heads", t, h, "mask")
                        for i in range(2):
                            o = sh[h][:, 4 * i:4 * i + 4, :]
                            ins = dve.tensor_tensor(o, o, B[0][i][:, :, :], ALU.add)
                    did("dve", ins, item)
                    if h == HB - 1 and x == "write":
                        squares(dve, item)

        @block.tensor
        def _(pe):
            pe.wait_ge(gmat, 3)
            for i, m in enumerate((env.cum, env.after)):
                pe.matmul(Z7[:, i, 0:NPT * HB], m[:, 0, :], g[:, 0:NPT, :], start=True, stop=True)
                pe.matmul(Z7[:, i, NPT * HB:NT * HB], m[:, 1, :], g[:, NPT, :], start=True, stop=True)
            pe.matmul(Z7[:, 2, 0:(2 * NPT + NB) * HB], env.ones[:, :], gm[:, :, :], start=True, stop=True).then_inc(sums, 1)
            pe.wait_ge(picked, 2)
            n = 2 * HB
            for k in range(n):
                pe.wait_ge(sq_made, k + 1)
                for i in range(NTG):
                    last = pe.matmul(rows[i], pick[:, n - 1 - k:2 * n - 1 - k], sq[k % SQR][:, i * TG:(i + 1) * TG],
                                     start=k == 0, stop=k == n - 1)
                last.then_inc(ss_made, 1)
            pe.wait_ge(rows_read, NTG)
            for t in range(NT):
                last = pe.transpose(Z6[:, 0, t * n:(t + 1) * n], row[:, t * P:(t + 1) * P], env.ident[0:n, 0:n])
            last.then_inc(ss_turned, 1)
            pe.wait_ge(c_in, 48)
            pe.wait_ge(actv, 8)
            def final(t):
                if t == 0:
                    wait(pe, "act", "prep", NPT - 1, "solve")
                if t >= 2:
                    pe.wait_ge(o_out, t - 1)
                pe.wait_ge(o_norm, t + 1)
                for h in range(HB):
                    last = pe.transpose(B[1][t % 2][:, h, :], C[:, h, t * P:(t + 1) * P], env.ident[:, :])
                last.then_inc(o_turned, 1)

            for item in SCHED:
                kind, t, *rest = item
                if not has("pe", item):
                    continue
                if kind == "final":
                    final(t)
                    continue
                if kind == "prep":
                    s, b = rest[0], B[t % 2]

                    def heads(bank, lhs, rhs, turn=False):
                        for h in range(HB):
                            a, r = lhs(t)[:, h, :], (env.ident[:, :] if rhs is None else rhs(t)[:, h, :])
                            if turn:
                                last = pe.transpose(bank[:, h, :], a, env.ident[:, :])
                            else:
                                last = pe.matmul(bank[:, h, :], a, r, start=True, stop=True)
                        return last

                    def sofar(eng, s_):
                        wait(pe, eng, "prep", t, s_)

                    if s == "turn":
                        if t >= 2:
                            wait(pe, "act", "prep", t - 2, "solve")
                            wait(pe, "dve", "prep", t - 2, f"inv{levels(t - 2) - 1}b")
                        for i in range(3):
                            ins = heads(b[i], lambda t_, i=i: C[:, 4 * i:4 * i + 4, t * P:(t + 1) * P], None, True)
                    elif s == "norm_turn":
                        sofar("dve", "turn")
                        heads(b[0], kn, None, True)
                        heads(b[1], kb, None, True)
                        sofar("act", "turn")
                        ins = heads(b[2], qn, None, True)
                    elif s == "decay":
                        sofar("act", "norm_turn")
                        sofar("dve", "norm_turn")
                        heads(b[0], qd, None, True)
                        sofar("pool", "norm_turn")
                        pe.matmul(b[1][:, :, :], env.ones[:, :], AT(t), start=True, stop=False)
                        ins = pe.matmul(b[1][:, :, :], env.ident[:, :], bc(env.shut[:, kb_of(t), :], 1, HB),
                                        start=False, stop=True)
                    elif s == "pair":
                        heads(b[2], knT, kbT)
                        sofar("act", "decay")
                        ins = heads(b[0], knT, qnT)
                    elif s == "inv0":
                        sofar("pool", "pair")
                        ins = heads(b[1], M0, None)
                    elif s.endswith("a"):
                        j = int(s[3])
                        if j == 1:
                            sofar("pool", "inv0")
                            sofar("dve", "inv0")
                        else:
                            sofar("pool", f"inv{j - 1}a")
                            sofar("dve", f"inv{j - 1}b")
                        ins = heads(b[0], (M0, M1)[j % 2], Dm)
                    elif s.endswith("b"):
                        sofar("act", s[:-1] + "a")
                        ins = heads(b[2], X, DT)
                        if int(s[3]) + 1 < levels(t):
                            ins = heads(b[1], DT, X)
                    else:
                        sofar("dve", f"inv{levels(t) - 1}b")
                        heads(b[0], kbe, DT)
                        ins = heads(b[1], DT, U)
                    did("pe", ins, item)
                elif kind == "scan":
                    ch, x = rest
                    r = slice(L * ch, L * ch + L)
                    if x == "read":
                        wait(pe, "act", "prep", t, "solve")
                        if (t, ch) == (0, 0):
                            pe.wait_ge(cleared, 1)
                        elif ch == 0:
                            wait(pe, "dve", "scan", t - 1, 1, "write")
                            wait(pe, "act", "scan", t - 1, 1, "write")
                        else:
                            wait(pe, "dve", "scan", t, 0, "write")
                        for h in range(HB):
                            last = pe.matmul(Z6[r, h, :], WT(t)[:, h, r], S[:, h, :], start=True, stop=True)
                        for h in range(HB):
                            last = pe.matmul(Z7[r, h, :], qdT(t)[:, h, r], S[:, h, :], start=h == 0, stop=False,
                                             skip_group_check=True)
                        did("pe", last, item)
                    else:
                        wait(pe, "dve", "scan", t, ch, "read")
                        for h in range(HB):
                            last = pe.matmul(Z6[:, h, :], kd(t)[r, h, :], vn[r, h, :], start=True, stop=True)
                        if ch == 1:
                            for h in range(HB):
                                last = pe.matmul(Z7[:, h, :], QK(t)[:, h, :], vn[:, h, :], start=False,
                                                 stop=h == HB - 1, skip_group_check=True)
                        did("pe", last, item)
                else:
                    h, x = rest
                    if x == "read":
                        wait(pe, "dve", *item)
                        pe.wait_ge(st_l[h], 16)
                        if h == 0:
                            wait(pe, "act", "scan", NPT - 1, 1, "write")
                            wait(pe, "dve", "scan", NPT - 1, 1, "write")
                        elif h >= 2:
                            wait(pe, "dve", "heads", t, h - 2, "mask")
                        for b_ in range(NB):
                            pe.matmul(ZR[h % 2][:, 0, :], wm[h % 2][:, b_ * P:(b_ + 1) * P], sh[h][:, b_, :],
                                      start=b_ == 0, stop=b_ == NB - 1)
                        for b_ in range(NB):
                            last = pe.matmul(Z7[:, h, :], qm[h % 2][:, b_ * P:(b_ + 1) * P], sh[h][:, b_, :],
                                             start=h == 0 and b_ == 0, stop=False, skip_group_check=True)
                        did("pe", last, item)
                    else:
                        wait(pe, "dve", "heads", t, h, "mask")
                        if h:
                            wait(pe, "dve", "heads", t, h - 1, "write")
                        pe.matmul(Z7[:, h, :], QK(t)[:, h, :], vn[:, h, :], start=False, stop=True, skip_group_check=True)
                        for i in range(2):
                            last = pe.matmul(B[0][i][:, :, :], kd(t)[:, h, :], vm[:, 4 * i:4 * i + 4, :],
                                             start=True, stop=True)
                        did("pe", last, item)


def split_activations(env, tag, src):
    hi, lo_p, lo_d = sems(env, tag, "x_hi_made", "x_lo_pool", "x_lo_dve")

    def act(e):
        for k in range(DC):
            e.activation(env.x_hi[:, k, :], src(k), ACT.Copy).then_inc(hi, 1)

    def low(e, mine, sem):
        for k in mine:
            e.wait_ge(hi, k + 1)
            e.tensor_tensor(env.x_lo[:, k, :], src(k), env.x_hi[:, k, :].bitcast(F32),
                            ALU.subtract).then_inc(sem, 1)

    def wait(e):
        e.wait_ge(lo_p, 2)
        e.wait_ge(lo_d, 6)

    return act, lambda e: low(e, (0, 4), lo_p), lambda e: low(e, (1, 2, 3, 5, 6, 7), lo_d), wait


class TokenStats:

    def __init__(self, env, tag, out, wide):
        self.env, self.out, self.wide = env, out, wide
        self.total, self.root, self.inv = sems(env, tag, "sq_total", "sq_root", "rms_inv")

    def pe(self, e, g, squares):
        for k, sq in enumerate(squares):
            last = e.matmul(self.wide[g][:, 0:TG], self.env.ones[:, :], sq, start=k == 0, stop=k == len(squares) - 1)
        last.then_inc(self.total, 1)

    def act(self, e, g):
        e.wait_ge(self.total, g + 1)
        e.activation(self.out[:, g * TG:(g + 1) * TG], self.wide[g][:, 0:TG], ACT.Sqrt,
                     bias=self.env.eps[:, 0:1], scale=1.0 / D).then_inc(self.root, 1)

    def dve(self, e, g):
        tk = slice(g * TG, (g + 1) * TG)
        e.wait_ge(self.root, g + 1)
        e.reciprocal(self.out[:, tk], self.out[:, tk]).then_inc(self.inv, 1)
        e.wait_ge(self.inv, g + 1)


class ColumnStats:

    def __init__(self, env, tag, sumsq, col, diag, groups, banks, wide):
        self.env, self.sumsq, self.col, self.diag = env, sumsq, col, diag
        self.groups, self.banks, self.wide = groups, banks, wide
        self.total, self.root, self.inv, self.diag_made, self.spread = sems(
            env, tag, "sq_total", "sq_root", "rms_inv", "rms_diag", "rms_spread")

    def pe_sum(self, e, g):
        for t in self.groups[g]:
            last = e.matmul(self.banks[g][:, t:t + 1], self.sumsq[:, t * P:(t + 1) * P], self.env.ones[:, 0:1],
                            start=True, stop=True)
        last.then_inc(self.total, 1)

    def pe_spread(self, e, g):
        e.wait_ge(self.diag_made, g + 1)
        ts = self.groups[g]
        for t in ts[::3]:
            e.matmul(self.wide[t // 3][:, 0:TG], self.env.ones[:, :], self.diag[:, t:t + 3, :],
                     start=True, stop=True).then_inc(self.spread, 1)

    def act(self, e, g):
        ts = slice(self.groups[g][0], self.groups[g][-1] + 1)
        e.wait_ge(self.total, g + 1)
        e.activation(self.col[:, ts], self.banks[g][:, ts], ACT.Sqrt, bias=self.env.eps[:, 0:1],
                     scale=1.0 / D).then_inc(self.root, 1)

    def dve(self, e, g):
        ts = slice(self.groups[g][0], self.groups[g][-1] + 1)
        n = len(self.groups[g])
        e.wait_ge(self.root, g + 1)
        e.reciprocal(self.col[:, ts], self.col[:, ts]).then_inc(self.inv, 1)
        e.wait_ge(self.inv, g + 1)
        e.tensor_tensor(self.diag[:, ts, :], bc(self.env.ident[:, :], 1, n), bc(self.col[:, ts], 2, P),
                        ALU.mult).then_inc(self.diag_made, 1)


def stage_merge(env):
    nc, I = env.nc, env.inp
    with ExitStack() as c:
        w, nxt = weight_pipe(env, "m", env.slabs), env.w_out_pipe
        free, g_free, sig = sems(env, "m", "free", "gates_free", "sigmoids")
        prod = w.prod
        g_in = sems(env, "m", "gates_landed0", "gates_landed1")
        gate = [c.enter_context(nc.sbuf_tensor(f"m_gates{i}", [P, 2, T], F32)) for i in range(2)]
        ps = [c.enter_context(nc.psum_tensor(f"m_ps{i}", [P, 512], F32)) for i in range(6)]
        s_act, s_pool, s_dve, s_wait = split_activations(
            env, "m", lambda k: (env.oa if k < 4 else env.ob)[:, k % 4, :])
        block = c.enter_context(nc.Block())
        CREDIT = 6
        HALF = DC // 2
        wa = I["w_proj_a"].rearrange("l (c p) n -> p (l c) n", p=P)
        wb = I["w_proj_b"].rearrange("l (c p) n -> p (l c) n", p=P)

        @block.sync
        def _(sp):
            with sp.Fori(0, HALF) as i:
                for s in range(2):
                    m = 2 * i + s
                    sp.wait_ge(w.lo_made, m + 1)
                    for k, src in enumerate((wa, wb)):
                        sp.dma_start(w.raw[s][:, 4 * k:4 * k + 4, :], src[:, :, bass.ds(m * P, P)]
                                     ).then_inc(w.landed[s], 16)
                    sp.wait_ge(g_free, m + 1)
                    row = (NSLAB[0] + m) * P
                    for k in range(2):
                        sp.dma_start(gate[s][:, k, :], env.proj[bass.ds(row + k * D, P), :]).then_inc(g_in[s], 16)
            for s in range(WRING):
                sp.wait_ge(w.lo_made, DC + s + 1)
                sp.dma_start(nxt.raw[s][:, :, :], I["w_out"].rearrange("l (c p) n -> p (l c) n", p=P)[
                    :, :, s * P:(s + 1) * P]).then_inc(nxt.landed[s], 16)

        @block.gpsimd
        def _(pool):
            pool.sem_inc(w.lo_made, WRING)
            s_pool(pool)
            with pool.Fori(0, HALF) as i:
                for s in range(2):
                    split_lo(pool, w, i, s)
            pool.sem_inc(nxt.lo_made, WRING)
            for s in range(WRING):
                split_lo(pool, nxt, 0, s)

        @block.scalar
        def _(act):
            def hi(i, s):
                act.wait_ge(w.landed[s], 32 * i + 32)
                act.wait_ge(w.prod, NTG * (2 * i + s + 1))
                act.activation(w.hi[s][:, :, :], w.raw[s][:, :, :], ACT.Copy).then_inc(w.hi_made, 1)

            def gates(i, s):
                act.wait_ge(g_in[s], 32 * i + 32)
                act.activation(gate[s][:, :, :], gate[s][:, :, :], ACT.Sigmoid).then_inc(sig, 1)

            s_act(act)
            with act.Fori(0, HALF) as i:
                for s in range(2):
                    hi(i, s)
                    gates(i, s)
            for s in range(WRING):
                split_hi(act, nxt, 0, s, last=(w.prod, NTG * (DC + s + 1)))

        @block.vector
        def _(dve):
            dve.sem_inc(free, CREDIT)
            dve.sem_inc(g_free, 2)
            s_dve(dve)
            with dve.Fori(0, HALF) as i:
                for s in range(2):
                    m = 2 * i + s
                    dve.wait_ge(sig, m + 1)
                    for g in range(NTG):
                        tk = slice(g * TG, (g + 1) * TG)
                        dve.wait_ge(prod, NTG * (m + WRING) + g + 1)
                        for k in range(2):
                            dve.tensor_tensor(gate[s][:, k, tk], gate[s][:, k, tk], ps[2 * g + k][:, 0:TG],
                                              ALU.mult).then_inc(free, 1)
                    dve.wait_ge(free, 6 * m + 6 + CREDIT)
                    dve.tensor_tensor(env.merged[:, bass.ds(m, 1), :], gate[s][:, 0:1, :], gate[s][:, 1:2, :],
                                      ALU.add).then_inc(g_free, 1)

        @block.tensor
        def _(pe):
            pe.sem_inc(prod, NTG * WRING)
            pe.sem_inc(nxt.prod, NTG * WRING)
            s_wait(pe)
            with pe.Fori(0, HALF) as i:
                for s in range(2):
                    m = 2 * i + s
                    pe.wait_ge(w.lo_made, m + 1 + WRING)
                    for g in range(NTG):
                        pe.wait_ge(free, 6 * m + 2 * g + 2)
                        for k in range(2):
                            last = slab_products(pe, w, s, env.x_hi, env.x_lo, ps[2 * g + k][:, 0:TG],
                                                 range(4 * k, 4 * k + 4), slice(g * TG, (g + 1) * TG))
                        last.then_inc(prod, 1)


def stage_out_proj(env):
    nc, I = env.nc, env.inp
    with ExitStack() as c:
        w, nxt = env.w_out_pipe, env.mlp_pipe
        free, sq_made, sq_free, x_turned, x_read_d, x_read_a, summed, added, squared2, saved, normed = sems(
            env, "o", "free", "sq_made", "sq_free", "x_turned", "x_read_dve", "x_read_act", "summed",
            "added", "squared2", "saved", "normed")
        x_in = sems(env, "o", "x_in0", "x_in1", "x_in2")
        prod = w.prod
        xt = c.enter_context(nc.sbuf_tensor("o_xt", [P, DC, T], F32))
        XR = 3
        x = [c.enter_context(nc.sbuf_tensor(f"o_x{i}", [P, D], F32)) for i in range(XR)]
        sq = [c.enter_context(nc.sbuf_tensor(f"o_sq{i}", [P, T], F32)) for i in range(2)]
        sumsq = c.enter_context(nc.sbuf_tensor("o_sumsq", [P, T], F32))
        col = c.enter_context(nc.sbuf_tensor("o_rms", [P, NT], F32))
        diag = c.enter_context(nc.sbuf_tensor("o_rms_diag", [P, NT, P], F32))
        ps = [c.enter_context(nc.psum_tensor(f"o_ps{i}", [P, 512], F32)) for i in range(6)]
        banks = [c.enter_context(nc.psum_tensor(f"o_cols{i}", [P, 512], F32)) for i in range(2)]
        st1 = ColumnStats(env, "o1", sumsq, col, diag, [range(NT)], [banks[0]], ps[0:3])
        st2 = ColumnStats(env, "o2", sumsq, col, diag, [range(3 * g, 3 * g + 3) for g in range(NTG)],
                          [banks[1], ps[3], ps[4]], ps[0:3])
        hi2, lo2p, lo2d, normed2, sum2 = sems(env, "o", "h_hi_made", "h_lo_pool", "h_lo_dve", "y_normed", "sum2")
        y = env.merged
        s_act, s_pool, s_dve, s_wait = split_activations(env, "o", lambda k: y[:, k, :])
        block = c.enter_context(nc.Block())
        CREDIT = 6
        HALF = DC // 2
        w_out = I["w_out"].rearrange("l (c p) n -> p (l c) n", p=P)
        xp = I["x_prompt"].rearrange("a (t p) d -> (a t) p d", p=P)
        xs = I["x_sample"].rearrange("b t d -> (b t) d")
        NG = 2 * NT

        def low(e, g, a, z, sem):
            tk = slice(g * TG, (g + 1) * TG)
            e.wait_ge(hi2, g + 1)
            e.tensor_tensor(env.x_lo[:, a:z, tk], y[:, a:z, tk], env.x_hi[:, a:z, tk].bitcast(F32),
                            ALU.subtract).then_inc(sem, 1)

        def group(g):
            return xt[:, 4 * (g % 2):4 * (g % 2) + 4, (g // 2) * P:(g // 2 + 1) * P]

        def x_read(e, g, sem, copy):
            e.wait_ge(x_turned, g + 1)
            copy(group(g), ps[g % 6][:, :].rearrange("p (c m) -> p c m", m=P)).then_inc(sem, 1)

        @block.sync
        def _(sp):
            for t in range(NT):
                if t >= XR:
                    sp.wait_ge(x_turned, 2 * (t - XR) + 2)
                sp.dma_start(x[t % XR][:, :], xp[t] if t < NPT else xs).then_inc(x_in[t % XR], 16)
            with sp.Fori(1, HALF) as i:
                for s in range(2):
                    load_slab(sp, w, i, s, w_out[:, :, bass.ds((2 * i + s) * P, P)])
            for a in range(2):
                sp.wait_ge(w.lo_made, DC + a + 1)
                sp.dma_start(nxt.raw[a][:, :, :], I["w_up"].rearrange("l (c p) n -> p (l c) n", p=P)[
                    :, :, a * P:(a + 1) * P]).then_inc(nxt.landed[a], 16)
            resid = env.resid.rearrange("(c p) t -> p c t", p=P)
            for g in range(NTG):
                tk = slice(g * TG, (g + 1) * TG)
                sp.wait_ge(added, g + 1)
                sp.dma_start(resid[:, :, tk], xt[:, :, tk]).then_inc(saved, 16)
            sp.wait_ge(saved, 16 * NTG)

        @block.gpsimd
        def _(pool):
            pool.sem_inc(sq_free, 2)
            pool.memset(sumsq[:, :], 0.0).then_inc(summed, 1)
            s_pool(pool)
            with pool.Fori(0, HALF - 1) as i:
                for s in range(2):
                    split_lo(pool, w, i + 1, s)
                    pool.wait_ge(summed, 2 * i + s + 1)
                    pool.wait_ge(sq_made, 2 * i + s + 1)
                    pool.tensor_tensor(sumsq[:, :], sumsq[:, :], sq[s][:, :], ALU.add).then_inc(summed, 1)
                    pool.wait_ge(summed, 2 * i + s + 2)
                    pool.sem_inc(sq_free, 1)
            for m in range(DC - 2, DC):
                pool.wait_ge(summed, m + 1)
                pool.wait_ge(sq_made, m + 1)
                pool.tensor_tensor(sumsq[:, :], sumsq[:, :], sq[m % 2][:, :], ALU.add).then_inc(summed, 1)
            pool.sem_inc(nxt.lo_made, 2)
            for a in range(2):
                pool.wait_ge(nxt.hi_made, a + 1)
                pool.tensor_tensor(nxt.lo[a][:, :, :], nxt.raw[a][:, :, :], nxt.hi[a][:, :, :].bitcast(F32),
                                   ALU.subtract).then_inc(nxt.lo_made, 1)
            for g in range(NTG):
                tk = slice(g * TG, (g + 1) * TG)
                pool.wait_ge(squared2, g + 1)
                for k in range(1, DC):
                    if k > 1:
                        pool.wait_ge(sum2, (DC - 1) * g + k - 1)
                    pool.tensor_tensor(sumsq[:, tk], y[:, 0, tk] if k == 1 else sumsq[:, tk], y[:, k, tk],
                                       ALU.add).then_inc(sum2, 1)
            for g in range(NTG):
                low(pool, g, 5, DC, lo2p)

        @block.scalar
        def _(act):
            s_act(act)
            for g in range(1, NG, 2):
                x_read(act, g, x_read_a, lambda d, s_: act.activation(d, s_, ACT.Copy))

            def square(m, s):
                act.wait_ge(free, 3 * m + 3 + CREDIT)
                act.wait_ge(sq_free, m + 1)
                act.activation(sq[s][:, :].unsqueeze(1), y[:, bass.ds(m, 1), :], ACT.Square).then_inc(sq_made, 1)

            with act.Fori(0, HALF - 1) as i:
                for s in range(2):
                    split_hi(act, w, i + 1, s)
                    square(2 * i + s, s)
            square(DC - 2, 0)
            for a in range(2):
                act.wait_ge(nxt.landed[a], 16)
                act.wait_ge(prod, NTG * (DC + a + 1))
                act.activation(nxt.hi[a][:, :, :], nxt.raw[a][:, :, :], ACT.Copy).then_inc(nxt.hi_made, 1)
            square(DC - 1, 1)
            st1.act(act, 0)

            def square2(g):
                tk = slice(g * TG, (g + 1) * TG)
                act.wait_ge(added, g + 1)
                act.activation(y[:, :, tk], xt[:, :, tk], ACT.Square).then_inc(squared2, 1)

            square2(0)
            square2(1)
            st2.act(act, 0)
            square2(2)
            st2.act(act, 1)
            st2.act(act, 2)
            for g in range(NTG):
                tk = slice(g * TG, (g + 1) * TG)
                act.wait_ge(normed, DC * (g + 1))
                act.activation(env.x_hi[:, :, tk], y[:, :, tk], ACT.Copy).then_inc(hi2, 1)

        @block.vector
        def _(dve):
            dve.sem_inc(free, CREDIT)
            s_dve(dve)
            for g in range(0, NG, 2):
                x_read(dve, g, x_read_d, dve.tensor_copy)
            s_wait(dve)
            with dve.Fori(0, HALF) as i:
                for s in range(2):
                    for g in range(NTG):
                        m = 3 * (2 * i + s) + g
                        dve.wait_ge(prod, m + 1 + CREDIT)
                        dve.tensor_copy(y[:, bass.ds(2 * i + s, 1), g * TG:(g + 1) * TG],
                                        ps[3 * s + g][:, 0:TG].unsqueeze(1)).then_inc(free, 1)
            st1.dve(dve, 0)
            for g in range(NTG):
                tk = slice(g * TG, (g + 1) * TG)
                dve.wait_ge(st1.spread, g + 1)
                for k in range(DC):
                    dve.scalar_tensor_tensor(out=y[:, k, tk], in0=y[:, k, tk], scalar=env.gains[:, 1, k:k + 1],
                                             in1=st1.wide[g][:, 0:TG], op0=ALU.mult, op1=ALU.mult).then_inc(normed2, 1)
                if g == 0:
                    dve.wait_ge(x_read_a, NT)
                dve.wait_ge(normed2, DC * (g + 1))
                dve.tensor_tensor(xt[:, :, tk], xt[:, :, tk], y[:, :, tk], ALU.add).then_inc(added, 1)
            dve.wait_ge(added, NTG)
            st2.dve(dve, 0)
            for g in range(NTG):
                tk = slice(g * TG, (g + 1) * TG)
                dve.wait_ge(st2.spread, g + 1)
                for k in range(DC):
                    dve.scalar_tensor_tensor(out=y[:, k, tk], in0=xt[:, k, tk], scalar=env.gains[:, 2, k:k + 1],
                                             in1=st2.wide[g][:, 0:TG], op0=ALU.mult, op1=ALU.mult).then_inc(normed, 1)
                if g + 1 < NTG:
                    st2.dve(dve, g + 1)
                if g:
                    low(dve, g - 1, 0, 5, lo2d)
            low(dve, NTG - 1, 0, 5, lo2d)

        @block.tensor
        def _(pe):
            for g in range(NG):
                t = g // 2
                pe.wait_ge(x_in[t % XR], 16 * (t // XR + 1))
                if g >= 6:
                    n = g - 6
                    pe.wait_ge(x_read_a if n % 2 else x_read_d, n // 2 + 1)
                for k in range(4):
                    cc = 4 * (g % 2) + k
                    last = pe.transpose(ps[g % 6][:, k * P:(k + 1) * P], x[t % XR][:, cc * P:(cc + 1) * P],
                                        env.ident[:, :])
                last.then_inc(x_turned, 1)
            pe.wait_ge(x_read_a, NT)
            pe.wait_ge(x_read_d, NT)
            s_wait(pe)
            with pe.Fori(0, HALF) as i:
                for s in range(2):
                    pe.wait_ge(w.lo_made, 2 * i + s + 1 + WRING)
                    for g in range(NTG):
                        m = 3 * (2 * i + s) + g
                        pe.wait_ge(free, m + 1)
                        last = slab_products(pe, w, s, env.x_hi, env.x_lo, ps[3 * s + g][:, 0:TG],
                                             range(DC), slice(g * TG, (g + 1) * TG))
                        last.then_inc(prod, 1)
            pe.wait_ge(free, 3 * DC + CREDIT)
            pe.wait_ge(summed, DC + 1)
            st1.pe_sum(pe, 0)
            st1.pe_spread(pe, 0)
            for g in range(NTG):
                pe.wait_ge(sum2, (DC - 1) * (g + 1))
                st2.pe_sum(pe, g)
                st2.pe_spread(pe, g)


def stage_mlp(env):
    nc, I = env.nc, env.inp
    NP_ = FF // (2 * P)
    with ExitStack() as c:
        def sb(name, shape, dt=F32):
            return c.enter_context(nc.sbuf_tensor("f_" + name, shape, dt))

        w = env.mlp_pipe
        raw = w.raw
        w_hi = w.hi + [sb(f"w_hi{i}", [P, DC, P], F32R) for i in range(2)]
        w_lo = w.lo + [sb(f"w_lo{i}", [P, DC, P], F32R) for i in range(2)]
        f_hi = [[sb(f"f_hi{i}{a}", [P, T], F32R) for a in range(2)] for i in range(2)]
        f_lo = [[sb(f"f_lo{i}{a}", [P, T], F32R) for a in range(2)] for i in range(2)]
        r = [sb(f"relu{i}", [P, TG]) for i in range(2)]
        f = [sb(f"f{i}", [P, TG]) for i in range(2)]
        acc = env.merged
        up = [c.enter_context(nc.psum_tensor(f"f_up{i}", [P, 512], F32)) for i in range(3)]
        down = [c.enter_context(nc.psum_tensor(f"f_down{i}", [P, 512], F32)) for i in range(4)]
        landed, hi_made, lo_made = w.landed, w.hi_made, w.lo_made
        up_made, up_read, squared, f_hi_made, f_lo_made = sems(
            env, "f", "up_made", "up_read", "squared", "f_hi_made", "f_lo_made")
        down_made, added, acc_clear = sems(env, "f", "down_made", "added", "acc_clear")
        block = c.enter_context(nc.Block())
        CU, CD = 3, 4
        w_up = I["w_up"].rearrange("l (c p) n -> p (l c) n", p=P)
        w_down = I["w_down"].rearrange("l (k p) n -> (l k) p n", p=P)
        N_D = DC * NTG


        @block.sync
        def _(sp):
            def load(n, a, src):
                sp.wait_ge(lo_made, n + 1)
                sp.dma_start(raw[a][:, :, :] if src[1] == "up" else raw[a][:, :, :].rearrange("p c n -> p (c n)"),
                             src[0]).then_inc(landed[a], 16)

            with sp.Fori(0, NP_ - 1) as j:
                for a in range(2):
                    load(j * 4 + 2 + a, a, (w_up[:, :, bass.ds(j * 2 * P + (2 + a) * P, P)], "up"))
                for a in range(2):
                    load(j * 4 + 4 + a, a, (w_down[bass.ds(j * 2 + a, 1)].rearrange("k p n -> p (k n)"), "down"))
            for a in range(2):
                load(4 * NP_ - 2 + a, a, (w_down[2 * NP_ - 2 + a], "down"))

        def cycle(split, hidden, j, par, last=False):
            split(j * 4 + 3, 1, True, j + 1)
            hidden(j + 1, 1 - par, 0)
            split(j * 4 + 4, 0, False, j)
            split(j * 4 + 5, 1, False, j)
            hidden(j + 1, 1 - par, 1)
            if not last:
                split(j * 4 + 6, 0, True, j + 2)

        def program(eng, split, hidden):
            for a in range(2):
                hidden(0, 0, a)
            split(2, 0, True, 1)
            cycle(split, hidden, 0, 0)
            cycle(split, hidden, 1, 1)
            with eng.Fori(1, (NP_ - 2) // 2) as i:
                for par in range(2):
                    cycle(split, hidden, i * 2 + par, par)
            cycle(split, hidden, NP_ - 2, 0, last=True)
            for a in range(2):
                split(4 * NP_ - 2 + a, a, False, NP_ - 1)

        @block.scalar
        def _(act):
            def split(n, a, is_up, j):
                slot = a if is_up else 2 + a
                act.wait_ge(landed[a], (n // 2 if isinstance(n, int) else j * 2 + (-1 if is_up else 2)) * 16 + 16)
                if not isinstance(j, int) or j:
                    act.wait_ge(*((up_made, j * 6 + 3 * a - 3) if is_up else (down_made, j * N_D)))
                act.activation(w_hi[slot][:, :, :], raw[a][:, :, :], ACT.Copy).then_inc(hi_made, 1)

            def hidden(j, par, a):
                for g in range(NTG):
                    e, s = j * 6 + 3 * a + g, (3 * a + g) % 2
                    act.wait_ge(up_made, e + 1)
                    act.activation(r[s][:, :], up[g][:, 0:TG], ACT.Relu).then_inc(up_read, 1)
                    act.wait_ge(up_read, e + 1 + CU)
                    act.wait_ge(f_lo_made, e + 1)
                    act.activation(f[s][:, :], r[s][:, :], ACT.Square).then_inc(squared, 1)
                    act.wait_ge(squared, e + 1)
                    act.activation(f_hi[par][a][:, g * TG:(g + 1) * TG], f[s][:, :], ACT.Copy).then_inc(f_hi_made, 1)

            act.sem_inc(up_read, CU)
            program(act, split, hidden)

        @block.gpsimd
        def _(pool):
            def split(n, a, is_up, j):
                slot = a if is_up else 2 + a
                pool.wait_ge(hi_made, n + 1)
                pool.tensor_tensor(w_lo[slot][:, :, :], raw[a][:, :, :], w_hi[slot][:, :, :].bitcast(F32),
                                   ALU.subtract).then_inc(lo_made, 1)

            def hidden(j, par, a):
                for g in range(NTG):
                    e, s = j * 6 + 3 * a + g, (3 * a + g) % 2
                    tk = slice(g * TG, (g + 1) * TG)
                    pool.wait_ge(f_hi_made, e + 1)
                    pool.tensor_tensor(f_lo[par][a][:, tk], f[s][:, :], f_hi[par][a][:, tk].bitcast(F32),
                                       ALU.subtract).then_inc(f_lo_made, 1)

            pool.sem_inc(f_lo_made, 2)
            program(pool, split, hidden)

        @block.vector
        def _(dve):
            dve.sem_inc(added, CD)
            dve.memset(acc[:, :, :], 0.0).then_inc(acc_clear, 1)
            dve.wait_ge(acc_clear, 1)
            with dve.Fori(0, NP_) as j:
                dve.wait_ge(added, j * N_D + CD)
                for d in range(N_D):
                    o, g = divmod(d, NTG)
                    a = acc[:, o, g * TG:(g + 1) * TG]
                    dve.wait_ge(down_made, j * N_D + d + 1)
                    dve.tensor_tensor(a, a, down[d % 4][:, 0:TG], ALU.add).then_inc(added, 1)

        @block.tensor
        def _(pe):
            def make_up(j):
                for a in range(2):
                    n = a if isinstance(j, int) and j == 0 else j * 4 - 2 + a
                    pe.wait_ge(lo_made, n + 1 + 2)
                    for g in range(NTG):
                        tk = slice(g * TG, (g + 1) * TG)
                        pe.wait_ge(up_read, j * 6 + 3 * a + g + 1)
                        k = 0
                        for cc in range(DC):
                            for p_, q_ in ((w_lo, env.x_hi), (w_hi, env.x_lo), (w_hi, env.x_hi)):
                                last = pe.matmul(up[g][:, 0:TG], p_[a][:, cc, :], q_[:, cc, tk],
                                                 start=k == 0, stop=k == 3 * DC - 1)
                                k += 1
                        last.then_inc(up_made, 1)

            def make_down(j, par, n):
                pe.wait_ge(lo_made, n + 2 + 2)
                pe.wait_ge(f_lo_made, j * 6 + 6 + 2)
                for d in range(N_D):
                    o, g = divmod(d, NTG)
                    tk = slice(g * TG, (g + 1) * TG)
                    pe.wait_ge(added, j * N_D + d + 1)
                    k = 0
                    for a in range(2):
                        for p_, q_ in ((w_lo, f_hi), (w_hi, f_lo), (w_hi, f_hi)):
                            last = pe.matmul(down[d % 4][:, 0:TG], p_[2 + a][:, o, :], q_[par][a][:, tk],
                                             start=k == 0, stop=k == 5)
                            k += 1
                    last.then_inc(down_made, 1)

            make_up(0)
            make_up(1)
            make_down(0, 0, 4)
            make_up(2)
            make_down(1, 1, 8)
            with pe.Fori(1, (NP_ - 2) // 2) as i:
                for par in range(2):
                    j = i * 2 + par
                    make_up(j + 1)
                    make_down(j, par, j * 4 + 4)
            make_up(NP_ - 1)
            make_down(NP_ - 2, 0, 4 * NP_ - 4)
            make_down(NP_ - 1, 1, 4 * NP_ - 2)


def stage_norm_out(env):
    nc, O_ = env.nc, env.out
    with ExitStack() as c:
        acc = env.merged
        res = c.enter_context(nc.sbuf_tensor("e_resid", [P, DC, T], F32))
        sq = c.enter_context(nc.sbuf_tensor("e_sq", [P, DC, T], F32))
        rstd = c.enter_context(nc.sbuf_tensor("e_rstd", [P, T], F32))
        y = [c.enter_context(nc.sbuf_tensor(f"e_y{i}", [P, D], F32)) for i in range(3)]
        ps = [c.enter_context(nc.psum_tensor(f"e_ps{i}", [P, 512], F32)) for i in range(4)]
        wide = [c.enter_context(nc.psum_tensor(f"e_wide{i}", [P, 512], F32)) for i in range(NTG)]
        st = TokenStats(env, "e1", rstd, wide)
        res_in, squared, scaled, added_d, added_p, turned, moved_a, moved_d, sent0, sent1, sent2 = sems(
            env, "e", "res_in", "squared", "scaled", "added_dve", "added_pool", "turned", "moved_act", "moved_dve",
            "sent0", "sent1", "sent2")
        sent = (sent0, sent1, sent2)
        block = c.enter_context(nc.Block())

        @block.sync
        def _(sp):
            sp.dma_start(res[:, :, :], env.resid.rearrange("(c p) t -> p c t", p=P)).then_inc(res_in, 16)
            yp = O_["y_prompt"].rearrange("a (t p) d -> (a t) p d", p=P)
            ys = O_["y_sample"].rearrange("b t d -> (b t) d")
            for t in range(NT):
                sp.wait_ge(moved_a, t + 1)
                sp.wait_ge(moved_d, t + 1)
                sp.dma_start(yp[t] if t < NPT else ys, y[t % 3][:, :]).then_inc(sent[t % 3], 16)
            for i in range(3):
                sp.wait_ge(sent[i], 16 * (NT // 3))

        def move(e, t, half, copy, sem):
            if t >= 3:
                e.wait_ge(sent[t % 3], 16 * (t // 3))
            n = 2 * t + half
            e.wait_ge(turned, n + 1)
            copy(y[t % 3][:, half * 512:(half + 1) * 512], ps[n % 4][:, :]).then_inc(sem, 1)

        def add(e, g, a, z, sem):
            tk = slice(g * TG, (g + 1) * TG)
            e.wait_ge(res_in, 16)
            e.wait_ge(scaled, DC * (g + 1))
            e.tensor_tensor(acc[:, a:z, tk], acc[:, a:z, tk], res[:, a:z, tk], ALU.add).then_inc(sem, 1)

        @block.gpsimd
        def _(pool):
            for g in range(NTG):
                add(pool, g, 5, DC, added_p)

        @block.scalar
        def _(act):
            for g in range(NTG):
                tk = slice(g * TG, (g + 1) * TG)
                act.activation(sq[:, :, tk], acc[:, :, tk], ACT.Square).then_inc(squared, 1)
            for g in range(NTG):
                st.act(act, g)
            for t in range(NT):
                move(act, t, 0, lambda d, s: act.activation(d, s, ACT.Copy), moved_a)

        @block.vector
        def _(dve):
            for g in range(NTG):
                tk = slice(g * TG, (g + 1) * TG)
                st.dve(dve, g)
                for k in range(DC):
                    dve.scalar_tensor_tensor(out=acc[:, k, tk], in0=acc[:, k, tk], scalar=env.gains[:, 3, k:k + 1],
                                             in1=rstd[:, tk], op0=ALU.mult, op1=ALU.mult).then_inc(scaled, 1)
                add(dve, g, 0, 5, added_d)
                if g:
                    for t in range(3 * g - 3, 3 * g):
                        move(dve, t, 1, dve.tensor_copy, moved_d)
            for t in range(NT - 3, NT):
                move(dve, t, 1, dve.tensor_copy, moved_d)

        @block.tensor
        def _(pe):
            for g in range(NTG):
                pe.wait_ge(squared, g + 1)
                st.pe(pe, g, [sq[:, k, g * TG:(g + 1) * TG] for k in range(DC)])
            for t in range(NT):
                pe.wait_ge(added_d, t // 3 + 1)
                pe.wait_ge(added_p, t // 3 + 1)
                for half in range(2):
                    n = 2 * t + half
                    if t >= 2:
                        pe.wait_ge(moved_d if half else moved_a, t - 1)
                    for i in range(4):
                        last = pe.transpose(ps[n % 4][:, i * P:(i + 1) * P], acc[:, 4 * half + i, t * P:(t + 1) * P],
                                            env.ident[:, :])
                    last.then_inc(turned, 1)


def build(nc, inp, out):
    with ExitStack() as ctx:
        env = Env()
        env.nc, env.inp, env.out, env.sems = nc, inp, out, []

        def sb(name, shape, dt=F32, c=ctx):
            return c.enter_context(nc.sbuf_tensor(name, shape, dt))

        env.ident, env.ones = sb("ident", [P, P]), sb("ones", [P, P])
        env.eps = sb("eps", [P, 1])
        env.gains = sb("gains", [P, 4, DC])
        env.proj = nc.dram_tensor("proj", [sum(NSLAB) * P, T], F32).ap()
        env.resid = nc.dram_tensor("resid", [D, T], F32).ap()
        inputs = ctx.enter_context(ExitStack())
        with ExitStack() as mix:
            env.flip = sb("flip", [P, P], c=mix)
            env.cum, env.after, env.shut = (sb(n, [P, 2, P], c=mix) for n in ("cum", "after", "shut"))
            env.level = sb("level", [P, len(LEVELS), P], c=mix)
            env.member = sb("member", [P, 2 + NB], c=mix)
            env.convw = sb("convw", [P, CW, CC], c=mix)
            env.dgain = sb("dgain", [P, 1], c=mix)
            env.alog, env.dtb = sb("alog", [P, HB], c=mix), sb("dtb", [P, HB], c=mix)
            env.state_t = sb("state_t", [P, CC, NB * (CW - 1)], c=mix)
            env.conv_tail = sb("conv_tail", [P, CC, (NB + 1) * (CW - 1)], c=mix)
            env.ab = sb("ab", [P, NT, 2 * HB], c=mix)
            env.qk_in, env.v_in = sems(env, "a", "qk_in", "v_in")
            with ExitStack() as qkv:
                with ExitStack() as xc:
                    env.x_hi, env.x_lo = sb("x_hi", [P, DC, T], F32R, xc), sb("x_lo", [P, DC, T], F32R, xc)
                    env.wab = sb("w_ab", [P, DC, 2 * HB], c=xc)
                    env.w_in_pipe = weight_pipe(env, "i", slab_memory(env, "i", xc))
                    env.ab_land, = sems(env, "i", "ab_land")
                    stage_norm_in(env)
                    env.q, env.k, env.v = (
                        qkv.enter_context(nc.sbuf_tensor(n, [P, 4, T], F32, side="right")) for n in ("q", "k", "v"))
                    stage_in_proj(env)
                env.oa = sb("oa", [P, 4, T], c=mix)
                stage_attention(env)
            env.ob = sb("ob", [P, 4, T], c=mix)
            stage_delta(env)
            clear_sems(env)

            def right(name, shape, dt=F32, c=inputs):
                return c.enter_context(nc.sbuf_tensor(name, shape, dt, side="right"))

            env.merged = right("merged", [P, DC, T], c=ctx)
            env.x_hi, env.x_lo = right("h_hi", [P, DC, T], F32R), right("h_lo", [P, DC, T], F32R)
            env.slabs = [[right(f"s_{kind}{i}", [P, DC, P], dt) for i in range(WRING)]
                         for kind, dt in (("w_raw", F32), ("w_hi", F32R), ("w_lo", F32R))]
            env.w_out_pipe, env.mlp_pipe = weight_pipe(env, "o", env.slabs), weight_pipe(env, "f", env.slabs)
            stage_merge(env)
        stage_out_proj(env)
        stage_mlp(env)
        inputs.close()
        stage_norm_out(env)


_INS = ['x_prompt', 'x_sample', 'cache_attn_k', 'cache_attn_v', 'state_conv', 'state_delta', 'norm_mix_pre', 'w_in',
        'rel_bias', 'conv_w', 'a_log', 'dt_bias', 'delta_norm_w', 'w_proj_a', 'w_proj_b', 'w_out', 'norm_mix_post',
        'norm_mlp_pre', 'w_up', 'w_down', 'norm_mlp_post']
_OUTS = {'y_prompt': (1, TP, D), 'y_sample': (NB, TS, D),
         'prompt_k': (1, 1, REACH, AH, AD), 'prompt_v': (1, 1, REACH, AH, AD),
         'prompt_conv': (1, 1, CW - 1, CONV), 'prompt_delta': (1, 1, HB, DK, DK),
         'sample_k': (1, NB, TS, AH, AD), 'sample_v': (1, NB, TS, AH, AD),
         'sample_conv': (1, NB, CW - 1, CONV), 'sample_delta': (1, NB, HB, DK, DK)}


def kernel(**inputs):
    import numpy as _np
    import concourse.bacc as _bacc
    from concourse import mybir as _mybir
    from concourse.bass_utils import run_bass_kernel_spmd as _run

    nc = _bacc.Bacc("TRN2", target_bir_lowering=False, num_devices=1)
    arrays, inp, out = {}, {}, {}
    for name in _INS:
        a = _np.ascontiguousarray(inputs[name])
        arrays[f"in_{name}"] = a
        inp[name] = nc.dram_tensor(f"in_{name}", a.shape, _mybir.dt.from_np(a.dtype), kind="ExternalInput").ap()
    for name, shape in _OUTS.items():
        out[name] = nc.dram_tensor(f"out_{name}", shape, _mybir.dt.float32, kind="ExternalOutput").ap()
    build(nc, inp, out)
    r = _run(nc, [arrays], core_ids=[0])
    return tuple(r.results[0][f"out_{name}"] for name in _OUTS)
```
